# Optimizing a Trainium2 kernel written in Bass

```python
import math
import jax, jax.numpy as jnp
from jax import lax
import numpy as np

D_MODEL = 2048
BATCH = 1
SEQ = 512
DEPTH = 1
DEC_BATCH = 8
DEC_SEQ = 1
PAST_LEN = 2048
PAGE_SIZE = 128

RWKV_DIM = D_MODEL // 2
RWKV_HEAD_DIM = 64
RWKV_HEADS = RWKV_DIM // RWKV_HEAD_DIM
DECAY_LORA = 64
AAA_LORA = 64
GATE_LORA = 128
RWKV_PROJ = 3 * RWKV_DIM + DECAY_LORA + AAA_LORA + GATE_LORA
DA_DIM = D_MODEL - RWKV_DIM
DA_QK_DIM = 64
DA_V_DIM = 2 * DA_QK_DIM
DA_HEADS = DA_DIM // DA_V_DIM
DA_PROJ = 3 * DA_DIM
IN_PROJ = RWKV_PROJ + DA_PROJ
MEM_TOKENS = 256
CROSS_HEADS = 4
CROSS_HEAD_DIM = D_MODEL // CROSS_HEADS
D_FF = ((8 * D_MODEL + 767) // 768) * 256
Q_BLOCK = 128
RMS_EPS = 1e-6
GN_EPS = 64e-5
NEG_INF = -1e30

kernel_name = "hymba_rwkv7_diffattn_decoder_step"

def _rmsnorm(x, g):
    xf = x.astype(jnp.float32)
    y = xf * lax.rsqrt(jnp.mean(xf * xf, axis=-1, keepdims=True) + RMS_EPS)
    return (y * g.astype(jnp.float32)).astype(x.dtype)

def _rwkv7_group(p, prev_row, S0, lp):
    f32 = jnp.float32
    b, t, _ = p.shape
    H, N = RWKV_HEADS, RWKV_HEAD_DIM
    p_prev = jnp.concatenate([prev_row[:, None, :].astype(p.dtype), p[:, :-1]], axis=1)
    ps = p + (p_prev - p) * lp['mu']
    o1, o2, o3 = RWKV_DIM, 2 * RWKV_DIM, 3 * RWKV_DIM
    o4 = o3 + DECAY_LORA
    o5 = o4 + AAA_LORA
    r, k, v = ps[..., :o1], ps[..., o1:o2], ps[..., o2:o3]
    wd, ad, gd = ps[..., o3:o4], ps[..., o4:o5], ps[..., o5:]
    w_log = -jax.nn.softplus(-(lp['w0'] + jnp.tanh(wd) @ lp['w2']).astype(f32)) - 0.5
    decay = jnp.exp(-jnp.exp(w_log))
    a = jax.nn.sigmoid((lp['a0'] + ad @ lp['a2']).astype(f32))
    g = jax.nn.sigmoid(gd) @ lp['g2']
    hs = lambda z: z.reshape(b, t, H, N)
    kk = hs((k * lp['k_k']).astype(f32))
    kk = kk * lax.rsqrt(jnp.maximum(jnp.sum(kk * kk, axis=-1, keepdims=True), 1e-24))
    k = k.astype(f32) * (1.0 + (a - 1.0) * lp['k_a'])
    r4, k4, v4, w4, a4 = hs(r.astype(f32)), hs(k), hs(v.astype(f32)), hs(decay), hs(a)
    avec = -kk
    bvec = kk * a4

    def step(S, inp):
        rt, wt, kt, vt, at, bt = inp
        S = (S * wt[:, :, None, :]
             + jnp.einsum('bhij,bhj->bhi', S, at)[..., None] * bt[:, :, None, :]
             + vt[..., None] * kt[:, :, None, :])
        return S, jnp.einsum('bhij,bhj->bhi', S, rt)

    tm = lambda z: jnp.moveaxis(z, 1, 0)
    S_fin, y = lax.scan(step, S0.astype(f32), (tm(r4), tm(w4), tm(k4), tm(v4), tm(avec), tm(bvec)))
    y = jnp.moveaxis(y, 0, 1)
    mean = jnp.mean(y, axis=-1, keepdims=True)
    var = jnp.mean(jnp.square(y - mean), axis=-1, keepdims=True)
    y = ((y - mean) * lax.rsqrt(var + GN_EPS)).reshape(b, t, RWKV_DIM) * lp['lnx_g'] + lp['lnx_b']
    bonus = jnp.sum(r4 * k4 * lp['r_k'], axis=-1, keepdims=True) * v4
    y = (y + bonus.reshape(b, t, RWKV_DIM)) * g
    return y.astype(p.dtype), S_fin.astype(S0.dtype), p[:, -1]

def _diff_attend(q, segs, q_pos, lam):
    scores = []
    for k, _, kp in segs:
        s = jnp.einsum('bthcd,bshcd->bchts', q, k).astype(jnp.float32)
        scores.append(jnp.where(kp[None, :] <= q_pos[:, None], s, NEG_INF))
    p = jax.nn.softmax(jnp.concatenate(scores, axis=-1), axis=-1)
    w = p[:, 0] - lam * p[:, 1]
    out = None
    off = 0
    for k, v, kp in segs:
        n = kp.shape[0]
        o = jnp.einsum('bhts,bshe->bthe', w[..., off:off + n], v.astype(jnp.float32))
        out = o if out is None else out + o
        off += n
    return out

def _prompt_attend(q, k, v, lam):
    b, t = q.shape[:2]
    nb = t // Q_BLOCK
    qb = jnp.moveaxis(q.reshape(b, nb, Q_BLOCK, DA_HEADS, 2, DA_QK_DIM), 1, 0)
    kpos = jnp.arange(t)

    def one(args):
        i, qi = args
        return _diff_attend(qi, [(k, v, kpos)], i * Q_BLOCK + jnp.arange(Q_BLOCK), lam)

    o = lax.map(one, (jnp.arange(nb), qb))
    return jnp.moveaxis(o, 0, 1).reshape(b, t, DA_HEADS, DA_V_DIM)

def _make_sample_attend(k_past, v_past):
    def attend(q, k, v, lam):
        P = k_past.shape[1]
        t = q.shape[1]
        new_pos = P + jnp.arange(t)
        return _diff_attend(q, [(k_past, v_past, jnp.arange(P)), (k, v, new_pos)], new_pos, lam)
    return attend

def _cross_attend(h, mk, mv, w_cq, w_co):
    b, t, _ = h.shape
    q = (h @ w_cq).reshape(b, t, CROSS_HEADS, CROSS_HEAD_DIM) * CROSS_HEAD_DIM ** -0.5
    s = jnp.einsum('bthe,bmhe->bhtm', q, mk).astype(jnp.float32)
    p = jax.nn.softmax(s, axis=-1).astype(mv.dtype)
    o = jnp.einsum('bhtm,bmhe->bthe', p, mv).reshape(b, t, D_MODEL)
    return o @ w_co

def _layer(x, prev_row, S0, attend, mem_k, mem_v, lp, lam_init):
    b, t, _ = x.shape
    h = _rmsnorm(x, lp['norm_mix_g'])
    pin = h @ lp['w_in']
    pr = pin[..., :RWKV_PROJ]
    pq = pin[..., RWKV_PROJ:RWKV_PROJ + DA_DIM]
    pk = pin[..., RWKV_PROJ + DA_DIM:RWKV_PROJ + 2 * DA_DIM]
    pv = pin[..., RWKV_PROJ + 2 * DA_DIM:]
    y_r, S_new, last_row = _rwkv7_group(pr, prev_row, S0, lp)
    q = pq.reshape(b, t, DA_HEADS, 2, DA_QK_DIM) * DA_QK_DIM ** -0.5
    k = pk.reshape(b, t, DA_HEADS, 2, DA_QK_DIM)
    v = pv.reshape(b, t, DA_HEADS, DA_V_DIM)
    f32 = jnp.float32
    lam = (jnp.exp(jnp.sum(lp['lq1'].astype(f32) * lp['lk1'].astype(f32)))
           - jnp.exp(jnp.sum(lp['lq2'].astype(f32) * lp['lk2'].astype(f32))) + lam_init)
    o = attend(q, k, v, lam)
    o = _rmsnorm(o, lp['subln_g']) * (1.0 - lam_init)
    y_d = o.reshape(b, t, DA_DIM).astype(x.dtype)
    x = x + jnp.concatenate([y_r, y_d], axis=-1) @ lp['w_o']
    x = x + _cross_attend(_rmsnorm(x, lp['norm_cross_g']), mem_k, mem_v, lp['w_cq'], lp['w_co'])
    hf = _rmsnorm(x, lp['norm_ffn_g'])
    x = x + (jax.nn.silu(hf @ lp['w_gate']) * (hf @ lp['w_up'])) @ lp['w_down']
    return x, k.reshape(b, t, DA_HEADS, 2 * DA_QK_DIM), v, S_new, last_row

def setup_inputs(seed: int = 0) -> dict:
    key = jax.random.key(seed)
    ks = iter(jax.random.split(key, 64))
    f32 = jnp.float32
    nrm = lambda shape, scale: jax.random.normal(next(ks), shape, f32) * scale
    gain = lambda shape: 1.0 + 0.05 * jax.random.normal(next(ks), shape, f32)
    n_pages = PAST_LEN // PAGE_SIZE
    n_used = DEC_BATCH * n_pages
    n_pool = n_used + max(1, n_used // 4)
    page_table = jax.random.permutation(next(ks), n_pool)[:n_used].reshape(DEC_BATCH, n_pages).astype(jnp.int32)
    L = DEPTH
    return {
        'x_prompt': nrm((BATCH, SEQ, D_MODEL), 1.0),
        'x_sample': nrm((DEC_BATCH, DEC_SEQ, D_MODEL), 1.0),
        'cache_k': nrm((L, n_pool, PAGE_SIZE, DA_HEADS, 2 * DA_QK_DIM), 1.0),
        'cache_v': nrm((L, n_pool, PAGE_SIZE, DA_HEADS, DA_V_DIM), 1.0),
        'cache_mem_k': nrm((L, DEC_BATCH, MEM_TOKENS, CROSS_HEADS, CROSS_HEAD_DIM), 1.0),
        'cache_mem_v': nrm((L, DEC_BATCH, MEM_TOKENS, CROSS_HEADS, CROSS_HEAD_DIM), 1.0),
        'state_wkv': nrm((L, DEC_BATCH, RWKV_HEADS, RWKV_HEAD_DIM, RWKV_HEAD_DIM), 0.5),
        'state_shift': nrm((L, DEC_BATCH, RWKV_PROJ), 1.0),
        'page_table': page_table,
        'mem_prompt': nrm((BATCH, MEM_TOKENS, D_MODEL), 1.0),
        'norm_mix_g': gain((L, D_MODEL)),
        'w_in': nrm((L, D_MODEL, IN_PROJ), D_MODEL ** -0.5),
        'tok_shift_mu': jax.random.uniform(next(ks), (L, RWKV_PROJ), f32),
        'rwkv_w0': jax.random.uniform(next(ks), (L, RWKV_DIM), f32, -4.0, 1.0),
        'rwkv_w2': nrm((L, DECAY_LORA, RWKV_DIM), 0.5 * DECAY_LORA ** -0.5),
        'rwkv_a0': nrm((L, RWKV_DIM), 0.1),
        'rwkv_a2': nrm((L, AAA_LORA, RWKV_DIM), 0.5 * AAA_LORA ** -0.5),
        'rwkv_g2': nrm((L, GATE_LORA, RWKV_DIM), GATE_LORA ** -0.5),
        'rwkv_k_k': 0.85 + nrm((L, RWKV_DIM), 0.05),
        'rwkv_k_a': 1.0 + nrm((L, RWKV_DIM), 0.05),
        'rwkv_r_k': nrm((L, RWKV_HEADS, RWKV_HEAD_DIM), 0.1),
        'rwkv_lnx_g': gain((L, RWKV_DIM)),
        'rwkv_lnx_b': nrm((L, RWKV_DIM), 0.02),
        'diff_lq1': nrm((L, DA_QK_DIM), 0.1),
        'diff_lk1': nrm((L, DA_QK_DIM), 0.1),
        'diff_lq2': nrm((L, DA_QK_DIM), 0.1),
        'diff_lk2': nrm((L, DA_QK_DIM), 0.1),
        'diff_subln_g': gain((L, DA_V_DIM)),
        'w_o': nrm((L, D_MODEL, D_MODEL), D_MODEL ** -0.5),
        'norm_cross_g': gain((L, D_MODEL)),
        'norm_mem_g': gain((L, D_MODEL)),
        'w_cq': nrm((L, D_MODEL, D_MODEL), D_MODEL ** -0.5),
        'w_ck': nrm((L, D_MODEL, D_MODEL), D_MODEL ** -0.5),
        'w_cv': nrm((L, D_MODEL, D_MODEL), D_MODEL ** -0.5),
        'w_co': nrm((L, D_MODEL, D_MODEL), D_MODEL ** -0.5),
        'norm_ffn_g': gain((L, D_MODEL)),
        'w_gate': nrm((L, D_MODEL, D_FF), D_MODEL ** -0.5),
        'w_up': nrm((L, D_MODEL, D_FF), D_MODEL ** -0.5),
        'w_down': nrm((L, D_FF, D_MODEL), D_FF ** -0.5),
        'final_norm_g': gain((D_MODEL,)),
    }

def reference(x_prompt, x_sample, cache_k, cache_v, cache_mem_k, cache_mem_v, state_wkv, state_shift,
              page_table, mem_prompt, norm_mix_g, w_in, tok_shift_mu, rwkv_w0, rwkv_w2, rwkv_a0, rwkv_a2,
              rwkv_g2, rwkv_k_k, rwkv_k_a, rwkv_r_k, rwkv_lnx_g, rwkv_lnx_b, diff_lq1, diff_lk1, diff_lq2,
              diff_lk2, diff_subln_g, w_o, norm_cross_g, norm_mem_g, w_cq, w_ck, w_cv, w_co, norm_ffn_g,
              w_gate, w_up, w_down, final_norm_g):
    b = x_prompt.shape[0]
    db = x_sample.shape[0]
    past_len = page_table.shape[1] * cache_k.shape[2]
    k_p, v_p, k_s, v_s = [], [], [], []
    S_p, S_s, sh_p, sh_s, mk_p, mv_p = [], [], [], [], [], []
    xp, xs = x_prompt, x_sample
    for l in range(DEPTH):
        lam_init = 0.8 - 0.6 * math.exp(-0.3 * l)
        lp = dict(norm_mix_g=norm_mix_g[l], w_in=w_in[l], mu=tok_shift_mu[l], w0=rwkv_w0[l], w2=rwkv_w2[l],
                  a0=rwkv_a0[l], a2=rwkv_a2[l], g2=rwkv_g2[l], k_k=rwkv_k_k[l], k_a=rwkv_k_a[l],
                  r_k=rwkv_r_k[l], lnx_g=rwkv_lnx_g[l], lnx_b=rwkv_lnx_b[l], lq1=diff_lq1[l], lk1=diff_lk1[l],
                  lq2=diff_lq2[l], lk2=diff_lk2[l], subln_g=diff_subln_g[l], w_o=w_o[l],
                  norm_cross_g=norm_cross_g[l], w_cq=w_cq[l], w_co=w_co[l], norm_ffn_g=norm_ffn_g[l],
                  w_gate=w_gate[l], w_up=w_up[l], w_down=w_down[l])
        memn = _rmsnorm(mem_prompt, norm_mem_g[l])
        mk = (memn @ w_ck[l]).reshape(b, MEM_TOKENS, CROSS_HEADS, CROSS_HEAD_DIM)
        mv = (memn @ w_cv[l]).reshape(b, MEM_TOKENS, CROSS_HEADS, CROSS_HEAD_DIM)
        zero_row = jnp.zeros((b, RWKV_PROJ), x_prompt.dtype)
        zero_S = jnp.zeros((b, RWKV_HEADS, RWKV_HEAD_DIM, RWKV_HEAD_DIM), state_wkv.dtype)
        xp, kn, vn, Sn, rown = _layer(xp, zero_row, zero_S, _prompt_attend, mk, mv, lp, lam_init)
        k_p.append(kn)
        v_p.append(vn)
        S_p.append(Sn)
        sh_p.append(rown)
        mk_p.append(mk)
        mv_p.append(mv)
        k_past = cache_k[l][page_table].reshape(db, past_len, DA_HEADS, 2, DA_QK_DIM)
        v_past = cache_v[l][page_table].reshape(db, past_len, DA_HEADS, DA_V_DIM)
        xs, kn, vn, Sn, rown = _layer(xs, state_shift[l], state_wkv[l], _make_sample_attend(k_past, v_past),
                                      cache_mem_k[l], cache_mem_v[l], lp, lam_init)
        k_s.append(kn)
        v_s.append(vn)
        S_s.append(Sn)
        sh_s.append(rown)
    y_prompt = _rmsnorm(xp, final_norm_g)
    y_sample = _rmsnorm(xs, final_norm_g)
    return (y_prompt, y_sample, jnp.stack(k_p), jnp.stack(v_p), jnp.stack(k_s), jnp.stack(v_s),
            jnp.stack(S_p), jnp.stack(S_s), jnp.stack(sh_p), jnp.stack(sh_s), jnp.stack(mk_p), jnp.stack(mv_p))


_drawn_inputs = setup_inputs


def setup_inputs(seed=0):
    import zlib

    import numpy as np

    out = dict(_drawn_inputs(seed))
    spreads = {}
    factors = {'rwkv_lnx_g': 3.081, 'rwkv_lnx_b': 7.837, 'diff_lk2': 4.298, 'norm_cross_g': 8.0}
    for name, (base, spread) in spreads.items():
        noise = np.random.default_rng([zlib.crc32(name.encode()), seed]).standard_normal(out[name].shape)
        drawn = base * np.exp(spread * noise) if base else spread * noise
        out[name] = __import__('jax').numpy.asarray(drawn.astype(out[name].dtype))
    for name, factor in factors.items():
        out[name] = (out[name] * factor).astype(out[name].dtype)
    return out
```

```python
import math
from contextlib import ExitStack

import numpy as np
import concourse.bass as bass
from concourse import mybir

D = 2048
SEQ = 512
NS = 8
TOK = SEQ + NS
HALF = TOK // 2
PAST, PAGE = 2048, 128
PAGES = PAST // PAGE
RW = D // 2
RW_PROJ = 3 * RW + 256
DA_HEADS = 8
MEM = 256
XH, XD = 4, 512
D_FF = ((8 * D + 767) // 768) * 256
KT = D // 128
RT = RW // 128
PROJ_T = RW_PROJ // 128
CH = 64
NCH = SEQ // CH
FFC = D_FF // 512
LAM_INIT = 0.8 - 0.6 * math.exp(-0.3 * 0)
DECAY = math.exp(-0.5)
BLK = 2048

QKV0 = 0
RWK0 = QKV0 + 24
CK0 = RWK0 + PROJ_T
CV0 = CK0 + KT
WO0 = CV0 + KT
CQ0 = WO0 + KT
CO0 = CQ0 + KT
FF0 = CO0 + KT
NBLK = FF0 + 12 * FFC

_cols = [("g_mix", KT), ("g_mem", KT), ("g_cross", KT), ("g_ffn", KT), ("g_final", KT), ("mu", PROJ_T),
         ("w0", RT), ("a0", RT), ("k_k", RT), ("k_a", RT), ("r_k", RT), ("lnx_g", RT), ("lnx_b", RT),
         ("subln", 1), ("lam_q", 1), ("lam_k", 1), ("shift", PROJ_T * NS)]
VEC = {}
_at = 0
for _n, _w in _cols:
    VEC[_n] = _at
    _at += _w
NVEC = _at
_cols = [("ident", 128), ("ones", 128), ("pair", 128), ("halves", 256), ("causal", 128), ("gram", 128),
         ("diag", CH), ("diag_t", CH), ("off_t", CH), ("start", TOK), ("two", 2)]
CON = {}
_at = 0
for _n, _w in _cols:
    CON[_n] = (_at, _at + _w)
    _at += _w
NCON = _at

f32 = mybir.dt.float32
f32r = mybir.dt.float32r
i32 = mybir.dt.int32
ALU = mybir.AluOpType
ACT = mybir.ActivationFunctionType
AX = mybir.AxisListType
SPANS = [(0, HALF), (HALF, HALF)]


def shape_constants():
    c = np.zeros((128, NCON), np.float32)

    def put(name, a):
        c[:, CON[name][0]:CON[name][1]] = a
    p = np.arange(128)[:, None]
    q = np.arange(128)[None, :]
    put("ident", p == q)
    put("ones", 1.0)
    put("pair", p // 64 == q // 64)
    put("halves", np.concatenate([np.broadcast_to(p < 64, (128, 128)), np.broadcast_to(p >= 64, (128, 128))], 1))
    put("causal", np.where(q <= p, 0.0, -1e30))
    s, t = p % 64, q % 64
    put("gram", np.where(q < 64, s < t, s <= t))
    s, t = p % 64, np.arange(64)[None, :]
    put("diag", (s < t) & (s // 8 == t // 8))
    put("diag_t", (t < s) & (s // 8 == t // 8))
    put("off_t", (t < s) & (s // 8 != t // 8))
    put("start", (np.arange(TOK) % CH != 0) & (np.arange(TOK) < SEQ))
    put("two", np.concatenate([p < 64, p >= 64], 1))
    return c


class Steps:

    def __init__(self, sem, names):
        self.sem, self.names = sem, list(names)
        assert len(set(self.names)) == len(self.names)

    def at(self, name, turn=0):
        return turn * len(self.names) + self.names.index(name) + 1


def decoder_kernel(nc, w, vec, con, xt, memt, kc, vc, mkc, mvc, s0, pages, w2a2, g2,
                   qkv, yo, wkv_p, wkv_s, shift, mk_o, mv_o, ymix, upto=99):
    stack = ExitStack()
    nsem = [0]

    def sem(name):
        nsem[0] += 1
        return stack.enter_context(nc.semaphore(name))

    def sb(st, name, shape, dt=f32):
        return st.enter_context(nc.sbuf_tensor(name, shape, dt))

    with stack:
        vt = sb(stack, "vt", [128, NVEC])
        cn = sb(stack, "cn", [128, NCON])
        lam = sb(stack, "lam", [128, 4])
        raw = sb(stack, "raw", [128, 2, BLK])
        ps = stack.enter_context(nc.psum_tensor("ps", [128, 8, 512], f32))
        bank = [ps[:, i, :] for i in range(8)]

        def C(name):
            return cn[:, CON[name][0]:CON[name][1]]

        def V(name, k=0):
            return vt[:, VEC[name] + k:VEC[name] + k + 1]

        const_in = sem("const_in")
        raw_in = [sem("raw_in0"), sem("raw_in1")]
        whi_done = sem("whi_done")
        wlo_done = sem("wlo_done")
        pe_done = sem("pe_done")
        out_done = sem("out_done")

        with nc.Block() as block:
            @block.sync
            def _(sp):
                sp.dma_start(vt[:, :], vec).then_inc(const_in, 16)
                sp.dma_start(cn[:, :], con).then_inc(const_in, 16)
                for u in range(2):
                    sp.dma_start(raw[:, u, :], w[u, :, :]).then_inc(raw_in[u], 16)
                sp.wait_ge(const_in, 32)

            @block.tensor
            def _(pe):
                pe.sem_inc(pe_done, 2)

            @block.vector
            def _(dve):
                dve.sem_inc(out_done, 2)

        def load_block(sp, g, u, ahead=2):
            sp.wait_ge(wlo_done, g + 1)
            src = w[g + ahead, :, :] if isinstance(g, int) else w[bass.ds(g + ahead, 1), :, :].rearrange("o p n -> p (o n)")
            sp.dma_start(raw[:, u, :], src).then_inc(raw_in[u], 16)

        def weight_hi(act, whi, g, u, turn):
            act.wait_ge(raw_in[u], turn * 16 + 16)
            act.wait_ge(pe_done, g + 1)
            act.activation(whi[:, u, :], raw[:, u, :], ACT.Copy).then_inc(whi_done, 1)

        def weight_lo(dve, whi, wlo, g, u):
            dve.wait_ge(whi_done, g + 1)
            dve.tensor_tensor(wlo[:, u, :], raw[:, u, :], whi[:, u, :].bitcast(f32),
                              ALU.subtract).then_inc(wlo_done, 1)

        jobs = [0]

        def project(name, g0, n, ah, al, whi, wlo, spans, evac, src=None, gain=None, stat=None, extra=None):
            j0 = jobs[0]
            jobs[0] += n
            assert g0 % 2 == 0 and n % 2 == 0 and j0 % 2 == 0
            h0 = g0 // 2
            T = spans[-1][0] + spans[-1][1]
            hi_done, lo_done, sq_done, ssq_done, ms_done, rms_done = (
                [sem(f"{name}_{x}") for x in ("hi", "lo", "sq", "ssq", "ms", "rms")] if src is not None else [None] * 6)
            scale = (lambda k: V(gain, k)) if gain else (lambda k: 1.0)

            def block_product(pe, g, j, u, first=False):
                pe.wait_ge(wlo_done, g + 1)
                pe.wait_ge(out_done, j + 1)
                for k in range(KT):
                    if first:
                        pe.wait_ge(lo_done, k + 1)
                    ks = slice(k * 128, k * 128 + 128)
                    for wt, at in ((whi, ah), (whi, al), (wlo, ah)):
                        for i, (a, m) in enumerate(spans):
                            mm = pe.matmul(bank[2 * u + i][:, 0:m], wt[:, u, ks], at[:, k, a:a + m],
                                           start=(k == 0 and wt is whi and at is ah),
                                           stop=(k == KT - 1 and wt is wlo))
                mm.then_inc(pe_done, 1)

            with nc.Block() as block:
                @block.sync
                def _(sp):
                    if g0 + n == NBLK:
                        with sp.Fori(0, n // 2 - 1) as t:
                            for u in range(2):
                                load_block(sp, t * 2 + (g0 + u), u)
                    else:
                        with sp.Fori(0, n // 2) as t:
                            for u in range(2):
                                load_block(sp, t * 2 + (g0 + u), u)

                @block.scalar
                def _(act):
                    for u in range(2):
                        weight_hi(act, whi, g0 + u, u, h0)
                        if u == 0 and src is not None:
                            for k in range(KT):
                                act.activation(ah[:, k, :], src[:, k, :], ACT.Copy, scale=scale(k)).then_inc(hi_done, 1)
                    if stat:
                        rstd, sq = stat
                        for k in range(KT):
                            if k >= 2:
                                act.wait_ge(ssq_done, k - 1)
                            act.activation(sq[:, k % 2, 0:T], src[:, k, :], ACT.Square).then_inc(sq_done, 1)
                        act.wait_ge(ms_done, len(spans))
                        act.activation(rstd[:, 0:T], rstd[:, 0:T], ACT.Sqrt).then_inc(rms_done, 1)
                    with act.Fori(1, n // 2) as t:
                        for u in range(2):
                            weight_hi(act, whi, t * 2 + (g0 + u), u, t + h0)

                @block.vector
                def _(dve):
                    for u in range(2):
                        weight_lo(dve, whi, wlo, g0 + u, u)
                        if u == 0 and src is not None:
                            for k in range(KT):
                                dve.wait_ge(hi_done, k + 1)
                                dve.scalar_tensor_tensor(al[:, k, :], src[:, k, :], scale(k), ah[:, k, :].bitcast(f32),
                                                         ALU.mult, ALU.subtract).then_inc(lo_done, 1)
                    if stat:
                        rstd, sq = stat
                        dve.wait_ge(ssq_done, KT)
                        for i, (a, m) in enumerate(spans):
                            dve.tensor_scalar(rstd[:, a:a + m], bank[4 + i][:, 0:m], 1.0 / D, 1e-6,
                                              ALU.mult, ALU.add).then_inc(ms_done, 1)
                        dve.wait_ge(rms_done, 1)
                        dve.reciprocal(rstd[:, 0:T], rstd[:, 0:T]).then_inc(rms_done, 1)
                        dve.wait_ge(rms_done, 2)
                    with dve.Fori(0, n // 2 - 1) as t:
                        for u in range(2):
                            dve.wait_ge(pe_done, t * 2 + (g0 + u + 3))
                            evac(dve, t * 2 + u, u, t)
                            weight_lo(dve, whi, wlo, t * 2 + (g0 + u + 2), u)
                    for u in range(2):
                        dve.wait_ge(pe_done, g0 + n + u + 1)
                        evac(dve, n - 2 + u, u, n // 2 - 1)

                @block.tensor
                def _(pe):
                    for u in range(2):
                        block_product(pe, g0 + u, j0 + u, u, first=(u == 0 and src is not None))
                        if u == 0 and stat:
                            for k in range(KT):
                                pe.wait_ge(sq_done, k + 1)
                                for i, (a, m) in enumerate(spans):
                                    mm = pe.matmul(bank[4 + i][:, 0:m], C("ones"), stat[1][:, k % 2, a:a + m],
                                                   start=(k == 0), stop=(k == KT - 1))
                                mm.then_inc(ssq_done, 1)
                    with pe.Fori(1, n // 2) as t:
                        for u in range(2):
                            block_product(pe, t * 2 + (g0 + u), t * 2 + (j0 + u), u)

                if extra:
                    extra(block)

        def tile_of(t, i):
            if isinstance(i, int):
                return t[:, i, :]
            return t[:, bass.ds(i, 1), :].rearrange("p o n -> p (o n)")

        def dram_tile(t, i):
            if isinstance(i, int):
                return t[i, :, :]
            return t[bass.ds(i, 1), :, :].rearrange("o p n -> p (o n)")

        with ExitStack() as mixing:
            rkv = sb(mixing, "rkv", [128, PROJ_T, TOK])
            with ExitStack() as st:
                ah = sb(st, "h_hi", [128, KT, TOK], f32r)
                al = sb(st, "h_lo", [128, KT, TOK], f32r)
                rstd = sb(st, "rstd_mix", [128, TOK])
                with ExitStack() as s2:
                    whi = sb(s2, "whi_a", [128, 2, BLK], f32r)
                    wlo = sb(s2, "wlo_a", [128, 2, BLK], f32r)
                    sq = sb(s2, "sq_a", [128, 2, TOK])
                    ev = sb(s2, "ev_a", [128, 2, TOK])
                    ev_out = sem("ev_out")
                    ev_free = sem("ev_free")
                    x_in = sem("x_in")
                    x = rkv[:, 0:KT, :]

                    with nc.Block() as block:
                        @block.sync
                        def _(sp):
                            for k in range(0, KT, 4):
                                sp.dma_start(x[:, k:k + 4, :], xt[k:k + 4, :, :].rearrange("k p n -> p k n")).then_inc(x_in, 16)
                            sp.wait_ge(x_in, 64)

                        @block.gpsimd
                        def _(pool):
                            pool.sem_inc(ev_free, 2)

                    def evac_qkv(dve, i, u, t):
                        dve.wait_ge(ev_free, i + 1)
                        for s, (a, m) in enumerate(SPANS):
                            ins = dve.tensor_tensor(ev[:, u, a:a + m], bank[2 * u + s][:, 0:m], rstd[:, a:a + m], ALU.mult)
                        ins.then_inc(out_done, 1)

                    def store_qkv(block):
                        @block.gpsimd
                        def _(pool):
                            with pool.Fori(0, 12) as t:
                                for u in range(2):
                                    pool.wait_ge(out_done, t * 2 + (u + 3))
                                    pool.dma_start(dram_tile(qkv, t * 2 + u), ev[:, u, :]).then_inc(ev_out, 16)
                                    pool.wait_ge(ev_out, t * 32 + 16 * (u + 1))
                                    pool.sem_inc(ev_free, 1)

                    project("qkv", QKV0, 24, ah, al, whi, wlo, SPANS, evac_qkv, x, "g_mix", (rstd, sq), store_qkv)

                    p = sb(s2, "p_row", [128, 1 + TOK])
                    dif = sb(s2, "p_dif", [128, TOK])
                    last = sb(s2, "p_last", [128, PROJ_T, 1 + NS])
                    sh = Steps(sem("shift_steps"), ["p0", "p1", "dif", "dif_s", "last", "ps"])
                    sh_out = sem("sh_out")

                    with nc.Block() as block:
                        @block.vector
                        def _(dve):
                            dve.memset(p[:, 0:1], 0.0).then_inc(sh_out, 1)
                            dve.wait_ge(sh_out, 1)

                    def evac_shift(dve, i, u, t):
                        for s, (a, m) in enumerate(SPANS):
                            dve.tensor_tensor(p[:, 1 + a:1 + a + m], bank[2 * u + s][:, 0:m], rstd[:, a:a + m],
                                              ALU.mult).then_inc(sh.sem, 1)
                        dve.wait_ge(sh.sem, i * 6 + 2)
                        dve.tensor_tensor(dif[:, 0:SEQ], p[:, 0:SEQ], p[:, 1:1 + SEQ], ALU.subtract).then_inc(sh.sem, 1)
                        prev = vt[:, bass.ds(VEC["shift"] + i * NS, NS)]
                        dve.tensor_tensor(dif[:, SEQ:TOK], prev, p[:, 1 + SEQ:1 + TOK], ALU.subtract).then_inc(sh.sem, 1)
                        dve.tensor_copy(tile_of(last, i), p[:, SEQ:1 + TOK]).then_inc(sh.sem, 1)
                        dve.wait_ge(sh.sem, i * 6 + 4)
                        dve.scalar_tensor_tensor(tile_of(rkv, i), dif[:, :], vt[:, bass.ds(VEC["mu"] + i, 1)], p[:, 1:1 + TOK],
                                                 ALU.mult, ALU.add).then_inc(sh.sem, 1)
                        dve.wait_ge(sh.sem, i * 6 + 6)
                        dve.sem_inc(out_done, 1)

                    project("rwkv", RWK0, PROJ_T, ah, al, whi, wlo, SPANS, evac_shift)

                    with nc.Block() as block:
                        @block.sync
                        def _(sp):
                            sp.dma_start(shift, last[:, :, :]).then_inc(sh_out, 16)
                            sp.wait_ge(sh_out, 17)

            if upto <= 1:
                return

            attn = ExitStack()
            yd = sb(attn, "yd", [128, DA_HEADS, TOK])
            ready = Steps(sem("lam_steps"), ["prod", "rhs", "sum", "exp", "lam", "neg", "g"])
            lam_e = lam[:, 0:2]
            neg_lam = lam[:, 2:3]
            sub_g = lam[:, 3:4]
            with ExitStack() as st:
                tmp = sb(st, "lam_tmp", [128, 4])
                qh = sb(st, "qkv_head", [128, 2, 3, TOK])
                vtok = sb(st, "v_tok", [128, 2, 4, 128])
                ex = sb(st, "exps", [128, 2, 2, SEQ])
                wt_ = sb(st, "weights", [128, 2, SEQ])
                wT = sb(st, "weights_T", [128, 2, 4, 128])
                mx = sb(st, "row_max", [128, 2, 2])
                nmx = sb(st, "neg_max", [128, 2, 2])
                rs = sb(st, "row_sum", [128, 2, 2])
                ri = sb(st, "row_inv", [128, 2, 2])
                heads_in = [sem("head_in0"), sem("head_in1")]
                act_start = sem("turn_start")
                head_ok = sem("head_ok")
                by_head = qkv.rearrange("(c h) p n -> h p c n", c=3)

                def head_rows(h):
                    return by_head[bass.ds(h, 1), :, :, :].rearrange("o p c n -> p (o c) n")
                turns = [(hh, i) for hh in range(2) for i in range(4)]
                P = Steps(sem("att_pe"), [x for hh in range(2) for x in
                                          [f"vt{hh}", f"s{hh}0"] + [y for i in range(4) for y in
                                           ([f"s{hh}{i + 1}"] if i < 3 else []) + [f"t{hh}{i}", f"o{hh}{i}"]]])
                A = Steps(sem("att_act"), [x for hh in range(2) for x in [f"vt{hh}"] + [y for i in range(4) for y in
                                           (f"e{hh}{i}0", f"e{hh}{i}1", f"t{hh}{i}")] + [f"o{hh}"]])
                V_ = Steps(sem("att_dve"), [f"{y}{hh}{i}" for hh, i in turns for y in
                                            ("mask", "max", "neg", "inv", "invl", "w0_", "w1_")])
                with nc.Block() as block:
                    @block.vector
                    def _(dve):
                        dve.tensor_tensor(tmp[:, 0:1], V("lam_q"), V("lam_k"), ALU.mult).then_inc(ready.sem, 1)
                        dve.wait_ge(ready.sem, ready.at("prod"))
                        dve.tensor_scalar(tmp[:, 1:3], C("two"), tmp[:, 0:1], None, ALU.mult).then_inc(ready.sem, 1)
                        dve.wait_ge(ready.sem, ready.at("exp"))
                        dve.scalar_tensor_tensor(tmp[:, 3:4], lam_e[:, 0:1], LAM_INIT, lam_e[:, 1:2], ALU.add,
                                                 ALU.subtract).then_inc(ready.sem, 1)
                        dve.wait_ge(ready.sem, ready.at("lam"))
                        dve.tensor_scalar(neg_lam, tmp[:, 3:4], -1.0, None, ALU.mult).then_inc(ready.sem, 1)
                        dve.tensor_scalar(sub_g, V("subln"), 1.0 - LAM_INIT, None, ALU.mult).then_inc(ready.sem, 1)
                        dve.wait_ge(ready.sem, ready.at("g"))

                    @block.tensor
                    def _(pe):
                        pe.wait_ge(ready.sem, ready.at("rhs"))
                        pe.matmul(ps[:, 7, 0:2], C("ones"), tmp[:, 1:3], start=True, stop=True).then_inc(ready.sem, 1)

                    @block.scalar
                    def _(act):
                        act.wait_ge(ready.sem, ready.at("sum"))
                        act.activation(lam_e, ps[:, 7, 0:2], ACT.Exp).then_inc(ready.sem, 1)

                    @block.sync
                    def _(sp):
                        for u in range(2):
                            sp.dma_start(qh[:, u, :, :], head_rows(u)).then_inc(heads_in[u], 16)

                with nc.Block() as block:
                    @block.sync
                    def _(sp):
                        with sp.Fori(0, 3) as t:
                            for u in range(2):
                                sp.wait_ge(P.sem, t * len(P.names) + P.at(f"s{u}3"))
                                sp.dma_start(qh[:, u, :, :], head_rows(t * 2 + (2 + u))).then_inc(heads_in[u], 16)

                    @block.tensor
                    def _(pe):
                        def at(t, steps, name):
                            return t * len(steps.names) + steps.at(name)

                        def scores(t, hh, i):
                            n = turns.index((hh, i))
                            if n >= 2:
                                pe.wait_ge(A.sem, at(t, A, "e%d%d1" % turns[n - 2]))
                            else:
                                pe.wait_ge(act_start, t + 1)
                            for c in range(2):
                                q = qh[64 * c:64 * c + 64, hh, 0, i * 128:i * 128 + 128]
                                k = qh[64 * c:64 * c + 64, hh, 1, 0:(i + 1) * 128]
                                mm = pe.matmul(ps[:, 2 * (i % 2) + c, 0:(i + 1) * 128], q, k, start=True, stop=True)
                            mm.then_inc(P.sem, 1)

                        with pe.Fori(0, 4) as t:
                            for hh in range(2):
                                pe.wait_ge(heads_in[hh], t * 16 + 16)
                                pe.wait_ge(head_ok, t * 2 + hh + 1)
                                for i in range(4):
                                    mm = pe.transpose(ps[:, 5, i * 128:i * 128 + 128], qh[:, hh, 2, i * 128:i * 128 + 128], C("ident"))
                                mm.then_inc(P.sem, 1)
                                scores(t, hh, 0)
                                for i in range(4):
                                    if i < 3:
                                        scores(t, hh, i + 1)
                                    pe.wait_ge(V_.sem, at(t, V_, f"w1_{hh}{i}"))
                                    if (hh, i) != (0, 0):
                                        pe.wait_ge(A.sem, at(t, A, "t%d%d" % turns[turns.index((hh, i)) - 1]))
                                    for s in range(i + 1):
                                        mm = pe.transpose(ps[:, 4, s * 128:s * 128 + 128], wt_[:, i % 2, s * 128:s * 128 + 128], C("ident"))
                                    mm.then_inc(P.sem, 1)
                                    pe.wait_ge(A.sem, at(t, A, f"t{hh}{i}"))
                                    if i == 0 and hh == 1:
                                        pe.wait_ge(A.sem, at(t, A, "o0"))
                                    for s in range(i + 1):
                                        mm = pe.matmul(ps[:, 6, i * 128:i * 128 + 128], vtok[:, hh, s, :], wT[:, i % 2, s, :],
                                                       start=(s == 0), stop=(s == i))
                                    mm.then_inc(P.sem, 1)

                    @block.scalar
                    def _(act):
                        def at(t, steps, name):
                            return t * len(steps.names) + steps.at(name)
                        with act.Fori(0, 4) as t:
                            act.sem_inc(act_start, 1)
                            act.sem_inc(head_ok, 1)
                            for hh in range(2):
                                act.wait_ge(P.sem, at(t, P, f"vt{hh}"))
                                act.activation(vtok[:, hh, :, :], ps[:, 5, :], ACT.Copy).then_inc(A.sem, 1)
                                for i in range(4):
                                    n = (i + 1) * 128
                                    act.wait_ge(V_.sem, at(t, V_, f"neg{hh}{i}"))
                                    for c in range(2):
                                        act.activation(ex[:, i % 2, c, 0:n], ps[:, 2 * (i % 2) + c, 0:n], ACT.Exp,
                                                       bias=nmx[:, i % 2, c:c + 1], scale=0.125,
                                                       accum_out=rs[:, i % 2, c:c + 1]).then_inc(A.sem, 1)
                                    act.wait_ge(P.sem, at(t, P, f"t{hh}{i}"))
                                    act.activation(wT[:, i % 2, 0:i + 1, :], ps[:, 4, 0:n], ACT.Copy).then_inc(A.sem, 1)
                                act.wait_ge(P.sem, at(t, P, f"o{hh}3"))
                                act.activation(yd[:, bass.ds(t * 2 + hh, 1), 0:SEQ].rearrange("p o n -> p (o n)"), ps[:, 6, :],
                                               ACT.Copy).then_inc(A.sem, 1)
                                if hh == 0:
                                    act.wait_ge(A.sem, at(t, A, "o0"))
                                    act.sem_inc(head_ok, 1)
                                else:
                                    act.wait_ge(A.sem, at(t, A, "o1"))

                    @block.vector
                    def _(dve):
                        def at(t, steps, name):
                            return t * len(steps.names) + steps.at(name)
                        with dve.Fori(0, 4) as t:
                            for hh, i in turns:
                                n, b = (i + 1) * 128, i % 2
                                dve.wait_ge(P.sem, at(t, P, f"s{hh}{i}"))
                                diag = ps[:, 2 * b:2 * b + 2, i * 128:n]
                                mask = C("causal").unsqueeze(1).to_broadcast([128, 2, 128])
                                dve.tensor_tensor(diag, diag, mask, ALU.add).then_inc(V_.sem, 1)
                                dve.wait_ge(V_.sem, at(t, V_, f"mask{hh}{i}"))
                                dve.reduce_max(mx[:, b, :], ps[:, 2 * b:2 * b + 2, 0:n], AX.X).then_inc(V_.sem, 1)
                                dve.wait_ge(V_.sem, at(t, V_, f"max{hh}{i}"))
                                dve.tensor_scalar(nmx[:, b, :], mx[:, b, :], -0.125, None, ALU.mult).then_inc(V_.sem, 1)
                                dve.wait_ge(A.sem, at(t, A, f"e{hh}{i}1"))
                                dve.reciprocal(ri[:, b, :], rs[:, b, :]).then_inc(V_.sem, 1)
                                dve.wait_ge(V_.sem, at(t, V_, f"inv{hh}{i}"))
                                dve.tensor_tensor(ri[:, b, 1:2], ri[:, b, 1:2], neg_lam, ALU.mult).then_inc(V_.sem, 1)
                                turn = turns.index((hh, i))
                                if turn >= 2:
                                    dve.wait_ge(P.sem, at(t, P, "t%d%d" % turns[turn - 2]))
                                dve.tensor_scalar(wt_[:, b, 0:n], ex[:, b, 0, 0:n], ri[:, b, 0:1], None, ALU.mult).then_inc(V_.sem, 1)
                                dve.wait_ge(V_.sem, at(t, V_, f"w0_{hh}{i}"))
                                dve.scalar_tensor_tensor(wt_[:, b, 0:n], ex[:, b, 1, 0:n], ri[:, b, 1:2], wt_[:, b, 0:n],
                                                         ALU.mult, ALU.add).then_inc(V_.sem, 1)

            if upto <= 2:
                with nc.Block() as block:
                    @block.sync
                    def _(sp):
                        s_ = sem("dbg")
                        sp.dma_start(ymix[8:16, :, 0:SEQ].rearrange("k p n -> p k n"), yd[:, :, 0:SEQ]).then_inc(s_, 16)
                        sp.wait_ge(s_, 16)
                return

            with ExitStack() as st:
                HC = 2 * DA_HEADS
                tab = sb(st, "page_ids", [1, NS * PAGES], i32)
                qs = sb(st, "qkv_s", [128, 24, NS])
                qbd = sb(st, "q_blocks", [128, NS, DA_HEADS, 2])
                ring = sb(st, "page_ring", [128, 4, RW])
                sc = sb(st, "scores_s", [128, NS, PAGES, HC])
                prod = sb(st, "qk_new", [128, DA_HEADS, NS])
                snew = sb(st, "score_new", [128, NS, DA_HEADS, 2])
                m1 = sb(st, "max_pages", [128, NS, HC])
                mall = sb(st, "max_all", [128, 1])
                mdiag = sb(st, "max_diag", [128, 128])
                mb = sb(st, "max_rows", [128, NS, HC])
                enew = sb(st, "exp_new", [128, NS, HC])
                part = sb(st, "sum_pages", [128, NS, HC])
                tot = sb(st, "sum_all", [128, NS, DA_HEADS, 2])
                wn2 = sb(st, "w_new2", [128, NS, DA_HEADS, 2])
                wn = sb(st, "w_new", [128, NS, DA_HEADS])
                ws = sb(st, "w_pages", [128, NS, PAGES, DA_HEADS])
                ov = sb(st, "new_v", [128, NS, DA_HEADS])
                samp_in = sem("samp_in")
                q_ready = sem("q_blocks_ready")
                page_in = [sem(f"page_in{i}") for i in range(4)]
                page_used = sem("page_used")
                sums_out = sem("sums_out")
                flat = lambda a: a.rearrange("p a b -> p (a b)")
                flat3 = lambda a: a.rearrange("p a b c -> p (a b c)")

                with nc.Block() as block:
                    @block.sync
                    def _(sp):
                        sp.dma_start(tab[:, :], pages).then_inc(samp_in, 16)
                        sp.dma_start(qs[:, :, :], qkv[:, :, SEQ:TOK].rearrange("k p n -> p k n")).then_inc(samp_in, 16)
                        sp.wait_ge(samp_in, 32)

                    @block.tensor
                    def _(pe):
                        pe.sem_inc(page_used, 4)

                    @block.vector
                    def _(dve):
                        dve.sem_inc(sums_out, 2)
                        dve.memset(qbd[:, :, :, :], 0.0).then_inc(q_ready, 1)
                        dve.wait_ge(samp_in, 32)
                        dve.wait_ge(q_ready, 1)
                        for c in range(2):
                            half = slice(64 * c, 64 * c + 64)
                            dve.tensor_copy(qbd[half, :, :, c], qs[half, 0:8, :].rearrange("p h b -> p b h")).then_inc(q_ready, 1)
                        dve.tensor_tensor(prod[:, :, :], qs[:, 0:8, :], qs[:, 8:16, :], ALU.mult).then_inc(q_ready, 1)

                def load_pages(sp, cache, t, bb, g0):
                    for pg in range(PAGES):
                        n = t * 32 + (bb * PAGES + pg)
                        sp.wait_ge(page_used, n + (g0 + 1))
                        page = sp.value_load(tab[0:1, bass.ds(n, 1)], min_val=0, max_val=cache.shape[0] - 1)
                        src = cache[bass.ds(page, 1), :, :, :].rearrange("o p a b -> p (o a b)")
                        sp.dma_start(ring[:, pg % 4, :], src).then_inc(page_in[pg % 4], 16)

                def page_product(pe, t, bb, g0, out, moving, values):
                    pe.wait_ge(sums_out, t * 2 + (bb + 1 + g0 // PAGES))
                    for pg in range(PAGES):
                        pe.wait_ge(page_in[pg % 4], t * 128 + (16 * (bb * 4 + pg // 4 + 1) + 4 * g0))
                        for h in range(DA_HEADS):
                            mm = pe.matmul(out(bb, pg, h), ring[:, pg % 4, h * 128:h * 128 + 128], moving(t * 2 + bb, pg, h),
                                           start=(pg == 0 and h == 0) if values else True,
                                           stop=(pg == PAGES - 1) if values else True, skip_group_check=values)
                        mm.then_inc(page_used, 1)

                def pass_block(cache, g0, out, moving, values, leave):
                    with nc.Block() as block:
                        @block.sync
                        def _(sp):
                            with sp.Fori(0, NS // 2) as t:
                                for bb in range(2):
                                    load_pages(sp, cache, t, bb, g0)

                        @block.tensor
                        def _(pe):
                            with pe.Fori(0, NS // 2) as t:
                                for bb in range(2):
                                    page_product(pe, t, bb, g0, out, moving, values)

                        @block.vector
                        def _(dve):
                            with dve.Fori(0, NS // 2) as t:
                                for bb in range(2):
                                    dve.wait_ge(page_used, t * 32 + (4 + g0 + (bb + 1) * PAGES))
                                    leave(dve, t * 2 + bb, bb)

                def k_out(bb, pg, h):
                    return ps[:, 6 + bb, pg * HC + 2 * h:pg * HC + 2 * h + 2]

                def k_moving(b, pg, h):
                    return qbd[:, bass.ds(b, 1), h, :].rearrange("p o c -> p (o c)")

                def k_leave(dve, b, bb):
                    dve.tensor_copy(sc[:, bass.ds(b, 1), :, :].rearrange("p o a c -> p (o a c)"),
                                    ps[:, 6 + bb, 0:PAGES * HC]).then_inc(sums_out, 1)

                pass_block(kc, 0, k_out, k_moving, False, k_leave)

                S = Steps(sem("soft_steps"), ["snew_mm", "snew", "m1", "m1_T", "mall", "mdiag", "mb_mm", "mb", "sub", "sub_new",
                                              "exp", "exp_new", "part", "sum_mm", "tot", "inv", "lam", "w2", "wn2", "ws", "wn", "ov"])
                with nc.Block() as block:
                    @block.tensor
                    def _(pe):
                        for c in range(2):
                            mm = pe.matmul(ps[:, 5, c * 64:c * 64 + 64], C("halves")[:, c * 128:c * 128 + 128],
                                           flat(prod[:, :, :]), start=True, stop=True)
                        mm.then_inc(S.sem, 1)
                        pe.wait_ge(S.sem, S.at("m1"))
                        pe.transpose(ps[:, 4, 0:128], flat(m1[:, :, :]), C("ident")).then_inc(S.sem, 1)
                        pe.wait_ge(S.sem, S.at("mdiag"))
                        pe.matmul(ps[:, 4, 128:256], C("ones"), mdiag[:, :], start=True, stop=True).then_inc(S.sem, 1)
                        pe.wait_ge(S.sem, S.at("part"))
                        pe.matmul(ps[:, 4, 256:384], C("ones"), flat(part[:, :, :]), start=True, stop=True).then_inc(S.sem, 1)

                    @block.scalar
                    def _(act):
                        act.wait_ge(S.sem, S.at("sub_new"))
                        e = sc[:, :, :, :].rearrange("p b g k -> p (b g k)")
                        act.activation(e, e, ACT.Exp, scale=0.125).then_inc(S.sem, 1)
                        act.wait_ge(S.sem, S.at("exp"))
                        act.activation(flat(enew[:, :, :]), flat(enew[:, :, :]), ACT.Exp, scale=0.125).then_inc(S.sem, 1)

                    @block.vector
                    def _(dve):
                        def did(ins, name):
                            ins.then_inc(S.sem, 1)
                            dve.wait_ge(S.sem, S.at(name))
                        dve.wait_ge(S.sem, S.at("snew_mm"))
                        did(dve.tensor_copy(snew[:, :, :, :].rearrange("p b h c -> p c h b"),
                                            ps[:, 5, 0:128].rearrange("p (c h b) -> p c h b", c=2, h=8)), "snew")
                        did(dve.reduce_max(m1[:, :, :], sc[:, :, :, :].rearrange("p b g k -> p b k g"), AX.X), "m1")
                        dve.wait_ge(S.sem, S.at("m1_T"))
                        did(dve.reduce_max(mall[:, :], ps[:, 4, 0:128], AX.X), "mall")
                        did(dve.tensor_scalar(mdiag[:, :], C("ident"), mall[:, :], None, ALU.mult), "mdiag")
                        dve.wait_ge(S.sem, S.at("mb_mm"))
                        did(dve.tensor_tensor(flat(mb[:, :, :]), ps[:, 4, 128:256], flat3(snew[:, :, :, :]), ALU.max), "mb")
                        did(dve.tensor_tensor(sc[:, :, :, :], sc[:, :, :, :],
                                              mb[:, :, :].unsqueeze(2).to_broadcast([128, NS, PAGES, HC]), ALU.subtract), "sub")
                        did(dve.tensor_tensor(flat(enew[:, :, :]), flat3(snew[:, :, :, :]), flat(mb[:, :, :]), ALU.subtract), "sub_new")
                        dve.wait_ge(S.sem, S.at("exp_new"))
                        did(dve.reduce_sum(part[:, :, :], sc[:, :, :, :].rearrange("p b g k -> p b k g"), AX.X), "part")
                        dve.wait_ge(S.sem, S.at("sum_mm"))
                        did(dve.tensor_tensor(flat3(tot[:, :, :, :]), ps[:, 4, 256:384], flat(enew[:, :, :]), ALU.add), "tot")
                        did(dve.reciprocal(flat3(tot[:, :, :, :]), flat3(tot[:, :, :, :])), "inv")
                        did(dve.tensor_scalar(tot[:, :, :, 1], tot[:, :, :, 1], neg_lam, None, ALU.mult), "lam")
                        inv = tot[:, :, :, :].rearrange("p b h c -> p b (h c)")
                        did(dve.tensor_tensor(sc[:, :, :, :], sc[:, :, :, :],
                                              inv.unsqueeze(2).to_broadcast([128, NS, PAGES, HC]), ALU.mult), "w2")
                        did(dve.tensor_tensor(flat3(wn2[:, :, :, :]), flat(enew[:, :, :]), flat3(tot[:, :, :, :]), ALU.mult), "wn2")
                        pair = sc[:, :, :, :].rearrange("p b g (h c) -> p (b g) h c", c=2)
                        did(dve.tensor_tensor(ws[:, :, :, :].rearrange("p b g h -> p (b g) h"), pair[:, :, :, 0], pair[:, :, :, 1],
                                              ALU.add), "ws")
                        did(dve.tensor_tensor(wn[:, :, :], wn2[:, :, :, 0], wn2[:, :, :, 1], ALU.add), "wn")
                        did(dve.tensor_tensor(ov[:, :, :], qs[:, 16:24, :].rearrange("p h b -> p b h"), wn[:, :, :], ALU.mult), "ov")

                def v_out(bb, pg, h):
                    return ps[:, 6 + bb, h:h + 1]

                def v_moving(b, pg, h):
                    return ws[:, bass.ds(b, 1), pg, h:h + 1].rearrange("p o c -> p (o c)")

                def v_leave(dve, b, bb):
                    dve.tensor_tensor(yd[:, :, bass.ds(b + SEQ, 1)].rearrange("p h o -> p (h o)"), ps[:, 6 + bb, 0:DA_HEADS],
                                      ov[:, bass.ds(b, 1), :].rearrange("p o h -> p (o h)"), ALU.add).then_inc(sums_out, 1)

                pass_block(vc.rearrange("g p h d -> g p h d"), 128, v_out, v_moving, True, v_leave)

            with ExitStack() as st:
                sq = sb(st, "yd_sq", [128, 2, TOK])
                rn = sb(st, "yd_rms", [128, 2, TOK])
                y_out = sem("y_out")
                NQ = Steps(sem("subln_act"), [f"{x}{h}" for h in range(8) for x in ("sq", "rt")])
                NP = Steps(sem("subln_pe"), [f"mm{h}" for h in range(8)])
                NV = Steps(sem("subln_dve"), [f"{x}{h}" for h in range(8) for x in ("ms0_", "ms1_", "inv", "y")])
                with nc.Block() as block:
                    @block.scalar
                    def _(act):
                        def square(h):
                            if h >= 2:
                                act.wait_ge(NP.sem, NP.at(f"mm{h - 2}"))
                            act.activation(sq[:, h % 2, :], yd[:, h, :], ACT.Square).then_inc(NQ.sem, 1)
                        for h in range(8):
                            square(h)
                            act.wait_ge(NV.sem, NV.at(f"ms1_{h}"))
                            act.activation(rn[:, h % 2, :], rn[:, h % 2, :], ACT.Sqrt).then_inc(NQ.sem, 1)

                    @block.tensor
                    def _(pe):
                        for h in range(8):
                            pe.wait_ge(NQ.sem, NQ.at(f"sq{h}"))
                            if h >= 2:
                                pe.wait_ge(NV.sem, NV.at(f"ms1_{h - 2}"))
                            for i, (a, m) in enumerate(SPANS):
                                mm = pe.matmul(ps[:, 2 * (h % 2) + i, 0:m], C("ones"), sq[:, h % 2, a:a + m], start=True, stop=True)
                            mm.then_inc(NP.sem, 1)

                    @block.vector
                    def _(dve):
                        for h in range(8):
                            dve.wait_ge(NP.sem, NP.at(f"mm{h}"))
                            for i, (a, m) in enumerate(SPANS):
                                dve.tensor_scalar(rn[:, h % 2, a:a + m], ps[:, 2 * (h % 2) + i, 0:m], 1.0 / 128, 1e-6,
                                                  ALU.mult, ALU.add).then_inc(NV.sem, 1)
                            dve.wait_ge(NQ.sem, NQ.at(f"rt{h}"))
                            dve.reciprocal(rn[:, h % 2, :], rn[:, h % 2, :]).then_inc(NV.sem, 1)
                            dve.wait_ge(NV.sem, NV.at(f"inv{h}"))
                            dve.scalar_tensor_tensor(yd[:, h, :], yd[:, h, :], sub_g, rn[:, h % 2, :],
                                                     ALU.mult, ALU.mult).then_inc(NV.sem, 1)

                    @block.sync
                    def _(sp):
                        for h in range(8):
                            sp.wait_ge(NV.sem, NV.at(f"y{h}"))
                            sp.dma_start(ymix[8 + h, :, :], yd[:, h, :]).then_inc(y_out, 16)
                        sp.wait_ge(y_out, 128)
            attn.close()
            if upto <= 3:
                return

            tile_r, tile_k, tile_v = rkv[:, 0:RT, :], rkv[:, RT:2 * RT, :], rkv[:, 2 * RT:3 * RT, :]
            au = sb(mixing, "iclr", [128, RT, TOK])
            kk = sb(mixing, "kk", [128, RT, TOK])
            cum = sb(mixing, "cum", [128, RT, TOK])
            g2s = sb(mixing, "g2s", [128, RW])
            flat = lambda a: a.rearrange("p a b -> p (a b)")
            lora_in = sem("lora_in")
            with ExitStack() as st:
                wa = sb(st, "w2a2s", [128, RW])
                sq = sb(st, "kk_sq", [128, 2, TOK])
                nr = sb(st, "kk_norm", [128, 2, TOK])
                tk = sb(st, "k_gain", [128, TOK])
                A = Steps(sem("prep_act"), ["tanh", "sig"] + [f"{x}{j}" for j in range(RT) for x in ("w0_", "w1_", "a0_", "a1_")]
                          + [f"rt{j}" for j in range(RT)])
                P = Steps(sem("prep_pe"), [f"{x}{j}" for j in range(RT) for x in ("w", "a")] + [f"n{j}" for j in range(RT)])
                W = Steps(sem("prep_dve"), ["kk0", "sq0"] + [f"{x}{j}" for j in range(RT) for x in
                          ("m0_", "m1_", "inv", "kn", "t", "kmod", "b", "cum")
                          + (("nkk", "nsq") if j + 1 < RT else ())])
                with nc.Block() as block:
                    @block.sync
                    def _(sp):
                        sp.dma_start(wa[:, :], w2a2).then_inc(lora_in, 16)
                        sp.dma_start(g2s[:, :], g2).then_inc(lora_in, 16)

                    @block.scalar
                    def _(act):
                        act.activation(rkv[0:64, 24, :], rkv[0:64, 24, :], ACT.Tanh).then_inc(A.sem, 1)
                        act.activation(rkv[:, 25, :], rkv[:, 25, :], ACT.Sigmoid).then_inc(A.sem, 1)
                        for j in range(RT):
                            for x, (out, bias) in enumerate(((cum, "w0"), (au, "a0"))):
                                act.wait_ge(P.sem, P.at("wa"[x] + str(j)))
                                for i, (a, m) in enumerate(SPANS):
                                    act.activation(out[:, j, a:a + m], ps[:, 4 * (j % 2) + 2 * x + i, 0:m], ACT.Sigmoid,
                                                   bias=V(bias, j)).then_inc(A.sem, 1)
                        for j in range(RT):
                            act.wait_ge(W.sem, W.at(f"m1_{j}"))
                            act.activation(nr[:, j % 2, :], nr[:, j % 2, :], ACT.Sqrt).then_inc(A.sem, 1)

                    @block.tensor
                    def _(pe):
                        pe.wait_ge(lora_in, 32)
                        pe.wait_ge(A.sem, A.at("tanh"))
                        for j in range(RT):
                            for x in range(2):
                                if j >= 2:
                                    pe.wait_ge(A.sem, A.at("wa"[x] + f"1_{j - 2}"))
                                half = slice(64 * x, 64 * x + 64)
                                for i, (a, m) in enumerate(SPANS):
                                    mm = pe.matmul(ps[:, 4 * (j % 2) + 2 * x + i, 0:m], wa[half, j * 128:j * 128 + 128],
                                                   rkv[half, 24, a:a + m], start=True, stop=True)
                                mm.then_inc(P.sem, 1)
                        for j in range(RT):
                            pe.wait_ge(W.sem, W.at("sq0") if j == 0 else W.at(f"nsq{j - 1}"))
                            if j < 2:
                                pe.wait_ge(A.sem, A.at(f"w1_{RT - 2 + j}"))
                            else:
                                pe.wait_ge(W.sem, W.at(f"m1_{j - 2}"))
                            for i, (a, m) in enumerate(SPANS):
                                mm = pe.matmul(ps[:, 4 * (j % 2) + i, 0:m], C("pair"), sq[:, j % 2, a:a + m], start=True, stop=True)
                            mm.then_inc(P.sem, 1)

                    @block.vector
                    def _(dve):
                        def did(ins, name):
                            ins.then_inc(W.sem, 1)
                            dve.wait_ge(W.sem, W.at(name))

                        def squares(j, a, b):
                            did(dve.tensor_scalar(kk[:, j, :], tile_k[:, j, :], V("k_k", j), None, ALU.mult), a)
                            if j >= 2:
                                dve.wait_ge(P.sem, P.at(f"n{j - 2}"))
                            did(dve.tensor_tensor(sq[:, j % 2, :], kk[:, j, :], kk[:, j, :], ALU.mult), b)
                        squares(0, "kk0", "sq0")
                        for j in range(RT):
                            dve.wait_ge(P.sem, P.at(f"n{j}"))
                            for i, (a, m) in enumerate(SPANS):
                                dve.tensor_scalar(nr[:, j % 2, a:a + m], ps[:, 4 * (j % 2) + i, 0:m], 1e-24, None,
                                                  ALU.max).then_inc(W.sem, 1)
                            dve.wait_ge(A.sem, A.at(f"rt{j}"))
                            did(dve.reciprocal(nr[:, j % 2, :], nr[:, j % 2, :]), f"inv{j}")
                            did(dve.tensor_tensor(kk[:, j, :], kk[:, j, :], nr[:, j % 2, :], ALU.mult), f"kn{j}")
                            did(dve.tensor_scalar(tk[:, :], au[:, j, :], -1.0, V("k_a", j), ALU.add, ALU.mult), f"t{j}")
                            did(dve.scalar_tensor_tensor(tile_k[:, j, :], tk[:, :], 1.0, tile_k[:, j, :], ALU.add, ALU.mult), f"kmod{j}")
                            did(dve.tensor_tensor(au[:, j, :], kk[:, j, :], au[:, j, :], ALU.mult), f"b{j}")
                            did(dve.tensor_tensor_scan(cum[:, j, :], C("start"), cum[:, j, :], 0.0, ALU.mult, ALU.add), f"cum{j}")
                            if j + 1 < RT:
                                squares(j + 1, f"nkk{j}", f"nsq{j}")

            with ExitStack() as st:
                sv = sb(st, "step_in", [128, 6, 2, 64])
                tv = sb(st, "step_vecs", [128, 6, 64])
                state = sb(st, "step_state", [128, 64, 64])
                prod = sb(st, "step_prod", [128, 64, 64])
                dec = sb(st, "step_decay", [128, RT, NS])
                sa = sb(st, "step_sa", [128, 64])
                yb = sb(st, "step_y", [128, 64])
                yd2 = sb(st, "step_y2", [128, 128])
                state_in, state_out = sem("state_in"), sem("state_out")
                S = Steps(sem("step"), ["dec"] + [f"v{i}" for i in range(6)] + ["T", "ta", "tb", "Sa", "sa", "Sw", "sab", "S1",
                                        "vk", "S2", "Sr", "y", "y0", "ya", "yb", "yT", "t2", "t2r", "oa", "ob"])
                with nc.Block() as block:
                    @block.sync
                    def _(sp):
                        sp.dma_start(state[:, :, :], s0).then_inc(state_in, 16)
                        sp.wait_ge(S.sem, S.at("S2"))
                        sp.dma_start(wkv_s, state[:, :, :]).then_inc(state_out, 16)
                        sp.wait_ge(state_out, 16)

                    @block.scalar
                    def _(act):
                        act.activation(dec[:, :, :], cum[:, :, SEQ:TOK], ACT.Exp, scale=-DECAY).then_inc(S.sem, 1)

                    @block.tensor
                    def _(pe):
                        pe.wait_ge(S.sem, S.at("v5"))
                        for i in range(6):
                            mm = pe.transpose(ps[:, i // 4, i % 4 * 128:i % 4 * 128 + 128], sv[:, i, :, :].rearrange("p a b -> p (a b)"),
                                              C("ident"))
                        mm.then_inc(S.sem, 1)
                        pe.wait_ge(S.sem, S.at("yb"))
                        pe.transpose(ps[:, 2, 0:128], yd2[:, :], C("ident")).then_inc(S.sem, 1)

                    @block.vector
                    def _(dve):
                        def did(ins, name):
                            ins.then_inc(S.sem, 1)
                            dve.wait_ge(S.sem, S.at(name))
                        dve.wait_ge(S.sem, S.at("dec"))
                        rows = [kk[:, :, SEQ:TOK], dec[:, :, :], au[:, :, SEQ:TOK], tile_k[:, :, SEQ:TOK], tile_v[:, :, SEQ:TOK],
                                tile_r[:, :, SEQ:TOK]]
                        for i, v in enumerate(rows):
                            did(dve.tensor_copy(sv[:, i, :, :].rearrange("p t (a b) -> p t a b", a=RT),
                                                v.unsqueeze(1).to_broadcast([128, 2, RT, NS])), f"v{i}")
                        dve.wait_ge(S.sem, S.at("T"))
                        both = ps[:, 0:2, :].rearrange("p a (b c) -> p (a b) c", b=4)
                        did(dve.tensor_copy(tv[0:64, :, :], both[0:64, 0:6, 0:64]), "ta")
                        did(dve.tensor_copy(tv[64:128, :, :], both[64:128, 0:6, 64:128]), "tb")
                        cols = lambda i: tv[:, i, :].unsqueeze(1).to_broadcast([128, 64, 64])
                        rows_ = lambda a: a.unsqueeze(2).to_broadcast([128, 64, 64])
                        st_, pr = state[:, :, :], prod[:, :, :]
                        dve.wait_ge(state_in, 16)
                        did(dve.tensor_tensor(pr, st_, cols(0), ALU.mult), "Sa")
                        did(dve.reduce_sum(sa[:, :], pr, AX.X), "sa")
                        did(dve.tensor_tensor(st_, st_, cols(1), ALU.mult), "Sw")
                        did(dve.tensor_tensor(pr, rows_(sa[:, :]), cols(2), ALU.mult), "sab")
                        did(dve.tensor_tensor(st_, st_, pr, ALU.subtract), "S1")
                        did(dve.tensor_tensor(pr, rows_(tv[:, 4, :]), cols(3), ALU.mult), "vk")
                        did(dve.tensor_tensor(st_, st_, pr, ALU.add), "S2")
                        did(dve.tensor_tensor(pr, st_, cols(5), ALU.mult), "Sr")
                        did(dve.reduce_sum(yb[:, :], pr, AX.X), "y")
                        did(dve.memset(yd2[:, :], 0.0), "y0")
                        did(dve.tensor_copy(yd2[0:64, 0:64], yb[0:64, :]), "ya")
                        did(dve.tensor_copy(yd2[64:128, 64:128], yb[64:128, :]), "yb")
                        dve.wait_ge(S.sem, S.at("yT"))
                        last_r, last_a = tile_r[:, :, SEQ:TOK], au[:, :, SEQ:TOK]
                        rk = vt[:, VEC["r_k"]:VEC["r_k"] + RT].unsqueeze(2).to_broadcast([128, RT, NS])
                        did(dve.tensor_tensor(last_a, last_r, tile_k[:, :, SEQ:TOK], ALU.mult), "t2")
                        did(dve.tensor_tensor(last_a, last_a, rk, ALU.mult), "t2r")
                        for x, name in ((0, "oa"), (64, "ob")):
                            did(dve.tensor_copy(last_r[x:x + 64], ps[x:x + 64, 2, x:x + 64].rearrange("p (a b) -> p a b", a=RT)), name)

            with ExitStack() as st:
                e65 = sb(st, "decay", [128, RT, CH + 1])
                ei = sb(st, "decay_inv", [128, RT, CH])
                stg = sb(st, "chunk", [128, RT, 4, CH])
                vst = sb(st, "chunk_v", [128, RT, 2, CH])
                qa = sb(st, "rhs_left", [128, 2, RT, CH])
                gr = sb(st, "out_right", [128, 2, RT, CH])
                sl = sb(st, "inverse", [128, 2, 6, 4 * 128])
                xs = sb(st, "solve", [128, RT, 128])
                svb = sb(st, "state_v", [128, 2, RT, CH])
                zb = sb(st, "sa_v", [128, 2, RT, CH])
                sbd = sb(st, "state_diag", [128, RT, 128])
                rh = sb(st, "rhs", [128, RT, CH])
                bk = sb(st, "bk_tok", [128, RT, 128])
                turn_ok = sem("turn_ok")
                zeroed = sem("zeroed")
                pool_woke = sem("pool_woke")
                A = Steps(sem("rw_act"), ["E", "Ei", "qa_a", "qa_b"] + [f"{x}{q}" for x in ("D2t", "D4t", "Nt", "XDt", "N2t", "N4t", "X")
                                                                      for q in range(2)] + ["bk", "v1", "v2", "v3", "v4", "rhs", "za", "y", "sd_a", "sd_b"])
                P = Steps(sem("rw_pe"), [f"mg{q}" for q in range(2)] + [f"{x}{q}" for xs_ in (("D2", "D2t"), ("D4t", "DX"), ("DXX",),
                          ("N", "Nt"), ("XDt",), ("N2", "N2t"), ("N4t", "NY"), ("NYY",), ("X",)) for q in range(2) for x in xs_]
                          + ["bk", "v", "rhs", "sa", "y", "s"])
                W = Steps(sem("rw_dve"), ["at", "rt", "u2a", "u3a", "u2b", "u3b"] + [f"{x}{q}" for q in range(2) for x in
                          ("dA", "dB", "tA", "tB", "oA", "oB", "x1", "gA", "gB", "kA", "kB")] +
                          [f"{x}{q}" for xs_ in (("D2",), ("X2",), ("XD",), ("N", "Y1"), ("N2",), ("Y2",), ("Y3",)) for q in range(2) for x in xs_]
                          + ["zb", "sA", "sB", "swA", "swB"])
                G = Steps(sem("rw_pool"), ["vst", "t2", "t2r"])

                def at(c, steps, name):
                    return c * len(steps.names) + steps.at(name)

                def chunk(t, c):
                    return t[:, :, bass.ds(c * CH, CH)]

                def blocks(t):
                    return t.rearrange("p (a b) -> p a b", a=4)

                AA, BB = slice(0, 64), slice(64, 128)
                with nc.Block() as block:
                    @block.vector
                    def _(dve):
                        dve.memset(sl[:, :, :, :], 0.0).then_inc(zeroed, 1)
                        dve.memset(svb[:, :, :, :], 0.0).then_inc(zeroed, 1)
                        dve.memset(sbd[:, :, :], 0.0).then_inc(zeroed, 1)
                        dve.memset(e65[:, :, 0:1], 1.0).then_inc(zeroed, 1)
                        dve.sem_inc(turn_ok, 1)

                with nc.Block() as block:
                    @block.gpsimd
                    def _(pool):
                        with pool.Fori(0, NCH) as c:
                            pool.wait_ge(turn_ok, c + 1)
                            pool.tensor_copy(vst[:, :, :, :], chunk(tile_v, c).unsqueeze(2).to_broadcast([128, RT, 2, CH])).then_inc(G.sem, 1)
                            pool.wait_ge(W.sem, at(c, W, "u3b"))
                            pool.sem_inc(pool_woke, 1)
                            pool.tensor_tensor(chunk(au, c), chunk(tile_r, c), chunk(tile_k, c), ALU.mult).then_inc(G.sem, 1)
                            pool.wait_ge(G.sem, at(c, G, "t2"))
                            pool.sem_inc(pool_woke, 1)
                            rk = vt[:, VEC["r_k"]:VEC["r_k"] + RT].unsqueeze(2).to_broadcast([128, RT, CH])
                            pool.tensor_tensor(chunk(au, c), chunk(au, c), rk, ALU.mult).then_inc(G.sem, 1)

                    @block.scalar
                    def _(act):
                        with act.Fori(0, NCH) as c:
                            def leave(dst, bank_, name, q=""):
                                act.wait_ge(P.sem, at(c, P, f"{name}{q}"))
                                act.activation(dst, bank_, ACT.Copy).then_inc(A.sem, 1)
                            act.wait_ge(turn_ok, c + 1)
                            act.activation(e65[:, :, 1:CH + 1], chunk(cum, c), ACT.Exp, scale=-DECAY).then_inc(A.sem, 1)
                            act.activation(ei[:, :, :], chunk(cum, c), ACT.Exp, scale=DECAY).then_inc(A.sem, 1)
                            act.wait_ge(W.sem, at(c, W, "at"))
                            act.activation(qa[AA, 0, :, :], stg[AA, :, 0, :], ACT.Copy).then_inc(A.sem, 1)
                            act.activation(qa[BB, 1, :, :], stg[BB, :, 0, :], ACT.Copy).then_inc(A.sem, 1)
                            for name, slot, b in (("D2t", 5, 1), ("D4t", 0, 0), ("Nt", 1, 1), ("XDt", 4, 0), ("N2t", 3, 0), ("N4t", 0, 0)):
                                for q in range(2):
                                    leave(sl[:, q, slot, :], ps[:, 4 + 2 * q + b, :], name, q)
                            for q in range(2):
                                leave(xs[:, 4 * q:4 * q + 4, :], ps[:, 5 + 2 * q, :], "X", q)
                            leave(bk[:, :, :], ps[:, 0:2, :], "bk")
                            vv = ps[:, 2:4, :].rearrange("p a (b c) -> p (a b) c", b=4)
                            act.wait_ge(P.sem, at(c, P, "v"))
                            for t in (svb, zb):
                                act.activation(t[BB, 0, :, :], vv[BB, :, 0:64], ACT.Copy).then_inc(A.sem, 1)
                                act.activation(t[AA, 1, :, :], vv[AA, :, 64:128], ACT.Copy).then_inc(A.sem, 1)
                            leave(rh[:, :, :], ps[:, 4, :], "rhs")
                            act.wait_ge(P.sem, at(c, P, "sa"))
                            act.activation(zb[AA, 0, :, :], ps[AA, 5, :], ACT.Copy).then_inc(A.sem, 1)
                            act.wait_ge(G.sem, at(c, G, "t2r"))
                            act.wait_ge(P.sem, at(c, P, "y"))
                            act.activation(chunk(tile_r, c), ps[:, 6, :].rearrange("p (a b) -> p a b", a=RT), ACT.Copy).then_inc(A.sem, 1)
                            act.wait_ge(W.sem, at(c, W, "swB"))
                            act.activation(sbd[AA, :, 0:64], svb[AA, 0, :, :], ACT.Copy).then_inc(A.sem, 1)
                            act.activation(sbd[BB, :, 64:128], svb[BB, 1, :, :], ACT.Copy).then_inc(A.sem, 1)

                    @block.vector
                    def _(dve):
                        with dve.Fori(0, NCH) as c:
                            def mask(name, rows, n):
                                return C(name)[rows, 0:n].unsqueeze(1).to_broadcast([64, 4, n])

                            def did(ins, name):
                                ins.then_inc(W.sem, 1)
                                dve.wait_ge(W.sem, at(c, W, name))
                            dve.wait_ge(turn_ok, c + 1)
                            dve.wait_ge(A.sem, at(c, A, "E"))
                            did(dve.scalar_tensor_tensor(stg[:, :, 0, :], chunk(kk, c), -1.0, e65[:, :, 0:CH], ALU.mult, ALU.mult), "at")
                            did(dve.tensor_tensor(stg[:, :, 1, :], chunk(tile_r, c), e65[:, :, 1:CH + 1], ALU.mult), "rt")
                            dve.wait_ge(A.sem, at(c, A, "Ei"))
                            bu, ku = chunk(au, c), chunk(tile_k, c)
                            did(dve.tensor_tensor(stg[AA, :, 2, :], bu[AA], ei[AA, :, :], ALU.mult), "u2a")
                            did(dve.tensor_tensor(stg[AA, :, 3, :], ku[AA], ei[AA, :, :], ALU.mult), "u3a")
                            did(dve.tensor_tensor(stg[BB, :, 2, :], ku[BB], ei[BB, :, :], ALU.mult), "u2b")
                            did(dve.tensor_tensor(stg[BB, :, 3, :], bu[BB], ei[BB, :, :], ALU.mult), "u3b")
                            for q in range(2):
                                dve.wait_ge(P.sem, at(c, P, f"mg{q}"))
                                js = slice(4 * q, 4 * q + 4)
                                for slot, m, name, x in ((0, 0, "diag", "d"), (1, 1, "diag_t", "t"), (2, 1, "off_t", "o")):
                                    for rows, y, off in ((AA, "A", 0), (BB, "B", 64)):
                                        src = ps[rows, 4 * q + (off > 0), :].rearrange("p (a m b) -> p a m b", a=4, m=2)[:, :, m, :]
                                        did(dve.tensor_tensor(blocks(sl[rows, q, slot, :])[:, :, off:off + 64], src,
                                                              mask(name, rows, 64), ALU.mult), f"{x}{y}{q}")
                                did(dve.tensor_tensor(blocks(sl[:, q, 3, :]), blocks(sl[:, q, 0, :]),
                                                      C("ident").unsqueeze(1).to_broadcast([128, 4, 128]), ALU.add), f"x1{q}")
                                for y, b in (("A", 2), ("B", 3)):
                                    did(dve.tensor_tensor(gr[:, b - 2, js, :], blocks(ps[:, 4 * q + b, :])[:, :, 64:128],
                                                          C("gram")[:, 64:128].unsqueeze(1).to_broadcast([128, 4, 64]), ALU.mult), f"g{y}{q}")
                                for y, b, rows in (("A", 2, BB), ("B", 3, AA)):
                                    did(dve.tensor_tensor(qa[rows, b - 2, js, :], blocks(ps[rows, 4 * q + b, :])[:, :, 0:64],
                                                          mask("gram", rows, 64), ALU.mult), f"k{y}{q}")

                            def both(name, need, fn):
                                for q in range(2):
                                    dve.wait_ge(P.sem, at(c, P, f"{need}{q}"))
                                    did(fn(q), f"{name}{q}")
                            out = lambda q, b: ps[:, 4 + 2 * q + b, :]
                            both("D2", "D2", lambda q: dve.tensor_copy(sl[:, q, 4, :], out(q, 0)))
                            both("X2", "DX", lambda q: dve.tensor_tensor(sl[:, q, 3, :], out(q, 1), sl[:, q, 3, :], ALU.add))
                            both("XD", "DXX", lambda q: dve.tensor_tensor(sl[:, q, 3, :], out(q, 0), sl[:, q, 3, :], ALU.add))
                            for q in range(2):
                                dve.wait_ge(P.sem, at(c, P, f"N{q}"))
                                did(dve.tensor_copy(sl[:, q, 0, :], out(q, 0)), f"N{q}")
                                did(dve.tensor_tensor(blocks(sl[:, q, 5, :]), blocks(sl[:, q, 0, :]),
                                                      C("ident").unsqueeze(1).to_broadcast([128, 4, 128]), ALU.add), f"Y1{q}")
                            both("N2", "N2", lambda q: dve.tensor_copy(sl[:, q, 2, :], out(q, 1)))
                            both("Y2", "NY", lambda q: dve.tensor_tensor(sl[:, q, 5, :], out(q, 1), sl[:, q, 5, :], ALU.add))
                            both("Y3", "NYY", lambda q: dve.tensor_tensor(sl[:, q, 5, :], out(q, 0), sl[:, q, 5, :], ALU.add))
                            dve.wait_ge(P.sem, at(c, P, "sa"))
                            did(dve.tensor_copy(zb[BB, 1, :, :], ps[BB, 5, :]), "zb")
                            dve.wait_ge(P.sem, at(c, P, "s"))
                            halves = ((AA, 0, "A"), (BB, 1, "B"))
                            for rows, x, y in halves:
                                did(dve.tensor_tensor(svb[rows, x, :, :], ps[rows, 7, :].rearrange("p (a b) -> p a b", a=RT),
                                                      svb[rows, x, :, :], ALU.add), f"s{y}")
                            for rows, x, y in halves:
                                did(dve.tensor_tensor(svb[rows, x, :, :], svb[rows, x, :, :],
                                                      e65[rows, :, CH:CH + 1].to_broadcast([64, RT, CH]), ALU.mult), f"sw{y}")
                            dve.wait_ge(A.sem, at(c, A, "sd_b"))
                            dve.sem_inc(turn_ok, 1)

                    @block.tensor
                    def _(pe):
                        with pe.Fori(0, NCH) as c:
                            pe.wait_ge(W.sem, at(c, W, "u3b"))
                            for q in range(2):
                                for n in range(4):
                                    j = 4 * q + n
                                    for rows, b in ((AA, 2), (BB, 3)):
                                        pe.matmul(ps[:, 4 * q + b, n * 128:n * 128 + 128], stg[rows, j, 2:4, :], stg[rows, j, 0:2, :],
                                                  start=True, stop=True)
                                    for rows, unit, b in ((AA, 2, 0), (BB, 3, 1)):
                                        pe.matmul(ps[rows, 4 * q + b, n * 128:n * 128 + 64], stg[rows, j, unit, :], stg[rows, j, 0, :],
                                                  start=True, stop=True)
                                        mm = pe.matmul(ps[rows, 4 * q + b, n * 128 + 64:n * 128 + 128], stg[rows, j, 0, :],
                                                       stg[rows, j, unit, :], start=True, stop=True)
                                mm.then_inc(P.sem, 1)

                            def four(q, b, left, right):
                                for n in range(4):
                                    ns = slice(n * 128, n * 128 + 128)
                                    mm = pe.matmul(ps[:, 4 + 2 * q + b, ns], sl[:, q, left, ns], sl[:, q, right, ns], start=True, stop=True)
                                mm.then_inc(P.sem, 1)

                            for q in range(2):
                                pe.wait_ge(W.sem, at(c, W, "kB1"))
                                four(q, 0, 1, 0)
                                four(q, 1, 0, 1)
                            for q in range(2):
                                pe.wait_ge(W.sem, at(c, W, f"D2{q}"))
                                pe.wait_ge(A.sem, at(c, A, f"D2t{q}"))
                                four(q, 0, 4, 5)
                                four(q, 1, 5, 3)
                            for q in range(2):
                                pe.wait_ge(A.sem, at(c, A, f"D4t{q}"))
                                pe.wait_ge(W.sem, at(c, W, f"X2{q}"))
                                four(q, 0, 0, 3)
                            for q in range(2):
                                pe.wait_ge(W.sem, at(c, W, f"XD{q}"))
                                four(q, 0, 2, 3)
                                four(q, 1, 3, 2)
                            for q in range(2):
                                pe.wait_ge(W.sem, at(c, W, f"N{q}"))
                                for n in range(4):
                                    ns = slice(n * 128, n * 128 + 128)
                                    mm = pe.transpose(ps[:, 4 + 2 * q, ns], sl[:, q, 3, ns], C("ident"))
                                mm.then_inc(P.sem, 1)
                            for q in range(2):
                                pe.wait_ge(A.sem, at(c, A, f"Nt{q}"))
                                four(q, 1, 1, 0)
                                pe.wait_ge(A.sem, at(c, A, f"XDt{q}"))
                                four(q, 0, 0, 1)
                            for q in range(2):
                                pe.wait_ge(W.sem, at(c, W, f"N2{q}"))
                                pe.wait_ge(A.sem, at(c, A, f"N2t{q}"))
                                four(q, 0, 2, 3)
                                four(q, 1, 3, 5)
                            for q in range(2):
                                pe.wait_ge(A.sem, at(c, A, f"N4t{q}"))
                                pe.wait_ge(W.sem, at(c, W, f"Y2{q}"))
                                four(q, 0, 0, 5)
                            for q in range(2):
                                pe.wait_ge(W.sem, at(c, W, f"Y3{q}"))
                                four(q, 1, 4, 5)
                            for j in range(RT):
                                mm = pe.transpose(ps[:, j // 4, j % 4 * 128:j % 4 * 128 + 128], stg[:, j, 2:4, :], C("ident"))
                            mm.then_inc(P.sem, 1)
                            pe.wait_ge(G.sem, at(c, G, "vst"))
                            for j in range(RT):
                                mm = pe.transpose(ps[:, 2 + j // 4, j % 4 * 128:j % 4 * 128 + 128], vst[:, j, :, :], C("ident"))
                            mm.then_inc(P.sem, 1)

                            def heads(b, left, right):
                                for j in range(RT):
                                    for rows, x in ((AA, 0), (BB, 1)):
                                        mm = pe.matmul(ps[rows, b, j * 64:j * 64 + 64], left(x, j), right(x, j), start=True, stop=True)
                                mm.then_inc(P.sem, 1)
                            pe.wait_ge(A.sem, at(c, A, "v2"))
                            heads(4, lambda x, j: qa[:, x, j, :], lambda x, j: svb[:, x, j, :])
                            pe.wait_ge(A.sem, at(c, A, "rhs"))
                            for j in range(RT):
                                mm = pe.matmul(ps[:, 5, j * 64:j * 64 + 64], xs[:, j, :], rh[:, j, :], start=True, stop=True)
                            mm.then_inc(P.sem, 1)
                            pe.wait_ge(A.sem, at(c, A, "za"))
                            pe.wait_ge(W.sem, at(c, W, "zb"))
                            for j in range(RT):
                                js = slice(j * 64, j * 64 + 64)
                                pe.matmul(ps[:, 6, js], sbd[:, j, :], stg[:, j, 1, :], start=True, stop=False, skip_group_check=True)
                                for rows, x in ((AA, 0), (BB, 1)):
                                    mm = pe.matmul(ps[rows, 6, js], zb[:, x, j, :], gr[:, x, j, :], start=False, stop=True,
                                                   skip_group_check=True)
                            mm.then_inc(P.sem, 1)
                            heads(7, lambda x, j: bk[:, j, 64 * x:64 * x + 64], lambda x, j: zb[:, x, j, :])

                wkv_out = sem("wkv_out")
                with nc.Block() as block:
                    @block.sync
                    def _(sp):
                        for rows, x in ((AA, 0), (BB, 1)):
                            sp.dma_start(wkv_p[rows], svb[rows, x, :, :]).then_inc(wkv_out, 16)
                        sp.wait_ge(wkv_out, 32)

            with ExitStack() as st:
                sq = sb(st, "y_sq", [128, 2, TOK])
                rn = sb(st, "y_rms", [128, 2, TOK])
                bv = sb(st, "bonus", [128, 2, TOK])
                P = Steps(sem("gn_pe"), ["mean0"] + [f"{x}{j}" for j in range(RT) for x in ("var", "bon", "gate") + (("nmean",) if j + 1 < RT else ())])
                A = Steps(sem("gn_act"), [f"{x}{j}" for j in range(RT) for x in ("sq", "rt")])
                W = Steps(sem("gn_dve"), [f"{x}{j}" for j in range(RT) for x in ("c0_", "c1_", "m0_", "m1_", "bv0_", "bv1_", "inv", "n", "gb", "add", "o0_", "o1_")])
                y_out = sem("yr_out")
                with nc.Block() as block:
                    @block.tensor
                    def _(pe):
                        def mean(j):
                            for i, (a, m) in enumerate(SPANS):
                                mm = pe.matmul(ps[:, i, 0:m], C("pair"), tile_r[:, j, a:a + m], start=True, stop=True)
                            mm.then_inc(P.sem, 1)
                        mean(0)
                        for j in range(RT):
                            pe.wait_ge(A.sem, A.at(f"sq{j}"))
                            if j:
                                pe.wait_ge(W.sem, W.at(f"o1_{j - 1}"))
                            for i, (a, m) in enumerate(SPANS):
                                mm = pe.matmul(ps[:, 2 + i, 0:m], C("pair"), sq[:, j % 2, a:a + m], start=True, stop=True)
                            mm.then_inc(P.sem, 1)
                            for i, (a, m) in enumerate(SPANS):
                                mm = pe.matmul(ps[:, 4 + i, 0:m], C("pair"), au[:, j, a:a + m], start=True, stop=True)
                            mm.then_inc(P.sem, 1)
                            for i, (a, m) in enumerate(SPANS):
                                mm = pe.matmul(ps[:, 6 + i, 0:m], g2s[:, j * 128:j * 128 + 128], rkv[:, 25, a:a + m], start=True, stop=True)
                            mm.then_inc(P.sem, 1)
                            if j + 1 < RT:
                                mean(j + 1)

                    @block.scalar
                    def _(act):
                        for j in range(RT):
                            act.wait_ge(W.sem, W.at(f"c1_{j}"))
                            act.activation(sq[:, j % 2, :], tile_r[:, j, :], ACT.Square).then_inc(A.sem, 1)
                            act.wait_ge(W.sem, W.at(f"m1_{j}"))
                            act.activation(rn[:, j % 2, :], rn[:, j % 2, :], ACT.Sqrt).then_inc(A.sem, 1)

                    @block.vector
                    def _(dve):
                        def did(ins, name):
                            ins.then_inc(W.sem, 1)
                            dve.wait_ge(W.sem, W.at(name))
                        for j in range(RT):
                            b = j % 2
                            dve.wait_ge(P.sem, P.at("mean0") if j == 0 else P.at(f"nmean{j - 1}"))
                            for i, (a, m) in enumerate(SPANS):
                                did(dve.scalar_tensor_tensor(tile_r[:, j, a:a + m], ps[:, i, 0:m], -1.0 / 64, tile_r[:, j, a:a + m],
                                                             ALU.mult, ALU.add), f"c{i}_{j}")
                            dve.wait_ge(P.sem, P.at(f"var{j}"))
                            for i, (a, m) in enumerate(SPANS):
                                did(dve.tensor_scalar(rn[:, b, a:a + m], ps[:, 2 + i, 0:m], 1.0 / 64, 64e-5, ALU.mult, ALU.add), f"m{i}_{j}")
                            dve.wait_ge(P.sem, P.at(f"bon{j}"))
                            for i, (a, m) in enumerate(SPANS):
                                did(dve.tensor_tensor(bv[:, b, a:a + m], ps[:, 4 + i, 0:m], tile_v[:, j, a:a + m], ALU.mult), f"bv{i}_{j}")
                            dve.wait_ge(A.sem, A.at(f"rt{j}"))
                            did(dve.reciprocal(rn[:, b, :], rn[:, b, :]), f"inv{j}")
                            did(dve.tensor_tensor(tile_r[:, j, :], tile_r[:, j, :], rn[:, b, :], ALU.mult), f"n{j}")
                            did(dve.tensor_scalar(tile_r[:, j, :], tile_r[:, j, :], V("lnx_g", j), V("lnx_b", j), ALU.mult, ALU.add), f"gb{j}")
                            did(dve.tensor_tensor(tile_r[:, j, :], tile_r[:, j, :], bv[:, b, :], ALU.add), f"add{j}")
                            dve.wait_ge(P.sem, P.at(f"gate{j}"))
                            for i, (a, m) in enumerate(SPANS):
                                did(dve.tensor_tensor(tile_r[:, j, a:a + m], ps[:, 6 + i, 0:m], tile_r[:, j, a:a + m], ALU.mult), f"o{i}_{j}")

                    @block.sync
                    def _(sp):
                        for j in range(RT):
                            sp.wait_ge(W.sem, W.at(f"o1_{j}"))
                            sp.dma_start(ymix[j, :, :], tile_r[:, j, :]).then_inc(y_out, 16)
                        sp.wait_ge(y_out, 16 * RT)
        if upto <= 4:
            return

        x = sb(stack, "x", [128, KT, TOK])
        with ExitStack() as st:
            mkb = sb(st, "mk", [128, KT, MEM])
            mvb = sb(st, "mv", [128, 2, D])
            memx = mvb[:, :, :].rearrange("p a (b c) -> p (a b) c", c=MEM)
            mh = sb(st, "mem_hi", [128, KT, MEM], f32r)
            ml = sb(st, "mem_lo", [128, KT, MEM], f32r)
            whi = sb(st, "whi_b", [128, 2, BLK], f32r)
            wlo = sb(st, "wlo_b", [128, 2, BLK], f32r)
            rstd = sb(st, "rstd_mem", [128, MEM])
            sq = sb(st, "sq_b", [128, 2, MEM])
            rcol = sb(st, "rstd_col", [128, 2])
            mem_in, mem_out, col_done = sem("mem_in"), sem("mem_out"), sem("col_done")
            with nc.Block() as block:
                @block.sync
                def _(sp):
                    sp.dma_start(memx, memt.rearrange("k p n -> p k n")).then_inc(mem_in, 16)
                    sp.wait_ge(mem_in, 16)

            def evac_ck(dve, i, u, t):
                dve.tensor_tensor(tile_of(mkb, i), ps[:, 2 * u, 0:MEM], rstd[:, :], ALU.mult).then_inc(out_done, 1)

            project("ck", CK0, KT, mh, ml, whi, wlo, [(0, MEM)], evac_ck, memx, "g_mem", (rstd, sq))

            j0 = jobs[0]
            jobs[0] += 4
            with nc.Block() as block:
                @block.sync
                def _(sp):
                    sp.dma_start(mk_o.rearrange("k p n -> p k n"), mkb[:, :, :]).then_inc(mem_out, 16)
                    with sp.Fori(0, 8) as t:
                        for u in range(2):
                            load_block(sp, t * 2 + (CV0 + u), u)

                @block.scalar
                def _(act):
                    act.wait_ge(col_done, 1)
                    act.activation(rcol[:, :], ps[:, 6, 0:2], ACT.Copy).then_inc(col_done, 1)
                    with act.Fori(0, 8) as t:
                        for u in range(2):
                            weight_hi(act, whi, t * 2 + (CV0 + u), u, t + CV0 // 2)

                @block.vector
                def _(dve):
                    dve.wait_ge(col_done, 2)
                    with dve.Fori(0, 2) as t:
                        for n in range(2):
                            for k in range(4):
                                weight_lo(dve, whi, wlo, t * 8 + (CV0 + 4 * n + k), k % 2)
                            dve.wait_ge(pe_done, t * 8 + (CV0 + 4 * n + 3 + 3))
                            for m in range(2):
                                ins = dve.tensor_scalar(mvb[:, m, bass.ds((t * 2 + n) * 512, 512)], ps[:, 2 * n + m, :],
                                                        rcol[:, m:m + 1], None, ALU.mult)
                            ins.then_inc(out_done, 1)

                @block.tensor
                def _(pe):
                    for m in range(2):
                        mm = pe.matmul(ps[:, 6, m:m + 1], rstd[0:1, m * 128:m * 128 + 128], C("ones")[0:1, 0:1], start=True, stop=True)
                    mm.then_inc(col_done, 1)
                    with pe.Fori(0, 2) as t:
                        for n in range(2):
                            pe.wait_ge(out_done, t * 2 + (j0 + n + 1))
                            for k4 in range(4):
                                pe.wait_ge(wlo_done, t * 8 + (CV0 + 4 * n + k4 + 1))
                                for k in range(4):
                                    for at, wt in ((mh, whi), (mh, wlo), (ml, whi)):
                                        for m in range(2):
                                            mm = pe.matmul(ps[:, 2 * n + m, :], at[:, 4 * k4 + k, m * 128:m * 128 + 128],
                                                           wt[:, k4 % 2, k * 512:k * 512 + 512],
                                                           start=(k4 == 0 and k == 0 and at is mh and wt is whi),
                                                           stop=(k4 == 3 and k == 3 and at is ml))
                                mm.then_inc(pe_done, 1)

            with nc.Block() as block:
                @block.sync
                def _(sp):
                    sp.dma_start(mv_o.rearrange("m p n -> p m n"), mvb[:, :, :]).then_inc(mem_out, 16)
                    sp.wait_ge(mem_out, 32)
        if upto <= 5:
            return

        def add_to_x(dve, i, u, t):
            for s, (a, m) in enumerate(SPANS):
                if isinstance(i, int):
                    xi = x[:, i, a:a + m]
                else:
                    xi = x[:, bass.ds(i, 1), a:a + m].rearrange("p o n -> p (o n)")
                ins = dve.tensor_tensor(xi, ps[:, 2 * u + s, 0:m], xi, ALU.add)
            ins.then_inc(out_done, 1)

        late = ExitStack()
        with ExitStack() as st:
            ah = sb(st, "y_hi", [128, KT, TOK], f32r)
            al = sb(st, "y_lo", [128, KT, TOK], f32r)
            whi = sb(st, "whi_c", [128, 2, BLK], f32r)
            wlo = sb(st, "wlo_c", [128, 2, BLK], f32r)
            y = sb(st, "y_mix", [128, KT, TOK])
            y_in = sem("y_in")
            with nc.Block() as block:
                @block.sync
                def _(sp):
                    sp.dma_start(y[:, :, :], ymix.rearrange("k p n -> p k n")).then_inc(y_in, 16)
                    sp.dma_start(x[:, :, :], xt.rearrange("k p n -> p k n")).then_inc(y_in, 16)
                    sp.wait_ge(y_in, 32)
            project("wo", WO0, KT, ah, al, whi, wlo, SPANS, add_to_x, y)

        qc = sb(late, "qc", [128, KT, TOK])
        with ExitStack() as st:
            ah = sb(st, "hx_hi", [128, KT, TOK], f32r)
            al = sb(st, "hx_lo", [128, KT, TOK], f32r)
            whi = sb(st, "whi_d", [128, 2, BLK], f32r)
            wlo = sb(st, "wlo_d", [128, 2, BLK], f32r)
            rstd = sb(st, "rstd_x", [128, TOK])
            sq = sb(st, "sq_d", [128, 2, TOK])

            def evac_q(dve, i, u, t):
                for s, (a, m) in enumerate(SPANS):
                    qi = qc[:, i, a:a + m] if isinstance(i, int) else qc[:, bass.ds(i, 1), a:a + m].rearrange("p o n -> p (o n)")
                    ins = dve.tensor_tensor(qi, ps[:, 2 * u + s, 0:m], rstd[:, a:a + m], ALU.mult)
                ins.then_inc(out_done, 1)
            project("cq", CQ0, KT, ah, al, whi, wlo, SPANS, evac_q, x, "g_cross", (rstd, sq))

        XS = XD ** -0.5
        with ExitStack() as st:
            mkb = sb(st, "mk2", [128, KT, MEM])
            mvb = sb(st, "mv2", [128, 2, D])
            ex = sb(st, "x_exp", [128, 2, MEM])
            xT = sb(st, "x_exp_T", [128, 2, 2, SEQ])
            mxs = sb(st, "x_max", [128, 2])
            nmx = sb(st, "x_neg", [128, 2])
            rs = sb(st, "x_sum", [128, 2])
            ri = sb(st, "x_inv", [128, 2])
            units = [(h, i) for h in range(XH) for i in range(4)]
            mkv_in = sem("mkv_in")
            P = Steps(sem("xp_pe"), ["s00"] + [y for n, (h, i) in enumerate(units) for y in
                      ([f"s{units[n + 1][0]}{units[n + 1][1]}"] if n < 15 else []) + [f"t{h}{i}"]
                      + ([f"o{h}{e}" for e in range(4)] if i == 3 else [])])
            A = Steps(sem("xp_act"), [y for h, i in units for y in [f"e{h}{i}", f"t{h}{i}"] + ([f"o{h}{e}" for e in range(4)] if i == 3 else [])])
            W = Steps(sem("xp_dve"), [f"{y}{h}{i}" for h, i in units for y in ("max", "neg", "inv", "w")])
            with nc.Block() as block:
                @block.sync
                def _(sp):
                    sp.dma_start(mkb[:, :, :], mk_o.rearrange("k p n -> p k n")).then_inc(mkv_in, 16)
                    sp.dma_start(mvb[:, :, :], mv_o.rearrange("m p n -> p m n")).then_inc(mkv_in, 16)

                @block.tensor
                def _(pe):
                    def scores(n):
                        h, i = units[n]
                        if n >= 2:
                            pe.wait_ge(A.sem, A.at("e%d%d" % units[n - 2]))
                        for e in range(4):
                            mm = pe.matmul(ps[:, n % 2, 0:MEM], qc[:, 4 * h + e, i * 128:i * 128 + 128], mkb[:, 4 * h + e, :],
                                           start=(e == 0), stop=(e == 3))
                        mm.then_inc(P.sem, 1)
                    pe.wait_ge(mkv_in, 32)
                    scores(0)
                    for n, (h, i) in enumerate(units):
                        if n < 15:
                            scores(n + 1)
                        pe.wait_ge(W.sem, W.at(f"w{h}{i}"))
                        if n >= 2:
                            pe.wait_ge(A.sem, A.at("t%d%d" % units[n - 2]))
                        for m in range(2):
                            mm = pe.transpose(ps[:, 2 + n % 2, m * 128:m * 128 + 128], ex[:, n % 2, m * 128:m * 128 + 128], C("ident"))
                        mm.then_inc(P.sem, 1)
                        if i == 3:
                            pe.wait_ge(A.sem, A.at(f"t{h}3"))
                            for e in range(4):
                                if h:
                                    pe.wait_ge(A.sem, A.at(f"o{h - 1}{e}"))
                                for m in range(2):
                                    mm = pe.matmul(ps[:, 4 + e, :], mvb[:, m, (4 * h + e) * 128:(4 * h + e) * 128 + 128],
                                                   xT[:, h % 2, m, :], start=(m == 0), stop=(m == 1))
                                mm.then_inc(P.sem, 1)

                @block.scalar
                def _(act):
                    for n, (h, i) in enumerate(units):
                        act.wait_ge(W.sem, W.at(f"neg{h}{i}"))
                        act.activation(ex[:, n % 2, :], ps[:, n % 2, 0:MEM], ACT.Exp, bias=nmx[:, n % 2:n % 2 + 1], scale=XS,
                                       accum_out=rs[:, n % 2:n % 2 + 1]).then_inc(A.sem, 1)
                        act.wait_ge(P.sem, P.at(f"t{h}{i}"))
                        act.activation(xT[:, h % 2, :, i * 128:i * 128 + 128], ps[:, 2 + n % 2, 0:256].rearrange("p (a b) -> p a b", a=2),
                                       ACT.Copy).then_inc(A.sem, 1)
                        if i == 3:
                            for e in range(4):
                                act.wait_ge(P.sem, P.at(f"o{h}{e}"))
                                act.activation(qc[:, 4 * h + e, 0:SEQ], ps[:, 4 + e, :], ACT.Copy).then_inc(A.sem, 1)

                @block.vector
                def _(dve):
                    def did(ins, name):
                        ins.then_inc(W.sem, 1)
                        dve.wait_ge(W.sem, W.at(name))
                    for n, (h, i) in enumerate(units):
                        b = slice(n % 2, n % 2 + 1)
                        dve.wait_ge(P.sem, P.at(f"s{h}{i}"))
                        did(dve.reduce_max(mxs[:, b], ps[:, n % 2, 0:MEM], AX.X), f"max{h}{i}")
                        if n >= 2:
                            dve.wait_ge(P.sem, P.at("t%d%d" % units[n - 2]))
                        did(dve.tensor_scalar(nmx[:, b], mxs[:, b], -XS, None, ALU.mult), f"neg{h}{i}")
                        dve.wait_ge(A.sem, A.at(f"e{h}{i}"))
                        did(dve.reciprocal(ri[:, b], rs[:, b]), f"inv{h}{i}")
                        did(dve.tensor_scalar(ex[:, n % 2, :], ex[:, n % 2, :], ri[:, b], None, ALU.mult), f"w{h}{i}")

        with ExitStack() as st:
            ring = sb(st, "mem_ring", [128, 2, KT * MEM])
            sc = sb(st, "x_scores", [128, NS, 2, XH])
            m1 = sb(st, "x_m1", [128, NS, XH])
            mall = sb(st, "x_mall", [32, 1])
            mdiag = sb(st, "x_mdiag", [32, 32])
            mb = sb(st, "x_mb", [128, NS, XH])
            part = sb(st, "x_part", [128, NS, XH])
            mem_c_in = [sem("mem_c_in0"), sem("mem_c_in1")]
            mem_c_used = sem("mem_c_used")
            cols_out = sem("cols_out")
            with nc.Block() as block:
                @block.tensor
                def _(pe):
                    pe.sem_inc(mem_c_used, 2)

                @block.vector
                def _(dve):
                    dve.sem_inc(cols_out, 2)

            def memory_pass(cache, b0, product, leave):
                with nc.Block() as block:
                    @block.sync
                    def _(sp):
                        with sp.Fori(0, NS // 2) as t:
                            for u in range(2):
                                sp.wait_ge(mem_c_used, t * 2 + (b0 + u + 1))
                                sp.dma_start(ring[:, u, :], cache[bass.ds(t * 2 + u, 1), :, :, :].rearrange("o p a b -> p (o a b)"))\
                                  .then_inc(mem_c_in[u], 16)

                    @block.tensor
                    def _(pe):
                        with pe.Fori(0, NS // 2) as t:
                            for u in range(2):
                                pe.wait_ge(cols_out, t * 2 + (b0 + u + 1))
                                pe.wait_ge(mem_c_in[u], t * 16 + (b0 * 8 + 16))
                                product(pe, t * 2 + u, u).then_inc(mem_c_used, 1)

                    @block.vector
                    def _(dve):
                        with dve.Fori(0, NS // 2) as t:
                            for u in range(2):
                                dve.wait_ge(mem_c_used, t * 2 + (b0 + u + 3))
                                leave(dve, t * 2 + u, u)

            def score_product(pe, b, u):
                keys = ring[:, u, :].rearrange("p (t m) -> p t m", m=MEM)
                for m in range(2):
                    for h in range(XH):
                        for e in range(4):
                            mm = pe.matmul(ps[:, u, m * XH + h:m * XH + h + 1], keys[:, 4 * h + e, m * 128:m * 128 + 128],
                                           qc[:, 4 * h + e, bass.ds(b + SEQ, 1)], start=(e == 0), stop=(e == 3))
                return mm

            def score_leave(dve, b, u):
                dve.tensor_copy(sc[:, bass.ds(b, 1), :, :].rearrange("p o a b -> p (o a b)"), ps[:, u, 0:2 * XH]).then_inc(cols_out, 1)

            memory_pass(mkc, 0, score_product, score_leave)
            S = Steps(sem("xs_soft"), ["m1", "m1_T", "mall", "mdiag", "mb_mm", "mb", "sub", "exp", "part", "sum_mm", "inv", "w"])
            with nc.Block() as block:
                @block.tensor
                def _(pe):
                    pe.wait_ge(S.sem, S.at("m1"))
                    pe.transpose(ps[0:32, 4, 0:128], m1[:, :, :].rearrange("p a b -> p (a b)"), C("ident")).then_inc(S.sem, 1)
                    pe.wait_ge(S.sem, S.at("mdiag"))
                    pe.matmul(ps[:, 5, 0:32], C("ones")[0:32, :], mdiag[:, :], start=True, stop=True).then_inc(S.sem, 1)
                    pe.wait_ge(S.sem, S.at("part"))
                    pe.matmul(ps[:, 6, 0:32], C("ones"), part[:, :, :].rearrange("p a b -> p (a b)"), start=True, stop=True).then_inc(S.sem, 1)

                @block.scalar
                def _(act):
                    act.wait_ge(S.sem, S.at("sub"))
                    e = sc[:, :, :, :].rearrange("p a b c -> p (a b c)")
                    act.activation(e, e, ACT.Exp, scale=XS).then_inc(S.sem, 1)

                @block.vector
                def _(dve):
                    def did(ins, name):
                        ins.then_inc(S.sem, 1)
                        dve.wait_ge(S.sem, S.at(name))
                    spread = lambda t: t[:, :, :].unsqueeze(2).to_broadcast([128, NS, 2, XH])
                    did(dve.tensor_tensor(m1[:, :, :], sc[:, :, 0, :], sc[:, :, 1, :], ALU.max), "m1")
                    dve.wait_ge(S.sem, S.at("m1_T"))
                    did(dve.reduce_max(mall[:, :], ps[0:32, 4, 0:128], AX.X), "mall")
                    did(dve.tensor_scalar(mdiag[:, :], C("ident")[0:32, 0:32], mall[:, :], None, ALU.mult), "mdiag")
                    dve.wait_ge(S.sem, S.at("mb_mm"))
                    did(dve.tensor_copy(mb[:, :, :].rearrange("p a b -> p (a b)"), ps[:, 5, 0:32]), "mb")
                    did(dve.tensor_tensor(sc[:, :, :, :], sc[:, :, :, :], spread(mb), ALU.subtract), "sub")
                    dve.wait_ge(S.sem, S.at("exp"))
                    did(dve.tensor_tensor(part[:, :, :], sc[:, :, 0, :], sc[:, :, 1, :], ALU.add), "part")
                    dve.wait_ge(S.sem, S.at("sum_mm"))
                    did(dve.reciprocal(mb[:, :, :].rearrange("p a b -> p (a b)"), ps[:, 6, 0:32]), "inv")
                    did(dve.tensor_tensor(sc[:, :, :, :], sc[:, :, :, :], spread(mb), ALU.mult), "w")

            def value_product(pe, b, u):
                values = ring[:, u, :].rearrange("p (m n) -> p m n", m=2)
                for h in range(KT):
                    for m in range(2):
                        mm = pe.matmul(ps[:, u, h:h + 1], values[:, m, h * 128:h * 128 + 128],
                                       sc[:, bass.ds(b, 1), m, h // 4:h // 4 + 1].rearrange("p o c -> p (o c)"),
                                       start=(m == 0), stop=(m == 1))
                return mm

            def value_leave(dve, b, u):
                dve.tensor_copy(qc[:, :, bass.ds(b + SEQ, 1)].rearrange("p h o -> p (h o)"), ps[:, u, 0:KT]).then_inc(cols_out, 1)

            memory_pass(mvc, NS, value_product, value_leave)

        with ExitStack() as st:
            ah = sb(st, "o_hi", [128, KT, TOK], f32r)
            al = sb(st, "o_lo", [128, KT, TOK], f32r)
            whi = sb(st, "whi_e", [128, 2, BLK], f32r)
            wlo = sb(st, "wlo_e", [128, 2, BLK], f32r)
            project("co", CO0, KT, ah, al, whi, wlo, SPANS, add_to_x, qc)
        late.close()

        with ExitStack() as st:
            ah = sb(st, "hf_hi", [128, KT, TOK], f32r)
            al = sb(st, "hf_lo", [128, KT, TOK], f32r)
            whi = sb(st, "whi_f", [128, 2, BLK], f32r)
            wlo = sb(st, "wlo_f", [128, 2, BLK], f32r)
            hh = sb(st, "hid_hi", [128, 4, TOK], f32r)
            hl = sb(st, "hid_lo", [128, 4, TOK], f32r)
            z = sb(st, "gate", [128, 2, TOK])
            sg = sb(st, "sigm", [128, 2, TOK])
            up = sb(st, "up", [128, 2, TOK])
            rstd = sb(st, "rstd_f", [128, TOK])
            sq = sb(st, "sq_f", [128, 2, TOK])
            j0 = jobs[0]
            assert j0 % 2 == 0 and FF0 % 2 == 0
            A = Steps(sem("ff_act"), [f"{y}{n}" for n in range(4) for y in ("sig", "hh")])
            W = Steps(sem("ff_dve"), [f"{y}{n}" for n in range(4) for y in ("z0_", "z1_", "u0_", "u1_", "zs", "hd", "hl")])
            down_done = sem("down_done")
            hi_done, lo_done, sq_done, ssq_done, ms_done, rms_done = [
                sem(f"ff_{y}") for y in ("hi", "lo", "sq", "ssq", "ms", "rms")]

            def at(c, steps, name):
                return c * len(steps.names) + steps.at(name)

            def turns_of(eng, body):
                body(0, True, False)
                with eng.Fori(1, FFC - 1) as c:
                    body(c, False, False)
                body(FFC - 1, False, True)

            with nc.Block() as block:
                @block.sync
                def _(sp):
                    with sp.Fori(0, 6 * FFC - 1) as t:
                        for u in range(2):
                            load_block(sp, t * 2 + (FF0 + u), u)

                @block.scalar
                def _(act):
                    def hi_of(c, i):
                        weight_hi(act, whi, c * 12 + (FF0 + i), i % 2, c * 6 + (FF0 // 2 + i // 2))

                    def body(c, first, last):
                        if first:
                            hi_of(0, 0)
                            for k in range(KT):
                                act.activation(ah[:, k, :], x[:, k, :], ACT.Copy, scale=V("g_ffn", k)).then_inc(hi_done, 1)
                            hi_of(0, 1)
                            for k in range(KT):
                                if k >= 2:
                                    act.wait_ge(ssq_done, k - 1)
                                act.activation(sq[:, k % 2, :], x[:, k, :], ACT.Square).then_inc(sq_done, 1)
                            act.wait_ge(ms_done, 2)
                            act.activation(rstd[:, :], rstd[:, :], ACT.Sqrt).then_inc(rms_done, 1)
                        for i in range(12):
                            if not (last and i >= 10):
                                hi_of(c, i + 2)
                            if i < 8 and i % 2 == 0:
                                n = i // 2
                                act.wait_ge(W.sem, at(c, W, f"z1_{n}"))
                                act.activation(sg[:, n % 2, :], z[:, n % 2, :], ACT.Sigmoid).then_inc(A.sem, 1)
                            elif i < 8:
                                n = i // 2
                                act.wait_ge(W.sem, at(c, W, f"hd{n}"))
                                act.activation(hh[:, n, :], up[:, n % 2, :], ACT.Copy).then_inc(A.sem, 1)
                    turns_of(act, body)

                @block.vector
                def _(dve):
                    def body(c, first, last):
                        def did(ins, name):
                            ins.then_inc(W.sem, 1)
                            dve.wait_ge(W.sem, at(c, W, name))

                        def lo_of(i):
                            if not (last and i >= 12):
                                weight_lo(dve, whi, wlo, c * 12 + (FF0 + i), i % 2)
                        if first:
                            lo_of(0)
                            for k in range(KT):
                                dve.wait_ge(hi_done, k + 1)
                                dve.scalar_tensor_tensor(al[:, k, :], x[:, k, :], V("g_ffn", k), ah[:, k, :].bitcast(f32),
                                                         ALU.mult, ALU.subtract).then_inc(lo_done, 1)
                            lo_of(1)
                            dve.wait_ge(ssq_done, KT)
                            for i, (a, m) in enumerate(SPANS):
                                dve.tensor_scalar(rstd[:, a:a + m], ps[:, 4 + i, 0:m], 1.0 / D, 1e-6, ALU.mult, ALU.add).then_inc(ms_done, 1)
                            dve.wait_ge(rms_done, 1)
                            dve.reciprocal(rstd[:, :], rstd[:, :]).then_inc(rms_done, 1)
                            dve.wait_ge(rms_done, 2)
                        for i in range(8):
                            n, b = i // 2, (i // 2) % 2
                            dve.wait_ge(pe_done, c * 12 + (FF0 + i + 3))
                            dst = (z, up)[i % 2]
                            for s, (a, m) in enumerate(SPANS):
                                ins = dve.tensor_tensor(dst[:, b, a:a + m], ps[:, 2 * (i % 2) + s, 0:m], rstd[:, a:a + m], ALU.mult)
                                did(ins, f"{'zu'[i % 2]}{s}_{n}")
                            dve.sem_inc(out_done, 1)
                            lo_of(i + 2)
                            if i % 2:
                                dve.wait_ge(A.sem, at(c, A, f"sig{n}"))
                                did(dve.tensor_tensor(z[:, b, :], z[:, b, :], sg[:, b, :], ALU.mult), f"zs{n}")
                                did(dve.tensor_tensor(up[:, b, :], z[:, b, :], up[:, b, :], ALU.mult), f"hd{n}")
                                dve.wait_ge(A.sem, at(c, A, f"hh{n}"))
                                did(dve.tensor_tensor(hl[:, n, :], up[:, b, :], hh[:, n, :].bitcast(f32), ALU.subtract), f"hl{n}")
                        for q in range(4):
                            for m_ in range(4):
                                if m_ < 3:
                                    dve.wait_ge(down_done, c * 12 + (3 * q + m_ + 1))
                                else:
                                    dve.wait_ge(pe_done, c * 12 + (FF0 + 8 + q + 3))
                                for s, (a, m) in enumerate(SPANS):
                                    xi = x[:, 4 * q + m_, a:a + m]
                                    ins = dve.tensor_tensor(xi, ps[:, 2 * (m_ % 2) + s, 0:m], xi, ALU.add)
                                ins.then_inc(out_done, 1)
                            lo_of(10 + q)
                    turns_of(dve, body)

                @block.tensor
                def _(pe):
                    def product(k, kcol, u, wslot, th, tl, first, last):
                        for wt, t in ((whi, th), (whi, tl), (wlo, th)):
                            for s, (a, m) in enumerate(SPANS):
                                mm = pe.matmul(ps[:, 2 * u + s, 0:m], wt[:, wslot, kcol:kcol + 128], t[:, k, a:a + m],
                                               start=(first and wt is whi and t is th), stop=(last and wt is wlo))
                        return mm

                    def body(c, first, last):
                        for i in range(8):
                            pe.wait_ge(wlo_done, c * 12 + (FF0 + i + 1))
                            pe.wait_ge(out_done, c * 24 + (j0 + i + 1))
                            for k in range(KT):
                                if first and i == 0:
                                    pe.wait_ge(lo_done, k + 1)
                                mm = product(k, k * 128, i % 2, i % 2, ah, al, k == 0, k == KT - 1)
                            mm.then_inc(pe_done, 1)
                            if first and i == 0:
                                for k in range(KT):
                                    pe.wait_ge(sq_done, k + 1)
                                    for s, (a, m) in enumerate(SPANS):
                                        mm = pe.matmul(ps[:, 4 + s, 0:m], C("ones"), sq[:, k % 2, a:a + m], start=(k == 0), stop=(k == KT - 1))
                                    mm.then_inc(ssq_done, 1)
                        for q in range(4):
                            pe.wait_ge(wlo_done, c * 12 + (FF0 + 8 + q + 1))
                            for m_ in range(4):
                                pe.wait_ge(out_done, c * 24 + (j0 + 8 + 4 * q + m_ + 1))
                                for k in range(4):
                                    if q == 0 and m_ == 0:
                                        pe.wait_ge(W.sem, at(c, W, f"hl{k}"))
                                    mm = product(k, (m_ * 4 + k) * 128, m_ % 2, q % 2, hh, hl, k == 0, k == 3)
                                mm.then_inc(down_done if m_ < 3 else pe_done, 1)
                    turns_of(pe, body)

        with ExitStack() as st:
            sq = sb(st, "sq_g", [128, 2, TOK])
            rstd = sb(st, "rstd_g", [128, TOK])
            fin = sem("fin_act")
            fin_pe, fin_dve, fin_out = sem("fin_pe"), sem("fin_dve"), sem("fin_out")
            with nc.Block() as block:
                @block.scalar
                def _(act):
                    for k in range(KT):
                        if k >= 2:
                            act.wait_ge(fin_pe, k - 1)
                        act.activation(sq[:, k % 2, :], x[:, k, :], ACT.Square).then_inc(fin, 1)
                    act.wait_ge(fin_dve, 2)
                    act.activation(rstd[:, :], rstd[:, :], ACT.Sqrt).then_inc(fin, 1)

                @block.tensor
                def _(pe):
                    for k in range(KT):
                        pe.wait_ge(fin, k + 1)
                        for s, (a, m) in enumerate(SPANS):
                            mm = pe.matmul(ps[:, 4 + s, 0:m], C("ones"), sq[:, k % 2, a:a + m], start=(k == 0), stop=(k == KT - 1))
                        mm.then_inc(fin_pe, 1)

                @block.vector
                def _(dve):
                    dve.wait_ge(fin_pe, KT)
                    for s, (a, m) in enumerate(SPANS):
                        dve.tensor_scalar(rstd[:, a:a + m], ps[:, 4 + s, 0:m], 1.0 / D, 1e-6, ALU.mult, ALU.add).then_inc(fin_dve, 1)
                    dve.wait_ge(fin, KT + 1)
                    dve.reciprocal(rstd[:, :], rstd[:, :]).then_inc(fin_dve, 1)
                    dve.wait_ge(fin_dve, 3)
                    for k in range(KT):
                        dve.scalar_tensor_tensor(x[:, k, :], x[:, k, :], V("g_final", k), rstd[:, :], ALU.mult, ALU.mult).then_inc(fin_dve, 1)

                @block.sync
                def _(sp):
                    for k in range(KT):
                        sp.wait_ge(fin_dve, 4 + k)
                        sp.dma_start(yo[k, :, :], x[:, k, :]).then_inc(fin_out, 16)
                    sp.wait_ge(fin_out, 16 * KT)




def blocks16(wt):
    n = wt.shape[1]
    return wt.reshape(KT, 128, n // 128, 128).transpose(2, 1, 0, 3).reshape(n // 128, 128, BLK)


def prepare(i):
    a = {k: np.asarray(v) for k, v in i.items()}
    w_in = a["w_in"][0]
    cv = a["w_cv"][0].reshape(4, 4, 128, 4, 512).transpose(3, 0, 2, 1, 4).reshape(16, 128, BLK)
    gate, up = blocks16(a["w_gate"][0]), blocks16(a["w_up"][0])
    down = a["w_down"][0].reshape(FFC, 4, 128, 4, 4, 128).transpose(0, 3, 2, 4, 1, 5).reshape(FFC, 4, 128, BLK)
    gu = np.stack([gate, up], 1).reshape(FFC, 8, 128, BLK)
    w = np.concatenate([blocks16(w_in[:, RW_PROJ:]), blocks16(w_in[:, :RW_PROJ]), blocks16(a["w_ck"][0]), cv,
                        blocks16(a["w_o"][0]), blocks16(a["w_cq"][0]), blocks16(a["w_co"][0]),
                        np.concatenate([gu, down], 1).reshape(12 * FFC, 128, BLK)])

    def feat(v):
        return np.asarray(v).reshape(-1, 128).T
    vec = np.concatenate([feat(a["norm_mix_g"][0]), feat(a["norm_mem_g"][0]), feat(a["norm_cross_g"][0]),
                          feat(a["norm_ffn_g"][0]), feat(a["final_norm_g"]), feat(a["tok_shift_mu"][0]),
                          feat(a["rwkv_w0"][0]), feat(a["rwkv_a0"][0]), feat(a["rwkv_k_k"][0]), feat(a["rwkv_k_a"][0]),
                          feat(a["rwkv_r_k"][0]), feat(a["rwkv_lnx_g"][0]), feat(a["rwkv_lnx_b"][0]),
                          feat(a["diff_subln_g"][0]),
                          np.concatenate([a["diff_lq1"][0], a["diff_lq2"][0]])[:, None],
                          np.concatenate([a["diff_lk1"][0], a["diff_lk2"][0]])[:, None],
                          a["state_shift"][0].reshape(NS, PROJ_T, 128).transpose(2, 1, 0).reshape(128, PROJ_T * NS)], 1)
    x = np.concatenate([a["x_prompt"][0], a["x_sample"][:, 0]])
    npool = a["cache_k"].shape[1]
    return {
        "w": w, "vec": vec, "con": shape_constants(),
        "xt": x.T.reshape(KT, 128, TOK),
        "memt": a["mem_prompt"][0].T.reshape(KT, 128, MEM),
        "kc": a["cache_k"][0].transpose(0, 3, 2, 1),
        "vc": a["cache_v"][0],
        "mkc": a["cache_mem_k"][0].reshape(NS, MEM, 16, 128).transpose(0, 3, 2, 1),
        "mvc": a["cache_mem_v"][0].reshape(NS, 2, 128, D).transpose(0, 2, 1, 3),
        "s0": a["state_wkv"][0].reshape(NS, RT, 2, 64, 64).transpose(2, 1, 0, 3, 4).reshape(128, 64, 64),
        "pages": a["page_table"].reshape(1, -1),
        "w2a2": np.concatenate([a["rwkv_w2"][0], a["rwkv_a2"][0]]),
        "g2": a["rwkv_g2"][0],
    }


OUTS = {"qkv": (24, 128, TOK), "yo": (KT, 128, TOK), "wkv_p": (128, RT, 64), "wkv_s": (128, 64, 64),
        "shift": (128, PROJ_T, 1 + NS), "mk_o": (KT, 128, MEM), "mv_o": (2, 128, D)}


def build(nc, shapes, upto=99):
    args = {n: nc.dram_tensor(n, s, i32 if n == "pages" else f32, kind="ExternalInput").ap() for n, s in shapes.items()}
    args |= {n: nc.dram_tensor(n, s, f32, kind="ExternalOutput").ap() for n, s in OUTS.items()}
    args["ymix"] = nc.dram_tensor("ymix", (KT, 128, TOK), f32, kind="ExternalOutput" if upto < 99 else "Internal").ap()
    decoder_kernel(nc, **args, upto=upto)


def kernel(**inputs):
    import concourse.bacc as bacc
    from concourse.bass_utils import run_bass_kernel_spmd
    arrays = {n: np.ascontiguousarray(v) for n, v in prepare(inputs).items()}
    nc = bacc.Bacc("TRN2", target_bir_lowering=False, num_devices=1)
    build(nc, {n: v.shape for n, v in arrays.items()})
    r = run_bass_kernel_spmd(nc, [arrays], core_ids=[0]).results[0]
    r = {n: np.asarray(r[n]) for n in OUTS}
    y = r["yo"].reshape(D, TOK).T
    k = r["qkv"][8:16].reshape(RW, TOK).T
    v = r["qkv"][16:24].reshape(RW, TOK).T
    sh = r["shift"].transpose(2, 1, 0).reshape(1 + NS, RW_PROJ)
    wp = r["wkv_p"].reshape(2, 64, RT, 64).transpose(2, 0, 3, 1).reshape(1, 1, 2 * RT, 64, 64)
    ws = r["wkv_s"].reshape(2, RT, NS, 64, 64).transpose(2, 1, 0, 3, 4).reshape(1, NS, 2 * RT, 64, 64)
    c = np.ascontiguousarray
    return (c(y[None, :SEQ]), c(y[SEQ:, None]), c(k[:SEQ].reshape(1, 1, SEQ, 8, 128)), c(v[:SEQ].reshape(1, 1, SEQ, 8, 128)),
            c(k[SEQ:].reshape(1, NS, 1, 8, 128)), c(v[SEQ:].reshape(1, NS, 1, 8, 128)), c(wp), c(ws),
            c(sh[None, :1]), c(sh[None, 1:]),
            c(r["mk_o"].reshape(D, MEM).T.reshape(1, 1, MEM, XH, XD)), c(r["mv_o"].reshape(1, 1, MEM, XH, XD)))
```

```python
import math
from contextlib import ExitStack

import numpy as np
import concourse.bass as bass
from concourse import mybir

D = 2048
SEQ = 512
NS = 8
TOK = SEQ + NS
HALF = TOK // 2
PAST, PAGE = 2048, 128
PAGES = PAST // PAGE
RW = D // 2
RW_PROJ = 3 * RW + 256
DA_HEADS = 8
MEM = 256
XH, XD = 4, 512
D_FF = ((8 * D + 767) // 768) * 256
KT = D // 128
RT = RW // 128
PROJ_T = RW_PROJ // 128
CH = 64
NCH = SEQ // CH
FFC = D_FF // 512
LAM_INIT = 0.8 - 0.6 * math.exp(-0.3 * 0)
DECAY = math.exp(-0.5)
BLK = 2048

QKV0 = 0
RWK0 = QKV0 + 24
CK0 = RWK0 + PROJ_T
CV0 = CK0 + KT
WO0 = CV0 + KT
CQ0 = WO0 + KT
CO0 = CQ0 + KT
FF0 = CO0 + KT
NBLK = FF0 + 12 * FFC

_cols = [("g_mix", KT), ("g_mem", KT), ("g_cross", KT), ("g_ffn", KT), ("g_final", KT), ("mu", PROJ_T),
         ("w0", RT), ("a0", RT), ("k_k", RT), ("k_a", RT), ("r_k", RT), ("lnx_g", RT), ("lnx_b", RT),
         ("subln", 1), ("lam_q", 1), ("lam_k", 1), ("shift", PROJ_T * NS)]
VEC = {}
_at = 0
for _n, _w in _cols:
    VEC[_n] = _at
    _at += _w
NVEC = _at
_cols = [("ident", 128), ("ones", 128), ("pair", 128), ("halves", 256), ("causal", 128), ("gram", 128),
         ("diag", CH), ("diag_t", CH), ("off_t", CH), ("start", TOK), ("two", 2), ("map0", 64), ("map1", 64)]
CON = {}
_at = 0
for _n, _w in _cols:
    CON[_n] = (_at, _at + _w)
    _at += _w
NCON = _at

f32 = mybir.dt.float32
f32r = mybir.dt.float32r
i32 = mybir.dt.int32
ALU = mybir.AluOpType
ACT = mybir.ActivationFunctionType
AX = mybir.AxisListType
SPANS = [(0, HALF), (HALF, HALF)]


def shape_constants():
    c = np.zeros((128, NCON), np.float32)

    def put(name, a):
        c[:, CON[name][0]:CON[name][1]] = a
    p = np.arange(128)[:, None]
    q = np.arange(128)[None, :]
    put("ident", p == q)
    put("ones", 1.0)
    put("pair", p // 64 == q // 64)
    put("halves", np.concatenate([np.broadcast_to(p < 64, (128, 128)), np.broadcast_to(p >= 64, (128, 128))], 1))
    put("causal", np.where(q <= p, 0.0, -1e30))
    s, t = p % 64, q % 64
    put("gram", np.where(q < 64, s < t, s <= t))
    s, t = p % 64, np.arange(64)[None, :]
    put("diag", (s < t) & (s // 8 == t // 8))
    put("diag_t", (t < s) & (s // 8 == t // 8))
    put("off_t", (t < s) & (s // 8 != t // 8))
    put("start", (np.arange(TOK) % CH != 0) & (np.arange(TOK) < SEQ))
    row, col = np.arange(128)[:, None], np.arange(64)[None, :]
    put("map0", row == 2 * col)
    put("map1", row == 2 * col + 1)
    put("two", np.concatenate([p < 64, p >= 64], 1))
    return c


class Steps:

    def __init__(self, sem, names):
        self.sem, self.names = sem, list(names)
        assert len(set(self.names)) == len(self.names)

    def at(self, name, turn=0):
        return turn * len(self.names) + self.names.index(name) + 1


def decoder_kernel(nc, w, vec, con, xt, memt, kc, vc, mkc, mvc, s0, pages, w2a2, g2,
                   qkv, yo, wkv_p, wkv_s, shift, mk_o, mv_o, ymix,
                   srow, orow, xsrow, xorow, upto=99):
    stack = ExitStack()
    nsem = [0]

    def sem(name):
        nsem[0] += 1
        return stack.enter_context(nc.semaphore(name))

    def sb(st, name, shape, dt=f32):
        return st.enter_context(nc.sbuf_tensor(name, shape, dt))

    with stack:
        vt = sb(stack, "vt", [128, NVEC])
        cn = sb(stack, "cn", [128, NCON])
        lam = sb(stack, "lam", [128, 4])
        raw = sb(stack, "raw", [128, 2, BLK])
        ps = stack.enter_context(nc.psum_tensor("ps", [128, 8, 512], f32))
        bank = [ps[:, i, :] for i in range(8)]

        def C(name):
            return cn[:, CON[name][0]:CON[name][1]]

        def V(name, k=0):
            return vt[:, VEC[name] + k:VEC[name] + k + 1]

        const_in = sem("const_in")
        raw_in = [sem("raw_in0"), sem("raw_in1")]
        whi_done = sem("whi_done")
        wlo_done = sem("wlo_done")
        pe_done = sem("pe_done")
        out_done = sem("out_done")

        with nc.Block() as block:
            @block.sync
            def _(sp):
                sp.dma_start(vt[:, :], vec).then_inc(const_in, 16)
                sp.dma_start(cn[:, :], con).then_inc(const_in, 16)
                for u in range(2):
                    sp.dma_start(raw[:, u, :], w[u, :, :]).then_inc(raw_in[u], 16)
                sp.wait_ge(const_in, 32)

            @block.tensor
            def _(pe):
                pe.sem_inc(pe_done, 2)

            @block.vector
            def _(dve):
                dve.sem_inc(out_done, 2)

        def load_block(sp, g, u, ahead=2):
            sp.wait_ge(wlo_done, g + 1)
            src = w[g + ahead, :, :] if isinstance(g, int) else w[bass.ds(g + ahead, 1), :, :].rearrange("o p n -> p (o n)")
            sp.dma_start(raw[:, u, :], src).then_inc(raw_in[u], 16)

        def weight_hi(act, whi, g, u, turn):
            act.wait_ge(raw_in[u], turn * 16 + 16)
            act.wait_ge(pe_done, g + 1)
            act.activation(whi[:, u, :], raw[:, u, :], ACT.Copy).then_inc(whi_done, 1)

        def weight_lo(dve, whi, wlo, g, u):
            dve.wait_ge(whi_done, g + 1)
            dve.tensor_tensor(wlo[:, u, :], raw[:, u, :], whi[:, u, :].bitcast(f32),
                              ALU.subtract).then_inc(wlo_done, 1)

        jobs = [0]

        def project(name, g0, n, ah, al, whi, wlo, spans, evac, src=None, gain=None, stat=None, extra=None):
            j0 = jobs[0]
            jobs[0] += n
            assert g0 % 2 == 0 and n % 2 == 0 and j0 % 2 == 0
            h0 = g0 // 2
            T = spans[-1][0] + spans[-1][1]
            hi_done, lo_done, sq_done, ssq_done, ms_done, rms_done = (
                [sem(f"{name}_{x}") for x in ("hi", "lo", "sq", "ssq", "ms", "rms")] if src is not None else [None] * 6)
            scale = (lambda k: V(gain, k)) if gain else (lambda k: 1.0)

            def block_product(pe, g, j, u, first=False):
                pe.wait_ge(wlo_done, g + 1)
                pe.wait_ge(out_done, j + 1)
                for k in range(KT):
                    if first:
                        pe.wait_ge(lo_done, k + 1)
                    ks = slice(k * 128, k * 128 + 128)
                    for wt, at in ((whi, ah), (whi, al), (wlo, ah)):
                        for i, (a, m) in enumerate(spans):
                            mm = pe.matmul(bank[2 * u + i][:, 0:m], wt[:, u, ks], at[:, k, a:a + m],
                                           start=(k == 0 and wt is whi and at is ah),
                                           stop=(k == KT - 1 and wt is wlo))
                mm.then_inc(pe_done, 1)

            with nc.Block() as block:
                @block.sync
                def _(sp):
                    if g0 + n == NBLK:
                        with sp.Fori(0, n // 2 - 1) as t:
                            for u in range(2):
                                load_block(sp, t * 2 + (g0 + u), u)
                    else:
                        with sp.Fori(0, n // 2) as t:
                            for u in range(2):
                                load_block(sp, t * 2 + (g0 + u), u)

                @block.scalar
                def _(act):
                    for u in range(2):
                        weight_hi(act, whi, g0 + u, u, h0)
                        if u == 0 and src is not None:
                            for k in range(KT):
                                act.activation(ah[:, k, :], src[:, k, :], ACT.Copy, scale=scale(k)).then_inc(hi_done, 1)
                    if stat:
                        rstd, sq = stat
                        for k in range(KT):
                            if k >= 2:
                                act.wait_ge(ssq_done, k - 1)
                            act.activation(sq[:, k % 2, 0:T], src[:, k, :], ACT.Square).then_inc(sq_done, 1)
                        act.wait_ge(ms_done, len(spans))
                        act.activation(rstd[:, 0:T], rstd[:, 0:T], ACT.Sqrt).then_inc(rms_done, 1)
                    with act.Fori(1, n // 2) as t:
                        for u in range(2):
                            weight_hi(act, whi, t * 2 + (g0 + u), u, t + h0)

                @block.vector
                def _(dve):
                    for u in range(2):
                        weight_lo(dve, whi, wlo, g0 + u, u)
                        if u == 0 and src is not None:
                            for k in range(KT):
                                dve.wait_ge(hi_done, k + 1)
                                dve.scalar_tensor_tensor(al[:, k, :], src[:, k, :], scale(k), ah[:, k, :].bitcast(f32),
                                                         ALU.mult, ALU.subtract).then_inc(lo_done, 1)
                    if stat:
                        rstd, sq = stat
                        dve.wait_ge(ssq_done, KT)
                        for i, (a, m) in enumerate(spans):
                            dve.tensor_scalar(rstd[:, a:a + m], bank[4 + i][:, 0:m], 1.0 / D, 1e-6,
                                              ALU.mult, ALU.add).then_inc(ms_done, 1)
                        dve.wait_ge(rms_done, 1)
                        dve.reciprocal(rstd[:, 0:T], rstd[:, 0:T]).then_inc(rms_done, 1)
                        dve.wait_ge(rms_done, 2)
                    with dve.Fori(0, n // 2 - 1) as t:
                        for u in range(2):
                            dve.wait_ge(pe_done, t * 2 + (g0 + u + 3))
                            evac(dve, t * 2 + u, u, t)
                            weight_lo(dve, whi, wlo, t * 2 + (g0 + u + 2), u)
                    for u in range(2):
                        dve.wait_ge(pe_done, g0 + n + u + 1)
                        evac(dve, n - 2 + u, u, n // 2 - 1)

                @block.tensor
                def _(pe):
                    for u in range(2):
                        block_product(pe, g0 + u, j0 + u, u, first=(u == 0 and src is not None))
                        if u == 0 and stat:
                            for k in range(KT):
                                pe.wait_ge(sq_done, k + 1)
                                for i, (a, m) in enumerate(spans):
                                    mm = pe.matmul(bank[4 + i][:, 0:m], C("ones"), stat[1][:, k % 2, a:a + m],
                                                   start=(k == 0), stop=(k == KT - 1))
                                mm.then_inc(ssq_done, 1)
                    with pe.Fori(1, n // 2) as t:
                        for u in range(2):
                            block_product(pe, t * 2 + (g0 + u), t * 2 + (j0 + u), u)

                if extra:
                    extra(block)

        def tile_of(t, i):
            if isinstance(i, int):
                return t[:, i, :]
            return t[:, bass.ds(i, 1), :].rearrange("p o n -> p (o n)")

        def dram_tile(t, i):
            if isinstance(i, int):
                return t[i, :, :]
            return t[bass.ds(i, 1), :, :].rearrange("o p n -> p (o n)")

        with ExitStack() as mixing:
            rkv = sb(mixing, "rkv", [128, PROJ_T, TOK])
            with ExitStack() as st:
                ah = sb(st, "h_hi", [128, KT, TOK], f32r)
                al = sb(st, "h_lo", [128, KT, TOK], f32r)
                rstd = sb(st, "rstd_mix", [128, TOK])
                with ExitStack() as s2:
                    whi = sb(s2, "whi_a", [128, 2, BLK], f32r)
                    wlo = sb(s2, "wlo_a", [128, 2, BLK], f32r)
                    sq = sb(s2, "sq_a", [128, 2, TOK])
                    ev = sb(s2, "ev_a", [128, 2, TOK])
                    ev_out = sem("ev_out")
                    ev_free = sem("ev_free")
                    x_in = sem("x_in")
                    x = rkv[:, 0:KT, :]

                    with nc.Block() as block:
                        @block.sync
                        def _(sp):
                            for k in range(0, KT, 4):
                                sp.dma_start(x[:, k:k + 4, :], xt[k:k + 4, :, :].rearrange("k p n -> p k n")).then_inc(x_in, 16)
                            sp.wait_ge(x_in, 64)

                        @block.gpsimd
                        def _(pool):
                            pool.sem_inc(ev_free, 2)

                    def evac_qkv(dve, i, u, t):
                        dve.wait_ge(ev_free, i + 1)
                        for s, (a, m) in enumerate(SPANS):
                            ins = dve.tensor_tensor(ev[:, u, a:a + m], bank[2 * u + s][:, 0:m], rstd[:, a:a + m], ALU.mult)
                        ins.then_inc(out_done, 1)

                    def store_qkv(block):
                        @block.gpsimd
                        def _(pool):
                            with pool.Fori(0, 12) as t:
                                for u in range(2):
                                    pool.wait_ge(out_done, t * 2 + (u + 3))
                                    pool.dma_start(dram_tile(qkv, t * 2 + u), ev[:, u, :]).then_inc(ev_out, 16)
                                    pool.wait_ge(ev_out, t * 32 + 16 * (u + 1))
                                    pool.sem_inc(ev_free, 1)

                    project("qkv", QKV0, 24, ah, al, whi, wlo, SPANS, evac_qkv, x, "g_mix", (rstd, sq), store_qkv)

                    p = sb(s2, "p_row", [128, 1 + TOK])
                    dif = sb(s2, "p_dif", [128, TOK])
                    last = sb(s2, "p_last", [128, PROJ_T, 1 + NS])
                    sh = Steps(sem("shift_steps"), ["p0", "p1", "dif", "dif_s", "last", "ps"])
                    sh_out = sem("sh_out")

                    with nc.Block() as block:
                        @block.vector
                        def _(dve):
                            dve.memset(p[:, 0:1], 0.0).then_inc(sh_out, 1)
                            dve.wait_ge(sh_out, 1)

                    def evac_shift(dve, i, u, t):
                        for s, (a, m) in enumerate(SPANS):
                            dve.tensor_tensor(p[:, 1 + a:1 + a + m], bank[2 * u + s][:, 0:m], rstd[:, a:a + m],
                                              ALU.mult).then_inc(sh.sem, 1)
                        dve.wait_ge(sh.sem, i * 6 + 2)
                        dve.tensor_tensor(dif[:, 0:SEQ], p[:, 0:SEQ], p[:, 1:1 + SEQ], ALU.subtract).then_inc(sh.sem, 1)
                        prev = vt[:, bass.ds(VEC["shift"] + i * NS, NS)]
                        dve.tensor_tensor(dif[:, SEQ:TOK], prev, p[:, 1 + SEQ:1 + TOK], ALU.subtract).then_inc(sh.sem, 1)
                        dve.tensor_copy(tile_of(last, i), p[:, SEQ:1 + TOK]).then_inc(sh.sem, 1)
                        dve.wait_ge(sh.sem, i * 6 + 4)
                        dve.scalar_tensor_tensor(tile_of(rkv, i), dif[:, :], vt[:, bass.ds(VEC["mu"] + i, 1)], p[:, 1:1 + TOK],
                                                 ALU.mult, ALU.add).then_inc(sh.sem, 1)
                        dve.wait_ge(sh.sem, i * 6 + 6)
                        dve.sem_inc(out_done, 1)

                    project("rwkv", RWK0, PROJ_T, ah, al, whi, wlo, SPANS, evac_shift)

                    with nc.Block() as block:
                        @block.sync
                        def _(sp):
                            sp.dma_start(shift, last[:, :, :]).then_inc(sh_out, 16)
                            sp.wait_ge(sh_out, 17)

            if upto <= 1:
                return

            attn = ExitStack()
            yd = sb(attn, "yd", [128, DA_HEADS, TOK])
            ready = Steps(sem("lam_steps"), ["prod", "rhs", "sum", "exp", "lam", "neg", "g"])
            lam_e = lam[:, 0:2]
            neg_lam = lam[:, 2:3]
            sub_g = lam[:, 3:4]
            with ExitStack() as st:
                tmp = sb(st, "lam_tmp", [128, 4])
                qh = sb(st, "qkv_head", [128, 2, 3, TOK])
                vtok = sb(st, "v_tok", [128, 2, 4, 128])
                ex = sb(st, "exps", [128, 2, 2, SEQ])
                wt_ = sb(st, "weights", [128, 2, SEQ])
                wT = sb(st, "weights_T", [128, 2, 4, 128])
                mx = sb(st, "row_max", [128, 2, 2])
                nmx = sb(st, "neg_max", [128, 2, 2])
                rs = sb(st, "row_sum", [128, 2, 2])
                ri = sb(st, "row_inv", [128, 2, 2])
                heads_in = [sem("head_in0"), sem("head_in1")]
                act_start = sem("turn_start")
                head_ok = sem("head_ok")
                by_head = qkv.rearrange("(c h) p n -> h p c n", c=3)

                def head_rows(h):
                    return by_head[bass.ds(h, 1), :, :, :].rearrange("o p c n -> p (o c) n")
                turns = [(hh, i) for hh in range(2) for i in range(4)]
                P = Steps(sem("att_pe"), [x for hh in range(2) for x in
                                          [f"vt{hh}", f"s{hh}0"] + [y for i in range(4) for y in
                                           ([f"s{hh}{i + 1}"] if i < 3 else []) + [f"t{hh}{i}", f"o{hh}{i}"]]])
                A = Steps(sem("att_act"), [x for hh in range(2) for x in [f"vt{hh}"] + [y for i in range(4) for y in
                                           (f"e{hh}{i}0", f"e{hh}{i}1", f"t{hh}{i}")] + [f"o{hh}"]])
                V_ = Steps(sem("att_dve"), [f"{y}{hh}{i}" for hh, i in turns for y in
                                            ("mask", "max", "neg", "inv", "invl", "w0_", "w1_")])
                with nc.Block() as block:
                    @block.vector
                    def _(dve):
                        dve.tensor_tensor(tmp[:, 0:1], V("lam_q"), V("lam_k"), ALU.mult).then_inc(ready.sem, 1)
                        dve.wait_ge(ready.sem, ready.at("prod"))
                        dve.tensor_scalar(tmp[:, 1:3], C("two"), tmp[:, 0:1], None, ALU.mult).then_inc(ready.sem, 1)
                        dve.wait_ge(ready.sem, ready.at("exp"))
                        dve.scalar_tensor_tensor(tmp[:, 3:4], lam_e[:, 0:1], LAM_INIT, lam_e[:, 1:2], ALU.add,
                                                 ALU.subtract).then_inc(ready.sem, 1)
                        dve.wait_ge(ready.sem, ready.at("lam"))
                        dve.tensor_scalar(neg_lam, tmp[:, 3:4], -1.0, None, ALU.mult).then_inc(ready.sem, 1)
                        dve.tensor_scalar(sub_g, V("subln"), 1.0 - LAM_INIT, None, ALU.mult).then_inc(ready.sem, 1)
                        dve.wait_ge(ready.sem, ready.at("g"))

                    @block.tensor
                    def _(pe):
                        pe.wait_ge(ready.sem, ready.at("rhs"))
                        pe.matmul(ps[:, 7, 0:2], C("ones"), tmp[:, 1:3], start=True, stop=True).then_inc(ready.sem, 1)

                    @block.scalar
                    def _(act):
                        act.wait_ge(ready.sem, ready.at("sum"))
                        act.activation(lam_e, ps[:, 7, 0:2], ACT.Exp).then_inc(ready.sem, 1)

                    @block.sync
                    def _(sp):
                        for u in range(2):
                            sp.dma_start(qh[:, u, :, :], head_rows(u)).then_inc(heads_in[u], 16)

                with nc.Block() as block:
                    @block.sync
                    def _(sp):
                        with sp.Fori(0, 3) as t:
                            for u in range(2):
                                sp.wait_ge(P.sem, t * len(P.names) + P.at(f"s{u}3"))
                                sp.dma_start(qh[:, u, :, :], head_rows(t * 2 + (2 + u))).then_inc(heads_in[u], 16)

                    @block.tensor
                    def _(pe):
                        def at(t, steps, name):
                            return t * len(steps.names) + steps.at(name)

                        def scores(t, hh, i):
                            n = turns.index((hh, i))
                            if n >= 2:
                                pe.wait_ge(A.sem, at(t, A, "e%d%d1" % turns[n - 2]))
                            else:
                                pe.wait_ge(act_start, t + 1)
                            for c in range(2):
                                q = qh[64 * c:64 * c + 64, hh, 0, i * 128:i * 128 + 128]
                                k = qh[64 * c:64 * c + 64, hh, 1, 0:(i + 1) * 128]
                                mm = pe.matmul(ps[:, 2 * (i % 2) + c, 0:(i + 1) * 128], q, k, start=True, stop=True)
                            mm.then_inc(P.sem, 1)

                        with pe.Fori(0, 4) as t:
                            for hh in range(2):
                                pe.wait_ge(heads_in[hh], t * 16 + 16)
                                pe.wait_ge(head_ok, t * 2 + hh + 1)
                                for i in range(4):
                                    mm = pe.transpose(ps[:, 5, i * 128:i * 128 + 128], qh[:, hh, 2, i * 128:i * 128 + 128], C("ident"))
                                mm.then_inc(P.sem, 1)
                                scores(t, hh, 0)
                                for i in range(4):
                                    if i < 3:
                                        scores(t, hh, i + 1)
                                    pe.wait_ge(V_.sem, at(t, V_, f"w1_{hh}{i}"))
                                    if (hh, i) != (0, 0):
                                        pe.wait_ge(A.sem, at(t, A, "t%d%d" % turns[turns.index((hh, i)) - 1]))
                                    for s in range(i + 1):
                                        mm = pe.transpose(ps[:, 4, s * 128:s * 128 + 128], wt_[:, i % 2, s * 128:s * 128 + 128], C("ident"))
                                    mm.then_inc(P.sem, 1)
                                    pe.wait_ge(A.sem, at(t, A, f"t{hh}{i}"))
                                    if i == 0 and hh == 1:
                                        pe.wait_ge(A.sem, at(t, A, "o0"))
                                    for s in range(i + 1):
                                        mm = pe.matmul(ps[:, 6, i * 128:i * 128 + 128], vtok[:, hh, s, :], wT[:, i % 2, s, :],
                                                       start=(s == 0), stop=(s == i))
                                    mm.then_inc(P.sem, 1)

                    @block.scalar
                    def _(act):
                        def at(t, steps, name):
                            return t * len(steps.names) + steps.at(name)
                        with act.Fori(0, 4) as t:
                            act.sem_inc(act_start, 1)
                            act.sem_inc(head_ok, 1)
                            for hh in range(2):
                                act.wait_ge(P.sem, at(t, P, f"vt{hh}"))
                                act.activation(vtok[:, hh, :, :], ps[:, 5, :], ACT.Copy).then_inc(A.sem, 1)
                                for i in range(4):
                                    n = (i + 1) * 128
                                    act.wait_ge(V_.sem, at(t, V_, f"neg{hh}{i}"))
                                    for c in range(2):
                                        act.activation(ex[:, i % 2, c, 0:n], ps[:, 2 * (i % 2) + c, 0:n], ACT.Exp,
                                                       bias=nmx[:, i % 2, c:c + 1], scale=0.125,
                                                       accum_out=rs[:, i % 2, c:c + 1]).then_inc(A.sem, 1)
                                    act.wait_ge(P.sem, at(t, P, f"t{hh}{i}"))
                                    act.activation(wT[:, i % 2, 0:i + 1, :], ps[:, 4, 0:n], ACT.Copy).then_inc(A.sem, 1)
                                act.wait_ge(P.sem, at(t, P, f"o{hh}3"))
                                act.activation(yd[:, bass.ds(t * 2 + hh, 1), 0:SEQ].rearrange("p o n -> p (o n)"), ps[:, 6, :],
                                               ACT.Copy).then_inc(A.sem, 1)
                                if hh == 0:
                                    act.wait_ge(A.sem, at(t, A, "o0"))
                                    act.sem_inc(head_ok, 1)
                                else:
                                    act.wait_ge(A.sem, at(t, A, "o1"))

                    @block.vector
                    def _(dve):
                        def at(t, steps, name):
                            return t * len(steps.names) + steps.at(name)
                        with dve.Fori(0, 4) as t:
                            for hh, i in turns:
                                n, b = (i + 1) * 128, i % 2
                                dve.wait_ge(P.sem, at(t, P, f"s{hh}{i}"))
                                diag = ps[:, 2 * b:2 * b + 2, i * 128:n]
                                mask = C("causal").unsqueeze(1).to_broadcast([128, 2, 128])
                                dve.tensor_tensor(diag, diag, mask, ALU.add).then_inc(V_.sem, 1)
                                dve.wait_ge(V_.sem, at(t, V_, f"mask{hh}{i}"))
                                dve.reduce_max(mx[:, b, :], ps[:, 2 * b:2 * b + 2, 0:n], AX.X).then_inc(V_.sem, 1)
                                dve.wait_ge(V_.sem, at(t, V_, f"max{hh}{i}"))
                                dve.tensor_scalar(nmx[:, b, :], mx[:, b, :], -0.125, None, ALU.mult).then_inc(V_.sem, 1)
                                dve.wait_ge(A.sem, at(t, A, f"e{hh}{i}1"))
                                dve.reciprocal(ri[:, b, :], rs[:, b, :]).then_inc(V_.sem, 1)
                                dve.wait_ge(V_.sem, at(t, V_, f"inv{hh}{i}"))
                                dve.tensor_tensor(ri[:, b, 1:2], ri[:, b, 1:2], neg_lam, ALU.mult).then_inc(V_.sem, 1)
                                turn = turns.index((hh, i))
                                if turn >= 2:
                                    dve.wait_ge(P.sem, at(t, P, "t%d%d" % turns[turn - 2]))
                                dve.tensor_scalar(wt_[:, b, 0:n], ex[:, b, 0, 0:n], ri[:, b, 0:1], None, ALU.mult).then_inc(V_.sem, 1)
                                dve.wait_ge(V_.sem, at(t, V_, f"w0_{hh}{i}"))
                                dve.scalar_tensor_tensor(wt_[:, b, 0:n], ex[:, b, 1, 0:n], ri[:, b, 1:2], wt_[:, b, 0:n],
                                                         ALU.mult, ALU.add).then_inc(V_.sem, 1)

            if upto <= 2:
                with nc.Block() as block:
                    @block.sync
                    def _(sp):
                        s_ = sem("dbg")
                        sp.dma_start(ymix[8:16, :, 0:SEQ].rearrange("k p n -> p k n"), yd[:, :, 0:SEQ]).then_inc(s_, 16)
                        sp.wait_ge(s_, 16)
                return

            with ExitStack() as st:
                HC = 2 * DA_HEADS
                SLOTS = 8
                tab = sb(st, "page_ids", [1, NS * PAGES], i32)
                qs = sb(st, "qkv_s", [128, 24, NS])
                qbd = sb(st, "q_blocks", [128, NS, DA_HEADS, 2])
                qz = sb(st, "q_columns", [128, NS, DA_HEADS * HC])
                ring = sb(st, "page_ring", [128, SLOTS, RW])
                cur = sb(st, "page_standing", [128, 2, 128])
                rows = sb(st, "rows_out", [HC, 2, PAST])
                sc = sb(st, "scores_s", [128, PAST])
                prod = sb(st, "qk_new", [128, NS, DA_HEADS, 2])
                col = sb(st, "softmax_cols", [128, 8])
                snew, m1, nm, part, enew, inv = [col[:, i:i + 1] for i in range(6)]
                comb = sb(st, "combine", [128, 64])
                comb_n = sb(st, "combine_new", [128, 64])
                ws = sb(st, "w_pages", [128, PAGES, NS * DA_HEADS])
                ov = sb(st, "new_v", [128, NS, DA_HEADS])
                oT = sb(st, "out_rows", [64, 128])
                samp_in = sem("samp_in")
                q_ready = sem("q_blocks_ready")
                cur_in = sem("page_standing_in")
                page_in = [sem(f"page_in{i}") for i in range(SLOTS)]
                page_used = sem("page_used")
                sums_out = sem("sums_out")
                row_out = sem("row_out")
                row_free = sem("row_free")

                with nc.Block() as block:
                    @block.sync
                    def _(sp):
                        sp.dma_start(tab[:, :], pages).then_inc(samp_in, 16)
                        sp.dma_start(qs[:, :, :], qkv[:, :, SEQ:TOK].rearrange("k p n -> p k n")).then_inc(samp_in, 16)
                        sp.wait_ge(samp_in, 32)

                    @block.tensor
                    def _(pe):
                        pe.sem_inc(page_used, SLOTS)

                    @block.gpsimd
                    def _(pool):
                        pool.sem_inc(row_free, 2)

                    @block.vector
                    def _(dve):
                        dve.sem_inc(sums_out, 2)
                        dve.memset(qz[:, :, :], 0.0).then_inc(q_ready, 1)
                        dve.memset(qbd[:, :, :, :], 0.0).then_inc(q_ready, 1)
                        dve.wait_ge(samp_in, 32)
                        dve.wait_ge(q_ready, 2)
                        for c in range(2):
                            half = slice(64 * c, 64 * c + 64)
                            q = qs[half, 0:8, :].rearrange("p h b -> p b h")
                            dve.tensor_copy(qbd[half, :, :, c], q).then_inc(q_ready, 1)
                            dve.tensor_copy(qz[half, :, c::HC + 2], q).then_inc(q_ready, 1)
                        dve.wait_ge(q_ready, 6)
                        k = qs[:, 8:16, :].rearrange("p h b -> p b h").unsqueeze(3).to_broadcast([128, NS, DA_HEADS, 2])
                        dve.tensor_tensor(prod[:, :, :, :], qbd[:, :, :, :], k, ALU.mult).then_inc(q_ready, 1)

                def load_pages(sp, cache, t, bb, g0):
                    for pg in range(PAGES):
                        n = t * 32 + (bb * PAGES + pg)
                        sp.wait_ge(page_used, n + (g0 + 1))
                        page = sp.value_load(tab[0:1, bass.ds(n, 1)], min_val=0, max_val=cache.shape[0] - 1)
                        src = cache[bass.ds(page, 1), :, :, :].rearrange("o p a b -> p (o a b)")
                        sp.dma_start(ring[:, pg % SLOTS, :], src).then_inc(page_in[pg % SLOTS], 16)

                def pass_block(cache, g0, operands, product, summed, store_to, store_from):
                    first = g0 // PAGES
                    with nc.Block() as block:
                        @block.scalar
                        def _(act):
                            with act.Fori(0, NS // 2) as t:
                                for bb in range(2):
                                    act.wait_ge(sums_out, t * 2 + (bb + 1 + first))
                                    act.activation(cur[:, bb, :], operands(t * 2 + bb), ACT.Copy).then_inc(cur_in, 1)

                        @block.sync
                        def _(sp):
                            with sp.Fori(0, NS // 2) as t:
                                for bb in range(2):
                                    load_pages(sp, cache, t, bb, g0)

                        @block.tensor
                        def _(pe):
                            with pe.Fori(0, NS // 2) as t:
                                for bb in range(2):
                                    pe.wait_ge(cur_in, t * 2 + (bb + 1 + first))
                                    pe.wait_ge(sums_out, t * 2 + (bb + 1 + first))
                                    for pg in range(PAGES):
                                        pe.wait_ge(page_in[pg % SLOTS], t * (512 // SLOTS) + 16 * ((g0 + bb * PAGES + pg) // SLOTS + 1))
                                        product(pe, bb, pg).then_inc(page_used, 1)

                        @block.vector
                        def _(dve):
                            with dve.Fori(0, NS // 2) as t:
                                for bb in range(2):
                                    dve.wait_ge(page_used, t * 32 + (SLOTS + g0 + (bb + 1) * PAGES))
                                    dve.wait_ge(row_free, t * 2 + (bb + 1 + first))
                                    src = summed(bb)
                                    dve.tensor_copy(store_from(bb), src).then_inc(sums_out, 1)

                        @block.gpsimd
                        def _(pool):
                            with pool.Fori(0, NS // 2) as t:
                                for bb in range(2):
                                    pool.wait_ge(sums_out, t * 2 + (bb + 3 + first))
                                    pool.dma_start(store_to(t * 2 + bb), store_from(bb)).then_inc(row_out, 16)
                                    pool.wait_ge(row_out, t * 32 + 16 * (bb + 1 + first))
                                    pool.sem_inc(row_free, 1)

                def k_operands(b):
                    return qz[:, bass.ds(b, 1), :].rearrange("p o n -> p (o n)")

                def k_product(pe, bb, pg):
                    at = (pg % 4) * PAGE
                    for h in range(DA_HEADS):
                        mm = pe.matmul(ps[0:HC, 4 * bb + pg // 4, at:at + PAGE], cur[:, bb, h * HC:h * HC + HC],
                                       ring[:, pg % SLOTS, h * 128:h * 128 + 128], start=(h == 0), stop=(h == DA_HEADS - 1))
                    return mm

                pass_block(kc, 0, k_operands, k_product, lambda bb: ps[0:HC, 4 * bb:4 * bb + 4, :].rearrange("p a b -> p (a b)"),
                           lambda b: srow[bass.ds(b, 1), :, :].rearrange("o r n -> (o r) n"), lambda bb: rows[:, bb, :])

                S = Steps(sem("soft_steps"), ["snew_mm", "snew", "m1", "m", "nm", "exp", "enew", "tot", "inv", "cmb0", "cmb", "cmb_n",
                                              "wn_mm", "ws_mm0", "ws_mm1", "ws0", "ws1", "ov"])
                with nc.Block() as block:
                    @block.sync
                    def _(sp):
                        sp.dma_start(sc[:, :], srow.rearrange("b r n -> (b r) n")).then_inc(samp_in, 16)

                    @block.tensor
                    def _(pe):
                        pe.matmul(ps[:, 4, 0:1], prod[:, :, :, :].rearrange("p a b c -> p (a b c)"), C("ones")[:, 0:1],
                                  start=True, stop=True).then_inc(S.sem, 1)
                        pe.wait_ge(S.sem, S.at("cmb_n"))
                        pe.matmul(ps[:, 4, 64:128], C("ones"), comb_n[:, :], start=True, stop=True).then_inc(S.sem, 1)
                        for half in range(2):
                            for g in range(8):
                                pg = half * 8 + g
                                mm = pe.matmul(ps[:, half, g * 64:g * 64 + 64], sc[:, pg * PAGE:pg * PAGE + PAGE], comb[:, :],
                                               start=True, stop=True)
                            mm.then_inc(S.sem, 1)

                    @block.scalar
                    def _(act):
                        act.wait_ge(S.sem, S.at("nm"))
                        act.activation(sc[:, :], sc[:, :], ACT.Exp, bias=nm, scale=0.125, accum_out=part).then_inc(S.sem, 1)
                        act.wait_ge(S.sem, S.at("exp"))
                        act.activation(enew, snew, ACT.Exp, bias=nm, scale=0.125).then_inc(S.sem, 1)

                    @block.vector
                    def _(dve):
                        def did(ins, name):
                            ins.then_inc(S.sem, 1)
                            dve.wait_ge(S.sem, S.at(name))
                        dve.wait_ge(S.sem, S.at("snew_mm"))
                        did(dve.tensor_copy(snew, ps[:, 4, 0:1]), "snew")
                        dve.wait_ge(samp_in, 48)
                        did(dve.reduce_max(m1, sc[:, :], AX.X), "m1")
                        did(dve.tensor_tensor(m1, m1, snew, ALU.max), "m")
                        did(dve.tensor_scalar(nm, m1, -0.125, None, ALU.mult), "nm")
                        dve.wait_ge(S.sem, S.at("enew"))
                        did(dve.tensor_tensor(part, part, enew, ALU.add), "tot")
                        did(dve.reciprocal(inv, part), "inv")
                        did(dve.scalar_tensor_tensor(comb[:, :], C("map1"), neg_lam, C("map0"), ALU.mult, ALU.add), "cmb0")
                        did(dve.tensor_scalar(comb[:, :], comb[:, :], inv, None, ALU.mult), "cmb")
                        did(dve.tensor_scalar(comb_n[:, :], comb[:, :], enew, None, ALU.mult), "cmb_n")
                        dve.wait_ge(S.sem, S.at("ws_mm1"))
                        for half in range(2):
                            did(dve.tensor_copy(ws[:, 8 * half:8 * half + 8, :].rearrange("p a b -> p (a b)"), ps[:, half, :]), f"ws{half}")
                        did(dve.tensor_tensor(ov[:, :, :], qs[:, 16:24, :].rearrange("p h b -> p b h"),
                                              ps[:, 4, 64:128].rearrange("p (b h) -> p b h", h=DA_HEADS), ALU.mult), "ov")

                def v_operands(b):
                    return ws[:, :, bass.ds(b * DA_HEADS, DA_HEADS)]

                def v_product(pe, bb, pg):
                    for n in range(2):
                        mm = pe.matmul(ps[0:DA_HEADS, 2 * bb + n, :], cur[:, bb, pg * DA_HEADS:(pg + 1) * DA_HEADS],
                                       ring[:, pg % SLOTS, n * 512:n * 512 + 512], start=(pg == 0), stop=(pg == PAGES - 1))
                    return mm

                pass_block(vc, 128, v_operands, v_product, lambda bb: ps[0:DA_HEADS, 2 * bb:2 * bb + 2, :].rearrange("p a b -> p (a b)"),
                           lambda b: orow[bass.ds(b, 1), 0:DA_HEADS * RW].rearrange("o (h n) -> (o h) n", n=RW),
                           lambda bb: rows[0:DA_HEADS, bb, 0:RW])
                own = orow.rearrange("b (h m) -> (b h) m", m=RW + 128)[:, 0:128]
                with nc.Block() as block:
                    @block.sync
                    def _(sp):
                        sp.dma_start(oT[:, :], own).then_inc(samp_in, 16)

                    @block.tensor
                    def _(pe):
                        pe.wait_ge(samp_in, 64)
                        pe.transpose(ps[:, 4, 0:64], oT[:, :], C("ident")[0:64, 0:64]).then_inc(q_ready, 1)

                    @block.vector
                    def _(dve):
                        dve.wait_ge(q_ready, 8)
                        dve.tensor_tensor(yd[:, :, SEQ:TOK].rearrange("p h b -> p b h"),
                                          ps[:, 4, 0:64].rearrange("p (b h) -> p b h", h=DA_HEADS), ov[:, :, :], ALU.add).then_inc(q_ready, 1)

            with ExitStack() as st:
                sq = sb(st, "yd_sq", [128, 2, TOK])
                rn = sb(st, "yd_rms", [128, 2, TOK])
                y_out = sem("y_out")
                NQ = Steps(sem("subln_act"), [f"{x}{h}" for h in range(8) for x in ("sq", "rt")])
                NP = Steps(sem("subln_pe"), [f"mm{h}" for h in range(8)])
                NV = Steps(sem("subln_dve"), [f"{x}{h}" for h in range(8) for x in ("ms0_", "ms1_", "inv", "y")])
                with nc.Block() as block:
                    @block.scalar
                    def _(act):
                        def square(h):
                            if h >= 2:
                                act.wait_ge(NP.sem, NP.at(f"mm{h - 2}"))
                            act.activation(sq[:, h % 2, :], yd[:, h, :], ACT.Square).then_inc(NQ.sem, 1)
                        for h in range(8):
                            square(h)
                            act.wait_ge(NV.sem, NV.at(f"ms1_{h}"))
                            act.activation(rn[:, h % 2, :], rn[:, h % 2, :], ACT.Sqrt).then_inc(NQ.sem, 1)

                    @block.tensor
                    def _(pe):
                        for h in range(8):
                            pe.wait_ge(NQ.sem, NQ.at(f"sq{h}"))
                            if h >= 2:
                                pe.wait_ge(NV.sem, NV.at(f"ms1_{h - 2}"))
                            for i, (a, m) in enumerate(SPANS):
                                mm = pe.matmul(ps[:, 2 * (h % 2) + i, 0:m], C("ones"), sq[:, h % 2, a:a + m], start=True, stop=True)
                            mm.then_inc(NP.sem, 1)

                    @block.vector
                    def _(dve):
                        for h in range(8):
                            dve.wait_ge(NP.sem, NP.at(f"mm{h}"))
                            for i, (a, m) in enumerate(SPANS):
                                dve.tensor_scalar(rn[:, h % 2, a:a + m], ps[:, 2 * (h % 2) + i, 0:m], 1.0 / 128, 1e-6,
                                                  ALU.mult, ALU.add).then_inc(NV.sem, 1)
                            dve.wait_ge(NQ.sem, NQ.at(f"rt{h}"))
                            dve.reciprocal(rn[:, h % 2, :], rn[:, h % 2, :]).then_inc(NV.sem, 1)
                            dve.wait_ge(NV.sem, NV.at(f"inv{h}"))
                            dve.scalar_tensor_tensor(yd[:, h, :], yd[:, h, :], sub_g, rn[:, h % 2, :],
                                                     ALU.mult, ALU.mult).then_inc(NV.sem, 1)

                    @block.sync
                    def _(sp):
                        for h in range(8):
                            sp.wait_ge(NV.sem, NV.at(f"y{h}"))
                            sp.dma_start(ymix[8 + h, :, :], yd[:, h, :]).then_inc(y_out, 16)
                        sp.wait_ge(y_out, 128)
            attn.close()
            if upto <= 3:
                return

            tile_r, tile_k, tile_v = rkv[:, 0:RT, :], rkv[:, RT:2 * RT, :], rkv[:, 2 * RT:3 * RT, :]
            au = sb(mixing, "iclr", [128, RT, TOK])
            kk = sb(mixing, "kk", [128, RT, TOK])
            cum = sb(mixing, "cum", [128, RT, TOK])
            g2s = sb(mixing, "g2s", [128, RW])
            flat = lambda a: a.rearrange("p a b -> p (a b)")
            lora_in = sem("lora_in")
            with ExitStack() as st:
                wa = sb(st, "w2a2s", [128, RW])
                sq = sb(st, "kk_sq", [128, 2, TOK])
                nr = sb(st, "kk_norm", [128, 2, TOK])
                tk = sb(st, "k_gain", [128, TOK])
                A = Steps(sem("prep_act"), ["tanh", "sig"] + [f"{x}{j}" for j in range(RT) for x in ("w0_", "w1_", "a0_", "a1_")]
                          + [f"rt{j}" for j in range(RT)])
                P = Steps(sem("prep_pe"), [f"{x}{j}" for j in range(RT) for x in ("w", "a")] + [f"n{j}" for j in range(RT)])
                W = Steps(sem("prep_dve"), ["kk0", "sq0"] + [f"{x}{j}" for j in range(RT) for x in
                          ("m0_", "m1_", "inv", "kn", "t", "kmod", "b", "cum")
                          + (("nkk", "nsq") if j + 1 < RT else ())])
                with nc.Block() as block:
                    @block.sync
                    def _(sp):
                        sp.dma_start(wa[:, :], w2a2).then_inc(lora_in, 16)
                        sp.dma_start(g2s[:, :], g2).then_inc(lora_in, 16)

                    @block.scalar
                    def _(act):
                        act.activation(rkv[0:64, 24, :], rkv[0:64, 24, :], ACT.Tanh).then_inc(A.sem, 1)
                        act.activation(rkv[:, 25, :], rkv[:, 25, :], ACT.Sigmoid).then_inc(A.sem, 1)
                        for j in range(RT):
                            for x, (out, bias) in enumerate(((cum, "w0"), (au, "a0"))):
                                act.wait_ge(P.sem, P.at("wa"[x] + str(j)))
                                for i, (a, m) in enumerate(SPANS):
                                    act.activation(out[:, j, a:a + m], ps[:, 4 * (j % 2) + 2 * x + i, 0:m], ACT.Sigmoid,
                                                   bias=V(bias, j)).then_inc(A.sem, 1)
                        for j in range(RT):
                            act.wait_ge(W.sem, W.at(f"m1_{j}"))
                            act.activation(nr[:, j % 2, :], nr[:, j % 2, :], ACT.Sqrt).then_inc(A.sem, 1)

                    @block.tensor
                    def _(pe):
                        pe.wait_ge(lora_in, 32)
                        pe.wait_ge(A.sem, A.at("tanh"))
                        for j in range(RT):
                            for x in range(2):
                                if j >= 2:
                                    pe.wait_ge(A.sem, A.at("wa"[x] + f"1_{j - 2}"))
                                half = slice(64 * x, 64 * x + 64)
                                for i, (a, m) in enumerate(SPANS):
                                    mm = pe.matmul(ps[:, 4 * (j % 2) + 2 * x + i, 0:m], wa[half, j * 128:j * 128 + 128],
                                                   rkv[half, 24, a:a + m], start=True, stop=True)
                                mm.then_inc(P.sem, 1)
                        for j in range(RT):
                            pe.wait_ge(W.sem, W.at("sq0") if j == 0 else W.at(f"nsq{j - 1}"))
                            if j < 2:
                                pe.wait_ge(A.sem, A.at(f"w1_{RT - 2 + j}"))
                            else:
                                pe.wait_ge(W.sem, W.at(f"m1_{j - 2}"))
                            for i, (a, m) in enumerate(SPANS):
                                mm = pe.matmul(ps[:, 4 * (j % 2) + i, 0:m], C("pair"), sq[:, j % 2, a:a + m], start=True, stop=True)
                            mm.then_inc(P.sem, 1)

                    @block.vector
                    def _(dve):
                        def did(ins, name):
                            ins.then_inc(W.sem, 1)
                            dve.wait_ge(W.sem, W.at(name))

                        def squares(j, a, b):
                            did(dve.tensor_scalar(kk[:, j, :], tile_k[:, j, :], V("k_k", j), None, ALU.mult), a)
                            if j >= 2:
                                dve.wait_ge(P.sem, P.at(f"n{j - 2}"))
                            did(dve.tensor_tensor(sq[:, j % 2, :], kk[:, j, :], kk[:, j, :], ALU.mult), b)
                        squares(0, "kk0", "sq0")
                        for j in range(RT):
                            dve.wait_ge(P.sem, P.at(f"n{j}"))
                            for i, (a, m) in enumerate(SPANS):
                                dve.tensor_scalar(nr[:, j % 2, a:a + m], ps[:, 4 * (j % 2) + i, 0:m], 1e-24, None,
                                                  ALU.max).then_inc(W.sem, 1)
                            dve.wait_ge(A.sem, A.at(f"rt{j}"))
                            did(dve.reciprocal(nr[:, j % 2, :], nr[:, j % 2, :]), f"inv{j}")
                            did(dve.tensor_tensor(kk[:, j, :], kk[:, j, :], nr[:, j % 2, :], ALU.mult), f"kn{j}")
                            did(dve.tensor_scalar(tk[:, :], au[:, j, :], -1.0, V("k_a", j), ALU.add, ALU.mult), f"t{j}")
                            did(dve.scalar_tensor_tensor(tile_k[:, j, :], tk[:, :], 1.0, tile_k[:, j, :], ALU.add, ALU.mult), f"kmod{j}")
                            did(dve.tensor_tensor(au[:, j, :], kk[:, j, :], au[:, j, :], ALU.mult), f"b{j}")
                            did(dve.tensor_tensor_scan(cum[:, j, :], C("start"), cum[:, j, :], 0.0, ALU.mult, ALU.add), f"cum{j}")
                            if j + 1 < RT:
                                squares(j + 1, f"nkk{j}", f"nsq{j}")

            with ExitStack() as st:
                sv = sb(st, "step_in", [128, 6, 2, 64])
                tv = sb(st, "step_vecs", [128, 6, 64])
                state = sb(st, "step_state", [128, 64, 64])
                prod = sb(st, "step_prod", [128, 64, 64])
                dec = sb(st, "step_decay", [128, RT, NS])
                sa = sb(st, "step_sa", [128, 64])
                yb = sb(st, "step_y", [128, 64])
                yd2 = sb(st, "step_y2", [128, 128])
                state_in, state_out = sem("state_in"), sem("state_out")
                S = Steps(sem("step"), ["dec"] + [f"v{i}" for i in range(6)] + ["T", "ta", "tb", "Sa", "sa", "Sw", "sab", "S1",
                                        "vk", "S2", "Sr", "y", "y0", "ya", "yb", "yT", "t2", "t2r", "oa", "ob"])
                with nc.Block() as block:
                    @block.sync
                    def _(sp):
                        sp.dma_start(state[:, :, :], s0).then_inc(state_in, 16)
                        sp.wait_ge(S.sem, S.at("S2"))
                        sp.dma_start(wkv_s, state[:, :, :]).then_inc(state_out, 16)
                        sp.wait_ge(state_out, 16)

                    @block.scalar
                    def _(act):
                        act.activation(dec[:, :, :], cum[:, :, SEQ:TOK], ACT.Exp, scale=-DECAY).then_inc(S.sem, 1)

                    @block.tensor
                    def _(pe):
                        pe.wait_ge(S.sem, S.at("v5"))
                        for i in range(6):
                            mm = pe.transpose(ps[:, i // 4, i % 4 * 128:i % 4 * 128 + 128], sv[:, i, :, :].rearrange("p a b -> p (a b)"),
                                              C("ident"))
                        mm.then_inc(S.sem, 1)
                        pe.wait_ge(S.sem, S.at("yb"))
                        pe.transpose(ps[:, 2, 0:128], yd2[:, :], C("ident")).then_inc(S.sem, 1)

                    @block.vector
                    def _(dve):
                        def did(ins, name):
                            ins.then_inc(S.sem, 1)
                            dve.wait_ge(S.sem, S.at(name))
                        dve.wait_ge(S.sem, S.at("dec"))
                        rows = [kk[:, :, SEQ:TOK], dec[:, :, :], au[:, :, SEQ:TOK], tile_k[:, :, SEQ:TOK], tile_v[:, :, SEQ:TOK],
                                tile_r[:, :, SEQ:TOK]]
                        for i, v in enumerate(rows):
                            did(dve.tensor_copy(sv[:, i, :, :].rearrange("p t (a b) -> p t a b", a=RT),
                                                v.unsqueeze(1).to_broadcast([128, 2, RT, NS])), f"v{i}")
                        dve.wait_ge(S.sem, S.at("T"))
                        both = ps[:, 0:2, :].rearrange("p a (b c) -> p (a b) c", b=4)
                        did(dve.tensor_copy(tv[0:64, :, :], both[0:64, 0:6, 0:64]), "ta")
                        did(dve.tensor_copy(tv[64:128, :, :], both[64:128, 0:6, 64:128]), "tb")
                        cols = lambda i: tv[:, i, :].unsqueeze(1).to_broadcast([128, 64, 64])
                        rows_ = lambda a: a.unsqueeze(2).to_broadcast([128, 64, 64])
                        st_, pr = state[:, :, :], prod[:, :, :]
                        dve.wait_ge(state_in, 16)
                        did(dve.tensor_tensor(pr, st_, cols(0), ALU.mult), "Sa")
                        did(dve.reduce_sum(sa[:, :], pr, AX.X), "sa")
                        did(dve.tensor_tensor(st_, st_, cols(1), ALU.mult), "Sw")
                        did(dve.tensor_tensor(pr, rows_(sa[:, :]), cols(2), ALU.mult), "sab")
                        did(dve.tensor_tensor(st_, st_, pr, ALU.subtract), "S1")
                        did(dve.tensor_tensor(pr, rows_(tv[:, 4, :]), cols(3), ALU.mult), "vk")
                        did(dve.tensor_tensor(st_, st_, pr, ALU.add), "S2")
                        did(dve.tensor_tensor(pr, st_, cols(5), ALU.mult), "Sr")
                        did(dve.reduce_sum(yb[:, :], pr, AX.X), "y")
                        did(dve.memset(yd2[:, :], 0.0), "y0")
                        did(dve.tensor_copy(yd2[0:64, 0:64], yb[0:64, :]), "ya")
                        did(dve.tensor_copy(yd2[64:128, 64:128], yb[64:128, :]), "yb")
                        dve.wait_ge(S.sem, S.at("yT"))
                        last_r, last_a = tile_r[:, :, SEQ:TOK], au[:, :, SEQ:TOK]
                        rk = vt[:, VEC["r_k"]:VEC["r_k"] + RT].unsqueeze(2).to_broadcast([128, RT, NS])
                        did(dve.tensor_tensor(last_a, last_r, tile_k[:, :, SEQ:TOK], ALU.mult), "t2")
                        did(dve.tensor_tensor(last_a, last_a, rk, ALU.mult), "t2r")
                        for x, name in ((0, "oa"), (64, "ob")):
                            did(dve.tensor_copy(last_r[x:x + 64], ps[x:x + 64, 2, x:x + 64].rearrange("p (a b) -> p a b", a=RT)), name)

            with ExitStack() as st:
                e65 = sb(st, "decay", [128, RT, CH + 1])
                ei = sb(st, "decay_inv", [128, RT, CH])
                stg = sb(st, "chunk", [128, RT, 4, CH])
                vst = sb(st, "chunk_v", [128, RT, 2, CH])
                qa = sb(st, "rhs_left", [128, 2, RT, CH])
                gr = sb(st, "out_right", [128, 2, RT, CH])
                sl = sb(st, "inverse", [128, 2, 6, 4 * 128])
                xs = sb(st, "solve", [128, RT, 128])
                svb = sb(st, "state_v", [128, 2, RT, CH])
                zb = sb(st, "sa_v", [128, 2, RT, CH])
                sbd = sb(st, "state_diag", [128, RT, 128])
                rh = sb(st, "rhs", [128, RT, CH])
                bk = sb(st, "bk_tok", [128, RT, 128])
                rc = sb(st, "chunk_r", [128, RT, CH])
                wl = sb(st, "chunk_decay", [128, RT, 1])
                turn_ok = sem("turn_ok")
                zeroed = sem("zeroed")
                pool_woke = sem("pool_woke")
                A0 = Steps(sem("stage_act"), ["E", "Ei", "qa_a", "qa_b"])
                W0 = Steps(sem("stage_dve"), ["at", "rt", "u2a", "u3a", "u2b", "u3b"])
                P0 = Steps(sem("gram_pe"), ["mg0", "mg1"])
                W1 = Steps(sem("mask_dve"), [f"{x}0" for x in ("dA", "dB", "tA", "tB", "oA", "oB", "x1", "kA", "kB", "gA", "gB")]
                           + [f"{x}1" for x in ("dA", "dB", "tA", "tB", "oA", "oB", "x1", "gA", "gB", "kA", "kB")])
                A = Steps(sem("rw_act"), ["wl", "D2t0", "bk", "D2t1", "D4t0", "D4t1", "v1", "v2", "v3", "v4"]
                          + [f"{x}{q}" for x in ("Nt", "XDt", "N2t", "N4t", "X") for q in range(2)] + ["rhs", "za", "y", "sd_a", "sd_b"])
                P = Steps(sem("rw_pe"), ["D20", "D2t0", "bk", "D21", "D2t1", "D4t0", "DX0", "D4t1", "DX1", "v"]
                          + [f"{x}{q}" for xs_ in (("DXX",), ("N", "Nt"), ("XDt",), ("N2", "N2t"), ("N4t", "NY"), ("NYY",), ("X",))
                             for q in range(2) for x in xs_] + ["rhs", "sa", "y", "s"])
                W = Steps(sem("rw_dve"), [f"{x}{q}" for xs_ in (("D2",), ("X2",), ("XD",), ("N", "Y1"), ("N2",), ("Y2",), ("Y3",))
                                          for q in range(2) for x in xs_] + ["zb", "sA", "sB", "swA", "swB"])
                G = Steps(sem("rw_pool"), ["vst", "rc", "t2", "t2r"])

                def at(c, steps, name):
                    return c * len(steps.names) + steps.at(name)

                def chunk(t, c):
                    return t[:, :, bass.ds(c * CH, CH)]

                def blocks(t):
                    return t.rearrange("p (a b) -> p a b", a=4)

                def turns_of(eng, body):
                    with eng.Fori(0, NCH - 1) as c:
                        body(c, False)
                    body(NCH - 1, True)

                AA, BB = slice(0, 64), slice(64, 128)
                with nc.Block() as block:
                    @block.vector
                    def _(dve):
                        dve.memset(sl[:, :, :, :], 0.0).then_inc(zeroed, 1)
                        dve.memset(svb[:, :, :, :], 0.0).then_inc(zeroed, 1)
                        dve.memset(sbd[:, :, :], 0.0).then_inc(zeroed, 1)
                        dve.memset(e65[:, :, 0:1], 1.0).then_inc(zeroed, 1)
                        dve.sem_inc(turn_ok, 1)

                with nc.Block() as block:
                    @block.gpsimd
                    def _(pool):
                        pool.wait_ge(W0.sem, W0.at("u3b"))
                        with pool.Fori(0, NCH) as c:
                            pool.wait_ge(turn_ok, c + 1)
                            pool.tensor_copy(vst[:, :, :, :], chunk(tile_v, c).unsqueeze(2).to_broadcast([128, RT, 2, CH])).then_inc(G.sem, 1)
                            pool.tensor_copy(rc[:, :, :], stg[:, :, 1, :]).then_inc(G.sem, 1)
                            pool.tensor_tensor(chunk(au, c), chunk(tile_r, c), chunk(tile_k, c), ALU.mult).then_inc(G.sem, 1)
                            pool.wait_ge(G.sem, at(c, G, "t2"))
                            pool.sem_inc(pool_woke, 1)
                            rk = vt[:, VEC["r_k"]:VEC["r_k"] + RT].unsqueeze(2).to_broadcast([128, RT, CH])
                            pool.tensor_tensor(chunk(au, c), chunk(au, c), rk, ALU.mult).then_inc(G.sem, 1)

                    @block.scalar
                    def _(act):
                        def decays(n):
                            act.activation(e65[:, :, 1:CH + 1], chunk(cum, n), ACT.Exp, scale=-DECAY).then_inc(A0.sem, 1)
                            act.activation(ei[:, :, :], chunk(cum, n), ACT.Exp, scale=DECAY).then_inc(A0.sem, 1)

                        def left_a(n):
                            act.wait_ge(W0.sem, at(n, W0, "at"))
                            act.activation(qa[AA, 0, :, :], stg[AA, :, 0, :], ACT.Copy).then_inc(A0.sem, 1)
                            act.activation(qa[BB, 1, :, :], stg[BB, :, 0, :], ACT.Copy).then_inc(A0.sem, 1)

                        def body(c, last):
                            def leave(dst, src, name):
                                act.wait_ge(P.sem, at(c, P, name))
                                act.activation(dst, src, ACT.Copy).then_inc(A.sem, 1)

                            def chain(name, slot, b, q):
                                leave(sl[:, q, slot, :], ps[:, 4 * q + b, :], f"{name}{q}")
                            act.activation(wl[:, :, :], e65[:, :, CH:CH + 1], ACT.Copy).then_inc(A.sem, 1)
                            chain("D2t", 5, 1, 0)
                            leave(bk[:, :, :], ps[:, 2:4, :], "bk")
                            chain("D2t", 5, 1, 1)
                            for q in range(2):
                                chain("D4t", 0, 0, q)
                            if not last:
                                act.wait_ge(A.sem, at(c, A, "wl"))
                                decays(c + 1)
                            vv = ps[:, 6:8, :].rearrange("p a (b c) -> p (a b) c", b=4)
                            act.wait_ge(P.sem, at(c, P, "v"))
                            for t in (svb, zb):
                                act.activation(t[BB, 0, :, :], vv[BB, :, 0:64], ACT.Copy).then_inc(A.sem, 1)
                                act.activation(t[AA, 1, :, :], vv[AA, :, 64:128], ACT.Copy).then_inc(A.sem, 1)
                            for name, slot, b in (("Nt", 1, 1), ("XDt", 4, 0), ("N2t", 3, 0), ("N4t", 0, 0)):
                                for q in range(2):
                                    chain(name, slot, b, q)
                            for q in range(2):
                                leave(xs[:, 4 * q:4 * q + 4, :], ps[:, 4 * q + 1, :], f"X{q}")
                            leave(rh[:, :, :], ps[:, 6, :], "rhs")
                            if not last:
                                left_a(c + 1)
                            act.wait_ge(P.sem, at(c, P, "sa"))
                            act.activation(zb[AA, 0, :, :], ps[AA, 7, :], ACT.Copy).then_inc(A.sem, 1)
                            act.wait_ge(G.sem, at(c, G, "t2r"))
                            act.wait_ge(P.sem, at(c, P, "y"))
                            act.activation(chunk(tile_r, c), ps[:, 4, :].rearrange("p (a b) -> p a b", a=RT), ACT.Copy).then_inc(A.sem, 1)
                            act.wait_ge(W.sem, at(c, W, "swB"))
                            act.activation(sbd[AA, :, 0:64], svb[AA, 0, :, :], ACT.Copy).then_inc(A.sem, 1)
                            act.activation(sbd[BB, :, 64:128], svb[BB, 1, :, :], ACT.Copy).then_inc(A.sem, 1)
                        decays(0)
                        left_a(0)
                        turns_of(act, body)

                    @block.vector
                    def _(dve):
                        def mask(name, rows, n):
                            return C(name)[rows, 0:n].unsqueeze(1).to_broadcast([64, 4, n])

                        def did(c, steps, ins, name):
                            ins.then_inc(steps.sem, 1)
                            dve.wait_ge(steps.sem, at(c, steps, name))

                        def stage(n, name):
                            rows = AA if name[-1] == "a" else BB
                            u = (au, tile_k) if name[-1] == "a" else (tile_k, au)
                            if name == "at":
                                dve.wait_ge(A0.sem, at(n, A0, "E"))
                                ins = dve.scalar_tensor_tensor(stg[:, :, 0, :], chunk(kk, n), -1.0, e65[:, :, 0:CH], ALU.mult, ALU.mult)
                            elif name == "rt":
                                ins = dve.tensor_tensor(stg[:, :, 1, :], chunk(tile_r, n), e65[:, :, 1:CH + 1], ALU.mult)
                            else:
                                if name == "u2a":
                                    dve.wait_ge(A0.sem, at(n, A0, "Ei"))
                                slot = int(name[1])
                                ins = dve.tensor_tensor(stg[rows, :, slot, :], chunk(u[slot - 2], n)[rows], ei[rows, :, :], ALU.mult)
                            did(n, W0, ins, name)

                        def powers(n, q, which):
                            slot, m, name = {"d": (0, 0, "diag"), "t": (1, 1, "diag_t"), "o": (2, 1, "off_t")}[which]
                            for rows, y, off in ((AA, "A", 0), (BB, "B", 64)):
                                src = ps[rows, 4 * q + (off > 0), :].rearrange("p (a m b) -> p a m b", a=4, m=2)[:, :, m, :]
                                did(n, W1, dve.tensor_tensor(blocks(sl[rows, q, slot, :])[:, :, off:off + 64], src,
                                                             mask(name, rows, 64), ALU.mult), f"{which}{y}{q}")

                        def plus_one(n, q):
                            did(n, W1, dve.tensor_tensor(blocks(sl[:, q, 3, :]), blocks(sl[:, q, 0, :]),
                                                         C("ident").unsqueeze(1).to_broadcast([128, 4, 128]), ALU.add), f"x1{q}")

                        def rights(n, q):
                            for y, b in (("A", 2), ("B", 3)):
                                did(n, W1, dve.tensor_tensor(gr[:, b - 2, 4 * q:4 * q + 4, :], blocks(ps[:, 4 * q + b, :])[:, :, 64:128],
                                                             C("gram")[:, 64:128].unsqueeze(1).to_broadcast([128, 4, 64]), ALU.mult), f"g{y}{q}")

                        def lefts(n, q):
                            for y, b, rows in (("A", 2, BB), ("B", 3, AA)):
                                did(n, W1, dve.tensor_tensor(qa[rows, b - 2, 4 * q:4 * q + 4, :], blocks(ps[rows, 4 * q + b, :])[:, :, 0:64],
                                                             mask("gram", rows, 64), ALU.mult), f"k{y}{q}")

                        def body(c, last):
                            def did_(ins, name):
                                did(c, W, ins, name)

                            def both(name, need, fn):
                                for q in range(2):
                                    dve.wait_ge(P.sem, at(c, P, f"{need}{q}"))
                                    did_(fn(q), f"{name}{q}")
                            out = lambda q, b: ps[:, 4 * q + b, :]

                            def next_stage(name):
                                if not last:
                                    stage(c + 1, name)
                            dve.wait_ge(P0.sem, at(c, P0, "mg1"))
                            for x in "dto":
                                powers(c, 1, x)
                            plus_one(c, 1)
                            dve.wait_ge(P.sem, at(c, P, "D20"))
                            did_(dve.tensor_copy(sl[:, 0, 4, :], out(0, 0)), "D20")
                            rights(c, 1)
                            lefts(c, 1)
                            dve.wait_ge(P.sem, at(c, P, "D21"))
                            did_(dve.tensor_copy(sl[:, 1, 4, :], out(1, 0)), "D21")
                            both("X2", "DX", lambda q: dve.tensor_tensor(sl[:, q, 3, :], out(q, 1), sl[:, q, 3, :], ALU.add))
                            dve.wait_ge(G.sem, at(c, G, "rc"))
                            next_stage("at")
                            both("XD", "DXX", lambda q: dve.tensor_tensor(sl[:, q, 3, :], out(q, 0), sl[:, q, 3, :], ALU.add))
                            next_stage("rt")
                            for q in range(2):
                                dve.wait_ge(P.sem, at(c, P, f"N{q}"))
                                did_(dve.tensor_copy(sl[:, q, 0, :], out(q, 0)), f"N{q}")
                                did_(dve.tensor_tensor(blocks(sl[:, q, 5, :]), blocks(sl[:, q, 0, :]),
                                                       C("ident").unsqueeze(1).to_broadcast([128, 4, 128]), ALU.add), f"Y1{q}")
                            next_stage("u2a")
                            both("N2", "N2", lambda q: dve.tensor_copy(sl[:, q, 2, :], out(q, 1)))
                            next_stage("u3a")
                            both("Y2", "NY", lambda q: dve.tensor_tensor(sl[:, q, 5, :], out(q, 1), sl[:, q, 5, :], ALU.add))
                            next_stage("u2b")
                            both("Y3", "NYY", lambda q: dve.tensor_tensor(sl[:, q, 5, :], out(q, 0), sl[:, q, 5, :], ALU.add))
                            next_stage("u3b")
                            if not last:
                                dve.wait_ge(P0.sem, at(c + 1, P0, "mg0"))
                                for x in "dt":
                                    powers(c + 1, 0, x)
                            dve.wait_ge(P.sem, at(c, P, "sa"))
                            did_(dve.tensor_copy(zb[BB, 1, :, :], ps[BB, 7, :]), "zb")
                            if not last:
                                powers(c + 1, 0, "o")
                                plus_one(c + 1, 0)
                                lefts(c + 1, 0)
                                dve.wait_ge(P.sem, at(c, P, "y"))
                                rights(c + 1, 0)
                            dve.wait_ge(P.sem, at(c, P, "s"))
                            halves = ((AA, 0, "A"), (BB, 1, "B"))
                            for rows, x, y in halves:
                                did_(dve.tensor_tensor(svb[rows, x, :, :], ps[rows, 5, :].rearrange("p (a b) -> p a b", a=RT),
                                                       svb[rows, x, :, :], ALU.add), f"s{y}")
                            for rows, x, y in halves:
                                did_(dve.tensor_tensor(svb[rows, x, :, :], svb[rows, x, :, :],
                                                       wl[rows, :, :].to_broadcast([64, RT, CH]), ALU.mult), f"sw{y}")
                            dve.wait_ge(A.sem, at(c, A, "sd_b"))
                            dve.sem_inc(turn_ok, 1)

                        for name in W0.names:
                            stage(0, name)
                        dve.wait_ge(P0.sem, P0.at("mg0"))
                        for x in "dto":
                            powers(0, 0, x)
                        plus_one(0, 0)
                        lefts(0, 0)
                        rights(0, 0)
                        turns_of(dve, body)

                    @block.tensor
                    def _(pe):
                        def grams(q):
                            for n in range(4):
                                j = 4 * q + n
                                for rows, b in ((AA, 2), (BB, 3)):
                                    pe.matmul(ps[:, 4 * q + b, n * 128:n * 128 + 128], stg[rows, j, 2:4, :], stg[rows, j, 0:2, :],
                                              start=True, stop=True)
                                for rows, unit, b in ((AA, 2, 0), (BB, 3, 1)):
                                    pe.matmul(ps[rows, 4 * q + b, n * 128:n * 128 + 64], stg[rows, j, unit, :], stg[rows, j, 0, :],
                                              start=True, stop=True)
                                    mm = pe.matmul(ps[rows, 4 * q + b, n * 128 + 64:n * 128 + 128], stg[rows, j, 0, :],
                                                   stg[rows, j, unit, :], start=True, stop=True)
                            mm.then_inc(P0.sem, 1)

                        def four(q, b, left, right):
                            for n in range(4):
                                ns = slice(n * 128, n * 128 + 128)
                                mm = pe.matmul(ps[:, 4 * q + b, ns], sl[:, q, left, ns], sl[:, q, right, ns], start=True, stop=True)
                            mm.then_inc(P.sem, 1)

                        def heads(b, left, right):
                            for j in range(RT):
                                for rows, x in ((AA, 0), (BB, 1)):
                                    mm = pe.matmul(ps[rows, b, j * 64:j * 64 + 64], left(x, j), right(x, j), start=True, stop=True)
                            mm.then_inc(P.sem, 1)

                        def body(c, last):
                            pe.wait_ge(W1.sem, at(c, W1, "x10"))
                            four(0, 0, 1, 0)
                            four(0, 1, 0, 1)
                            pe.wait_ge(W1.sem, at(c, W1, "gB0"))
                            for j in range(RT):
                                mm = pe.transpose(ps[:, 2 + j // 4, j % 4 * 128:j % 4 * 128 + 128], stg[:, j, 2:4, :], C("ident"))
                            mm.then_inc(P.sem, 1)
                            pe.wait_ge(W1.sem, at(c, W1, "x11"))
                            four(1, 0, 1, 0)
                            four(1, 1, 0, 1)
                            for q in range(2):
                                pe.wait_ge(W.sem, at(c, W, f"D2{q}"))
                                pe.wait_ge(A.sem, at(c, A, f"D2t{q}"))
                                four(q, 0, 4, 5)
                                four(q, 1, 5, 3)
                            pe.wait_ge(W1.sem, at(c, W1, "kB1"))
                            pe.wait_ge(G.sem, at(c, G, "vst"))
                            for j in range(RT):
                                mm = pe.transpose(ps[:, 6 + j // 4, j % 4 * 128:j % 4 * 128 + 128], vst[:, j, :, :], C("ident"))
                            mm.then_inc(P.sem, 1)
                            for q in range(2):
                                pe.wait_ge(A.sem, at(c, A, f"D4t{q}"))
                                pe.wait_ge(W.sem, at(c, W, f"X2{q}"))
                                four(q, 0, 0, 3)
                            for q in range(2):
                                pe.wait_ge(W.sem, at(c, W, f"XD{q}"))
                                four(q, 0, 2, 3)
                                four(q, 1, 3, 2)
                            for q in range(2):
                                pe.wait_ge(W.sem, at(c, W, f"N{q}"))
                                for n in range(4):
                                    ns = slice(n * 128, n * 128 + 128)
                                    mm = pe.transpose(ps[:, 4 * q, ns], sl[:, q, 3, ns], C("ident"))
                                mm.then_inc(P.sem, 1)
                            for q in range(2):
                                pe.wait_ge(A.sem, at(c, A, f"Nt{q}"))
                                four(q, 1, 1, 0)
                                pe.wait_ge(A.sem, at(c, A, f"XDt{q}"))
                                four(q, 0, 0, 1)
                            for q in range(2):
                                pe.wait_ge(W.sem, at(c, W, f"N2{q}"))
                                pe.wait_ge(A.sem, at(c, A, f"N2t{q}"))
                                four(q, 0, 2, 3)
                                four(q, 1, 3, 5)
                            for q in range(2):
                                pe.wait_ge(A.sem, at(c, A, f"N4t{q}"))
                                pe.wait_ge(W.sem, at(c, W, f"Y2{q}"))
                                four(q, 0, 0, 5)
                            for q in range(2):
                                pe.wait_ge(W.sem, at(c, W, f"Y3{q}"))
                                four(q, 1, 4, 5)
                            pe.wait_ge(A0.sem, at(c, A0, "qa_b"))
                            pe.wait_ge(A.sem, at(c, A, "v4"))
                            pe.wait_ge(turn_ok, c + 1)
                            heads(6, lambda x, j: qa[:, x, j, :], lambda x, j: svb[:, x, j, :])
                            if not last:
                                pe.wait_ge(A.sem, at(c, A, "X0"))
                                pe.wait_ge(W0.sem, at(c + 1, W0, "u3b"))
                                grams(0)
                            pe.wait_ge(A.sem, at(c, A, "rhs"))
                            for j in range(RT):
                                mm = pe.matmul(ps[:, 7, j * 64:j * 64 + 64], xs[:, j, :], rh[:, j, :], start=True, stop=True)
                            mm.then_inc(P.sem, 1)
                            pe.wait_ge(A.sem, at(c, A, "za"))
                            pe.wait_ge(W.sem, at(c, W, "zb"))
                            for j in range(RT):
                                js = slice(j * 64, j * 64 + 64)
                                pe.matmul(ps[:, 4, js], sbd[:, j, :], rc[:, j, :], start=True, stop=False, skip_group_check=True)
                                for rows, x in ((AA, 0), (BB, 1)):
                                    mm = pe.matmul(ps[rows, 4, js], zb[:, x, j, :], gr[:, x, j, :], start=False, stop=True,
                                                   skip_group_check=True)
                            mm.then_inc(P.sem, 1)
                            heads(5, lambda x, j: bk[:, j, 64 * x:64 * x + 64], lambda x, j: zb[:, x, j, :])
                            if not last:
                                pe.wait_ge(A.sem, at(c, A, "y"))
                                pe.wait_ge(W.sem, at(c, W, "sB"))
                                grams(1)
                        pe.wait_ge(W0.sem, W0.at("u3b"))
                        for q in range(2):
                            grams(q)
                        turns_of(pe, body)

                wkv_out = sem("wkv_out")
                with nc.Block() as block:
                    @block.sync
                    def _(sp):
                        for rows, x in ((AA, 0), (BB, 1)):
                            sp.dma_start(wkv_p[rows], svb[rows, x, :, :]).then_inc(wkv_out, 16)
                        sp.wait_ge(wkv_out, 32)

            with ExitStack() as st:
                sq = sb(st, "y_sq", [128, 2, TOK])
                rn = sb(st, "y_rms", [128, 2, TOK])
                bv = sb(st, "bonus", [128, 2, TOK])
                P = Steps(sem("gn_pe"), ["mean0"] + [f"{x}{j}" for j in range(RT) for x in ("var", "bon", "gate") + (("nmean",) if j + 1 < RT else ())])
                A = Steps(sem("gn_act"), [f"{x}{j}" for j in range(RT) for x in ("sq", "rt")])
                W = Steps(sem("gn_dve"), [f"{x}{j}" for j in range(RT) for x in ("c0_", "c1_", "m0_", "m1_", "bv0_", "bv1_", "inv", "n", "gb", "add", "o0_", "o1_")])
                y_out = sem("yr_out")
                with nc.Block() as block:
                    @block.tensor
                    def _(pe):
                        def mean(j):
                            for i, (a, m) in enumerate(SPANS):
                                mm = pe.matmul(ps[:, i, 0:m], C("pair"), tile_r[:, j, a:a + m], start=True, stop=True)
                            mm.then_inc(P.sem, 1)
                        mean(0)
                        for j in range(RT):
                            pe.wait_ge(A.sem, A.at(f"sq{j}"))
                            if j:
                                pe.wait_ge(W.sem, W.at(f"o1_{j - 1}"))
                            for i, (a, m) in enumerate(SPANS):
                                mm = pe.matmul(ps[:, 2 + i, 0:m], C("pair"), sq[:, j % 2, a:a + m], start=True, stop=True)
                            mm.then_inc(P.sem, 1)
                            for i, (a, m) in enumerate(SPANS):
                                mm = pe.matmul(ps[:, 4 + i, 0:m], C("pair"), au[:, j, a:a + m], start=True, stop=True)
                            mm.then_inc(P.sem, 1)
                            for i, (a, m) in enumerate(SPANS):
                                mm = pe.matmul(ps[:, 6 + i, 0:m], g2s[:, j * 128:j * 128 + 128], rkv[:, 25, a:a + m], start=True, stop=True)
                            mm.then_inc(P.sem, 1)
                            if j + 1 < RT:
                                mean(j + 1)

                    @block.scalar
                    def _(act):
                        for j in range(RT):
                            act.wait_ge(W.sem, W.at(f"c1_{j}"))
                            act.activation(sq[:, j % 2, :], tile_r[:, j, :], ACT.Square).then_inc(A.sem, 1)
                            act.wait_ge(W.sem, W.at(f"m1_{j}"))
                            act.activation(rn[:, j % 2, :], rn[:, j % 2, :], ACT.Sqrt).then_inc(A.sem, 1)

                    @block.vector
                    def _(dve):
                        def did(ins, name):
                            ins.then_inc(W.sem, 1)
                            dve.wait_ge(W.sem, W.at(name))
                        for j in range(RT):
                            b = j % 2
                            dve.wait_ge(P.sem, P.at("mean0") if j == 0 else P.at(f"nmean{j - 1}"))
                            for i, (a, m) in enumerate(SPANS):
                                did(dve.scalar_tensor_tensor(tile_r[:, j, a:a + m], ps[:, i, 0:m], -1.0 / 64, tile_r[:, j, a:a + m],
                                                             ALU.mult, ALU.add), f"c{i}_{j}")
                            dve.wait_ge(P.sem, P.at(f"var{j}"))
                            for i, (a, m) in enumerate(SPANS):
                                did(dve.tensor_scalar(rn[:, b, a:a + m], ps[:, 2 + i, 0:m], 1.0 / 64, 64e-5, ALU.mult, ALU.add), f"m{i}_{j}")
                            dve.wait_ge(P.sem, P.at(f"bon{j}"))
                            for i, (a, m) in enumerate(SPANS):
                                did(dve.tensor_tensor(bv[:, b, a:a + m], ps[:, 4 + i, 0:m], tile_v[:, j, a:a + m], ALU.mult), f"bv{i}_{j}")
                            dve.wait_ge(A.sem, A.at(f"rt{j}"))
                            did(dve.reciprocal(rn[:, b, :], rn[:, b, :]), f"inv{j}")
                            did(dve.tensor_tensor(tile_r[:, j, :], tile_r[:, j, :], rn[:, b, :], ALU.mult), f"n{j}")
                            did(dve.tensor_scalar(tile_r[:, j, :], tile_r[:, j, :], V("lnx_g", j), V("lnx_b", j), ALU.mult, ALU.add), f"gb{j}")
                            did(dve.tensor_tensor(tile_r[:, j, :], tile_r[:, j, :], bv[:, b, :], ALU.add), f"add{j}")
                            dve.wait_ge(P.sem, P.at(f"gate{j}"))
                            for i, (a, m) in enumerate(SPANS):
                                did(dve.tensor_tensor(tile_r[:, j, a:a + m], ps[:, 6 + i, 0:m], tile_r[:, j, a:a + m], ALU.mult), f"o{i}_{j}")

                    @block.sync
                    def _(sp):
                        for j in range(RT):
                            sp.wait_ge(W.sem, W.at(f"o1_{j}"))
                            sp.dma_start(ymix[j, :, :], tile_r[:, j, :]).then_inc(y_out, 16)
                        sp.wait_ge(y_out, 16 * RT)
        if upto <= 4:
            return

        x = sb(stack, "x", [128, KT, TOK])
        with ExitStack() as st:
            mkb = sb(st, "mk", [128, KT, MEM])
            mvb = sb(st, "mv", [128, 2, D])
            memx = mvb[:, :, :].rearrange("p a (b c) -> p (a b) c", c=MEM)
            mh = sb(st, "mem_hi", [128, KT, MEM], f32r)
            ml = sb(st, "mem_lo", [128, KT, MEM], f32r)
            whi = sb(st, "whi_b", [128, 2, BLK], f32r)
            wlo = sb(st, "wlo_b", [128, 2, BLK], f32r)
            rstd = sb(st, "rstd_mem", [128, MEM])
            sq = sb(st, "sq_b", [128, 2, MEM])
            rcol = sb(st, "rstd_col", [128, 2])
            mem_in, mem_out, col_done = sem("mem_in"), sem("mem_out"), sem("col_done")
            with nc.Block() as block:
                @block.sync
                def _(sp):
                    sp.dma_start(memx, memt.rearrange("k p n -> p k n")).then_inc(mem_in, 16)
                    sp.wait_ge(mem_in, 16)

            def evac_ck(dve, i, u, t):
                dve.tensor_tensor(tile_of(mkb, i), ps[:, 2 * u, 0:MEM], rstd[:, :], ALU.mult).then_inc(out_done, 1)

            project("ck", CK0, KT, mh, ml, whi, wlo, [(0, MEM)], evac_ck, memx, "g_mem", (rstd, sq))

            j0 = jobs[0]
            jobs[0] += 4
            with nc.Block() as block:
                @block.sync
                def _(sp):
                    sp.dma_start(mk_o.rearrange("k p n -> p k n"), mkb[:, :, :]).then_inc(mem_out, 16)
                    with sp.Fori(0, 8) as t:
                        for u in range(2):
                            load_block(sp, t * 2 + (CV0 + u), u)

                @block.scalar
                def _(act):
                    act.wait_ge(col_done, 1)
                    act.activation(rcol[:, :], ps[:, 6, 0:2], ACT.Copy).then_inc(col_done, 1)
                    with act.Fori(0, 8) as t:
                        for u in range(2):
                            weight_hi(act, whi, t * 2 + (CV0 + u), u, t + CV0 // 2)

                @block.vector
                def _(dve):
                    dve.wait_ge(col_done, 2)
                    with dve.Fori(0, 2) as t:
                        for n in range(2):
                            for k in range(4):
                                weight_lo(dve, whi, wlo, t * 8 + (CV0 + 4 * n + k), k % 2)
                            dve.wait_ge(pe_done, t * 8 + (CV0 + 4 * n + 3 + 3))
                            for m in range(2):
                                ins = dve.tensor_scalar(mvb[:, m, bass.ds((t * 2 + n) * 512, 512)], ps[:, 2 * n + m, :],
                                                        rcol[:, m:m + 1], None, ALU.mult)
                            ins.then_inc(out_done, 1)

                @block.tensor
                def _(pe):
                    for m in range(2):
                        mm = pe.matmul(ps[:, 6, m:m + 1], rstd[0:1, m * 128:m * 128 + 128], C("ones")[0:1, 0:1], start=True, stop=True)
                    mm.then_inc(col_done, 1)
                    with pe.Fori(0, 2) as t:
                        for n in range(2):
                            pe.wait_ge(out_done, t * 2 + (j0 + n + 1))
                            for k4 in range(4):
                                pe.wait_ge(wlo_done, t * 8 + (CV0 + 4 * n + k4 + 1))
                                for k in range(4):
                                    for at, wt in ((mh, whi), (mh, wlo), (ml, whi)):
                                        for m in range(2):
                                            mm = pe.matmul(ps[:, 2 * n + m, :], at[:, 4 * k4 + k, m * 128:m * 128 + 128],
                                                           wt[:, k4 % 2, k * 512:k * 512 + 512],
                                                           start=(k4 == 0 and k == 0 and at is mh and wt is whi),
                                                           stop=(k4 == 3 and k == 3 and at is ml))
                                mm.then_inc(pe_done, 1)

            with nc.Block() as block:
                @block.sync
                def _(sp):
                    sp.dma_start(mv_o.rearrange("m p n -> p m n"), mvb[:, :, :]).then_inc(mem_out, 16)
                    sp.wait_ge(mem_out, 32)
        if upto <= 5:
            return

        def add_to_x(dve, i, u, t):
            for s, (a, m) in enumerate(SPANS):
                if isinstance(i, int):
                    xi = x[:, i, a:a + m]
                else:
                    xi = x[:, bass.ds(i, 1), a:a + m].rearrange("p o n -> p (o n)")
                ins = dve.tensor_tensor(xi, ps[:, 2 * u + s, 0:m], xi, ALU.add)
            ins.then_inc(out_done, 1)

        late = ExitStack()
        with ExitStack() as st:
            ah = sb(st, "y_hi", [128, KT, TOK], f32r)
            al = sb(st, "y_lo", [128, KT, TOK], f32r)
            whi = sb(st, "whi_c", [128, 2, BLK], f32r)
            wlo = sb(st, "wlo_c", [128, 2, BLK], f32r)
            y = sb(st, "y_mix", [128, KT, TOK])
            y_in = sem("y_in")
            with nc.Block() as block:
                @block.sync
                def _(sp):
                    sp.dma_start(y[:, :, :], ymix.rearrange("k p n -> p k n")).then_inc(y_in, 16)
                    sp.dma_start(x[:, :, :], xt.rearrange("k p n -> p k n")).then_inc(y_in, 16)
                    sp.wait_ge(y_in, 32)
            project("wo", WO0, KT, ah, al, whi, wlo, SPANS, add_to_x, y)

        qc = sb(late, "qc", [128, KT, TOK])
        with ExitStack() as st:
            ah = sb(st, "hx_hi", [128, KT, TOK], f32r)
            al = sb(st, "hx_lo", [128, KT, TOK], f32r)
            whi = sb(st, "whi_d", [128, 2, BLK], f32r)
            wlo = sb(st, "wlo_d", [128, 2, BLK], f32r)
            rstd = sb(st, "rstd_x", [128, TOK])
            sq = sb(st, "sq_d", [128, 2, TOK])

            def evac_q(dve, i, u, t):
                for s, (a, m) in enumerate(SPANS):
                    qi = qc[:, i, a:a + m] if isinstance(i, int) else qc[:, bass.ds(i, 1), a:a + m].rearrange("p o n -> p (o n)")
                    ins = dve.tensor_tensor(qi, ps[:, 2 * u + s, 0:m], rstd[:, a:a + m], ALU.mult)
                ins.then_inc(out_done, 1)
            project("cq", CQ0, KT, ah, al, whi, wlo, SPANS, evac_q, x, "g_cross", (rstd, sq))

        XS = XD ** -0.5
        with ExitStack() as st:
            mkb = sb(st, "mk2", [128, KT, MEM])
            mvb = sb(st, "mv2", [128, 2, D])
            ex = sb(st, "x_exp", [128, 2, MEM])
            xT = sb(st, "x_exp_T", [128, 2, 2, SEQ])
            mxs = sb(st, "x_max", [128, 2])
            nmx = sb(st, "x_neg", [128, 2])
            rs = sb(st, "x_sum", [128, 2])
            ri = sb(st, "x_inv", [128, 2])
            units = [(h, i) for h in range(XH) for i in range(4)]
            mkv_in = sem("mkv_in")
            P = Steps(sem("xp_pe"), ["s00"] + [y for n, (h, i) in enumerate(units) for y in
                      ([f"s{units[n + 1][0]}{units[n + 1][1]}"] if n < 15 else []) + [f"t{h}{i}"]
                      + ([f"o{h}{e}" for e in range(4)] if i == 3 else [])])
            A = Steps(sem("xp_act"), [y for h, i in units for y in [f"e{h}{i}", f"t{h}{i}"] + ([f"o{h}{e}" for e in range(4)] if i == 3 else [])])
            W = Steps(sem("xp_dve"), [f"{y}{h}{i}" for h, i in units for y in ("max", "neg", "inv", "w")])
            with nc.Block() as block:
                @block.sync
                def _(sp):
                    sp.dma_start(mkb[:, :, :], mk_o.rearrange("k p n -> p k n")).then_inc(mkv_in, 16)
                    sp.dma_start(mvb[:, :, :], mv_o.rearrange("m p n -> p m n")).then_inc(mkv_in, 16)

                @block.tensor
                def _(pe):
                    def scores(n):
                        h, i = units[n]
                        if n >= 2:
                            pe.wait_ge(A.sem, A.at("e%d%d" % units[n - 2]))
                        for e in range(4):
                            mm = pe.matmul(ps[:, n % 2, 0:MEM], qc[:, 4 * h + e, i * 128:i * 128 + 128], mkb[:, 4 * h + e, :],
                                           start=(e == 0), stop=(e == 3))
                        mm.then_inc(P.sem, 1)
                    pe.wait_ge(mkv_in, 32)
                    scores(0)
                    for n, (h, i) in enumerate(units):
                        if n < 15:
                            scores(n + 1)
                        pe.wait_ge(W.sem, W.at(f"w{h}{i}"))
                        if n >= 2:
                            pe.wait_ge(A.sem, A.at("t%d%d" % units[n - 2]))
                        for m in range(2):
                            mm = pe.transpose(ps[:, 2 + n % 2, m * 128:m * 128 + 128], ex[:, n % 2, m * 128:m * 128 + 128], C("ident"))
                        mm.then_inc(P.sem, 1)
                        if i == 3:
                            pe.wait_ge(A.sem, A.at(f"t{h}3"))
                            for e in range(4):
                                if h:
                                    pe.wait_ge(A.sem, A.at(f"o{h - 1}{e}"))
                                for m in range(2):
                                    mm = pe.matmul(ps[:, 4 + e, :], mvb[:, m, (4 * h + e) * 128:(4 * h + e) * 128 + 128],
                                                   xT[:, h % 2, m, :], start=(m == 0), stop=(m == 1))
                                mm.then_inc(P.sem, 1)

                @block.scalar
                def _(act):
                    for n, (h, i) in enumerate(units):
                        act.wait_ge(W.sem, W.at(f"neg{h}{i}"))
                        act.activation(ex[:, n % 2, :], ps[:, n % 2, 0:MEM], ACT.Exp, bias=nmx[:, n % 2:n % 2 + 1], scale=XS,
                                       accum_out=rs[:, n % 2:n % 2 + 1]).then_inc(A.sem, 1)
                        act.wait_ge(P.sem, P.at(f"t{h}{i}"))
                        act.activation(xT[:, h % 2, :, i * 128:i * 128 + 128], ps[:, 2 + n % 2, 0:256].rearrange("p (a b) -> p a b", a=2),
                                       ACT.Copy).then_inc(A.sem, 1)
                        if i == 3:
                            for e in range(4):
                                act.wait_ge(P.sem, P.at(f"o{h}{e}"))
                                act.activation(qc[:, 4 * h + e, 0:SEQ], ps[:, 4 + e, :], ACT.Copy).then_inc(A.sem, 1)

                @block.vector
                def _(dve):
                    def did(ins, name):
                        ins.then_inc(W.sem, 1)
                        dve.wait_ge(W.sem, W.at(name))
                    for n, (h, i) in enumerate(units):
                        b = slice(n % 2, n % 2 + 1)
                        dve.wait_ge(P.sem, P.at(f"s{h}{i}"))
                        did(dve.reduce_max(mxs[:, b], ps[:, n % 2, 0:MEM], AX.X), f"max{h}{i}")
                        if n >= 2:
                            dve.wait_ge(P.sem, P.at("t%d%d" % units[n - 2]))
                        did(dve.tensor_scalar(nmx[:, b], mxs[:, b], -XS, None, ALU.mult), f"neg{h}{i}")
                        dve.wait_ge(A.sem, A.at(f"e{h}{i}"))
                        did(dve.reciprocal(ri[:, b], rs[:, b]), f"inv{h}{i}")
                        did(dve.tensor_scalar(ex[:, n % 2, :], ex[:, n % 2, :], ri[:, b], None, ALU.mult), f"w{h}{i}")

        with ExitStack() as st:
            ring = sb(st, "mem_ring", [128, 2, KT * MEM])
            qz = sb(st, "x_q_columns", [128, NS, KT * XH])
            cur = sb(st, "x_standing", [128, 2, KT * XH])
            rows = sb(st, "x_rows_out", [XH, 2, D])
            sc = sb(st, "x_scores", [NS * XH, MEM])
            col = sb(st, "x_softmax_cols", [NS * XH, 4])
            m1, nm, part, inv = [col[:, i:i + 1] for i in range(4)]
            scale_ = sb(st, "x_scale", [NS * XH, NS * XH])
            ws = sb(st, "x_weights", [128, 2, NS * XH])
            oT = sb(st, "x_out_rows", [NS * XH, XD])
            mem_c_in = [sem("mem_c_in0"), sem("mem_c_in1")]
            mem_c_used = sem("mem_c_used")
            cols_out = sem("cols_out")
            cur_in = sem("x_standing_in")
            row_out = sem("x_row_out")
            row_free = sem("x_row_free")
            q_ready = sem("x_q_ready")
            rows_in = sem("x_rows_in")
            with nc.Block() as block:
                @block.tensor
                def _(pe):
                    pe.sem_inc(mem_c_used, 2)

                @block.gpsimd
                def _(pool):
                    pool.sem_inc(row_free, 2)

                @block.vector
                def _(dve):
                    dve.sem_inc(cols_out, 2)
                    dve.memset(qz[:, :, :], 0.0).then_inc(q_ready, 1)
                    dve.wait_ge(q_ready, 1)
                    for h in range(XH):
                        at = 4 * h * XH + h
                        dve.tensor_copy(qz[:, :, at:at + 3 * XH + 1:XH],
                                        qc[:, 4 * h:4 * h + 4, SEQ:TOK].rearrange("p e b -> p b e")).then_inc(q_ready, 1)

            def memory_pass(cache, b0, operands, product, summed, store_to, store_from):
                with nc.Block() as block:
                    @block.sync
                    def _(sp):
                        with sp.Fori(0, NS // 2) as t:
                            for u in range(2):
                                sp.wait_ge(mem_c_used, t * 2 + (b0 + u + 1))
                                sp.dma_start(ring[:, u, :], cache[bass.ds(t * 2 + u, 1), :, :, :].rearrange("o p a b -> p (o a b)"))\
                                  .then_inc(mem_c_in[u], 16)

                    @block.tensor
                    def _(pe):
                        with pe.Fori(0, NS // 2) as t:
                            for u in range(2):
                                pe.wait_ge(cols_out, t * 2 + (b0 + u + 1))
                                pe.wait_ge(cur_in, t * 2 + (b0 + u + 1))
                                pe.wait_ge(mem_c_in[u], t * 16 + (b0 * 8 + 16))
                                product(pe, u).then_inc(mem_c_used, 1)

                    @block.scalar
                    def _(act):
                        with act.Fori(0, NS // 2) as t:
                            for u in range(2):
                                act.wait_ge(mem_c_used, t * 2 + (b0 + u + 1))
                                dst, src = operands(t * 2 + u, u)
                                act.activation(dst, src, ACT.Copy).then_inc(cur_in, 1)

                    @block.vector
                    def _(dve):
                        with dve.Fori(0, NS // 2) as t:
                            for u in range(2):
                                dve.wait_ge(mem_c_used, t * 2 + (b0 + u + 3))
                                dve.wait_ge(row_free, t * 2 + (b0 + u + 1))
                                dve.tensor_copy(store_from(u), summed(u)).then_inc(cols_out, 1)

                    @block.gpsimd
                    def _(pool):
                        with pool.Fori(0, NS // 2) as t:
                            for u in range(2):
                                pool.wait_ge(cols_out, t * 2 + (b0 + u + 3))
                                pool.dma_start(store_to(t * 2 + u), store_from(u)).then_inc(row_out, 16)
                                pool.wait_ge(row_out, t * 32 + 16 * (b0 + u + 1))
                                pool.sem_inc(row_free, 1)

            def score_operands(b, u):
                return cur[:, u, :], qz[:, bass.ds(b, 1), :].rearrange("p o n -> p (o n)")

            def score_product(pe, u):
                for k in range(KT):
                    mm = pe.matmul(ps[0:XH, 4 * u, 0:MEM], cur[:, u, k * XH:k * XH + XH], ring[:, u, k * MEM:(k + 1) * MEM],
                                   start=(k == 0), stop=(k == KT - 1))
                return mm

            memory_pass(mkc, 0, score_operands, score_product, lambda u: ps[0:XH, 4 * u, 0:MEM],
                        lambda b: xsrow[bass.ds(b, 1), :, :].rearrange("o r n -> (o r) n"), lambda u: rows[:, u, 0:MEM])
            S = Steps(sem("xs_soft"), ["m1", "nm", "exp", "inv", "scale", "mm", "ws"])
            with nc.Block() as block:
                @block.sync
                def _(sp):
                    sp.dma_start(sc[:, :], xsrow.rearrange("b r n -> (b r) n")).then_inc(rows_in, 16)

                @block.tensor
                def _(pe):
                    pe.wait_ge(S.sem, S.at("scale"))
                    for m in range(2):
                        mm = pe.matmul(ps[:, 4, m * 32:m * 32 + 32], sc[:, m * 128:m * 128 + 128], scale_[:, :], start=True, stop=True)
                    mm.then_inc(S.sem, 1)

                @block.scalar
                def _(act):
                    act.wait_ge(S.sem, S.at("nm"))
                    act.activation(sc[:, :], sc[:, :], ACT.Exp, bias=nm, scale=XS, accum_out=part).then_inc(S.sem, 1)

                @block.vector
                def _(dve):
                    def did(ins, name):
                        ins.then_inc(S.sem, 1)
                        dve.wait_ge(S.sem, S.at(name))
                    dve.wait_ge(rows_in, 16)
                    did(dve.reduce_max(m1, sc[:, :], AX.X), "m1")
                    did(dve.tensor_scalar(nm, m1, -XS, None, ALU.mult), "nm")
                    dve.wait_ge(S.sem, S.at("exp"))
                    did(dve.reciprocal(inv, part), "inv")
                    did(dve.tensor_scalar(scale_[:, :], C("ident")[0:32, 0:32], inv, None, ALU.mult), "scale")
                    dve.wait_ge(S.sem, S.at("mm"))
                    did(dve.tensor_copy(ws[:, :, :].rearrange("p a b -> p (a b)"), ps[:, 4, 0:64]), "ws")

            def value_operands(b, u):
                return (cur[:, u, 0:2 * XH].rearrange("p (a b) -> p a b", a=2), ws[:, :, bass.ds(b * XH, XH)])

            def value_product(pe, u):
                for m in range(2):
                    for n in range(4):
                        mm = pe.matmul(ps[0:XH, 4 * u + n, :], cur[:, u, m * XH:m * XH + XH],
                                       ring[:, u, m * D + n * 512:m * D + n * 512 + 512], start=(m == 0), stop=(m == 1))
                return mm

            memory_pass(mvc, NS, value_operands, value_product,
                        lambda u: ps[0:XH, 4 * u:4 * u + 4, :].rearrange("p a b -> p (a b)"),
                        lambda b: xorow[bass.ds(b, 1), 0:XH * D].rearrange("o (h n) -> (o h) n", n=D), lambda u: rows[:, u, :])
            own = xorow.rearrange("b (h m) -> (b h) m", m=D + XD)[:, 0:XD]
            with nc.Block() as block:
                @block.sync
                def _(sp):
                    sp.dma_start(oT[:, :], own).then_inc(rows_in, 16)

                @block.tensor
                def _(pe):
                    pe.wait_ge(rows_in, 32)
                    for e in range(4):
                        mm = pe.transpose(ps[:, 4, e * 32:e * 32 + 32], oT[:, e * 128:e * 128 + 128], C("ident")[0:32, 0:32])
                    mm.then_inc(q_ready, 1)

                @block.vector
                def _(dve):
                    dve.wait_ge(q_ready, XH + 2)
                    for e in range(4):
                        dve.tensor_copy(qc[:, e::4, SEQ:TOK].rearrange("p h b -> p b h"),
                                        ps[:, 4, e * 32:e * 32 + 32].rearrange("p (b h) -> p b h", h=XH)).then_inc(q_ready, 1)

        with ExitStack() as st:
            ah = sb(st, "o_hi", [128, KT, TOK], f32r)
            al = sb(st, "o_lo", [128, KT, TOK], f32r)
            whi = sb(st, "whi_e", [128, 2, BLK], f32r)
            wlo = sb(st, "wlo_e", [128, 2, BLK], f32r)
            project("co", CO0, KT, ah, al, whi, wlo, SPANS, add_to_x, qc)
        late.close()

        with ExitStack() as st:
            ah = sb(st, "hf_hi", [128, KT, TOK], f32r)
            al = sb(st, "hf_lo", [128, KT, TOK], f32r)
            whi = sb(st, "whi_f", [128, 2, BLK], f32r)
            wlo = sb(st, "wlo_f", [128, 2, BLK], f32r)
            hh = sb(st, "hid_hi", [128, 4, TOK], f32r)
            hl = sb(st, "hid_lo", [128, 4, TOK], f32r)
            z = sb(st, "gate", [128, 2, TOK])
            sg = sb(st, "sigm", [128, 2, TOK])
            up = sb(st, "up", [128, 2, TOK])
            rstd = sb(st, "rstd_f", [128, TOK])
            sq = sb(st, "sq_f", [128, 2, TOK])
            j0 = jobs[0]
            assert j0 % 2 == 0 and FF0 % 2 == 0
            A = Steps(sem("ff_act"), [f"{y}{n}" for n in range(4) for y in ("sig", "hh")])
            W = Steps(sem("ff_dve"), [f"{y}{n}" for n in range(4) for y in ("z0_", "z1_", "u0_", "u1_", "zs", "hd", "hl")])
            down_done = sem("down_done")
            hi_done, lo_done, sq_done, ssq_done, ms_done, rms_done = [
                sem(f"ff_{y}") for y in ("hi", "lo", "sq", "ssq", "ms", "rms")]

            def at(c, steps, name):
                return c * len(steps.names) + steps.at(name)

            def turns_of(eng, body):
                body(0, True, False)
                with eng.Fori(1, FFC - 1) as c:
                    body(c, False, False)
                body(FFC - 1, False, True)

            with nc.Block() as block:
                @block.sync
                def _(sp):
                    with sp.Fori(0, 6 * FFC - 1) as t:
                        for u in range(2):
                            load_block(sp, t * 2 + (FF0 + u), u)

                @block.scalar
                def _(act):
                    def hi_of(c, i):
                        weight_hi(act, whi, c * 12 + (FF0 + i), i % 2, c * 6 + (FF0 // 2 + i // 2))

                    def body(c, first, last):
                        if first:
                            hi_of(0, 0)
                            for k in range(KT):
                                act.activation(ah[:, k, :], x[:, k, :], ACT.Copy, scale=V("g_ffn", k)).then_inc(hi_done, 1)
                            hi_of(0, 1)
                            for k in range(KT):
                                if k >= 2:
                                    act.wait_ge(ssq_done, k - 1)
                                act.activation(sq[:, k % 2, :], x[:, k, :], ACT.Square).then_inc(sq_done, 1)
                            act.wait_ge(ms_done, 2)
                            act.activation(rstd[:, :], rstd[:, :], ACT.Sqrt).then_inc(rms_done, 1)
                        for i in range(12):
                            if not (last and i >= 10) and i != 7:
                                hi_of(c, i + 2)
                            if i < 8 and i % 2 == 0:
                                n = i // 2
                                act.wait_ge(W.sem, at(c, W, f"z1_{n}"))
                                act.activation(sg[:, n % 2, :], z[:, n % 2, :], ACT.Sigmoid).then_inc(A.sem, 1)
                            elif i < 8:
                                n = i // 2
                                act.wait_ge(W.sem, at(c, W, f"hd{n}"))
                                act.activation(hh[:, n, :], up[:, n % 2, :], ACT.Copy).then_inc(A.sem, 1)
                            if i == 7:
                                hi_of(c, 9)
                    turns_of(act, body)

                @block.vector
                def _(dve):
                    def body(c, first, last):
                        def did(ins, name):
                            ins.then_inc(W.sem, 1)
                            dve.wait_ge(W.sem, at(c, W, name))

                        def lo_of(i):
                            if not (last and i >= 12):
                                weight_lo(dve, whi, wlo, c * 12 + (FF0 + i), i % 2)
                        if first:
                            lo_of(0)
                            for k in range(KT):
                                dve.wait_ge(hi_done, k + 1)
                                dve.scalar_tensor_tensor(al[:, k, :], x[:, k, :], V("g_ffn", k), ah[:, k, :].bitcast(f32),
                                                         ALU.mult, ALU.subtract).then_inc(lo_done, 1)
                            lo_of(1)
                            dve.wait_ge(ssq_done, KT)
                            for i, (a, m) in enumerate(SPANS):
                                dve.tensor_scalar(rstd[:, a:a + m], ps[:, 4 + i, 0:m], 1.0 / D, 1e-6, ALU.mult, ALU.add).then_inc(ms_done, 1)
                            dve.wait_ge(rms_done, 1)
                            dve.reciprocal(rstd[:, :], rstd[:, :]).then_inc(rms_done, 1)
                            dve.wait_ge(rms_done, 2)
                        for i in range(8):
                            n, b = i // 2, (i // 2) % 2
                            dve.wait_ge(pe_done, c * 12 + (FF0 + i + 3))
                            dst = (z, up)[i % 2]
                            for s, (a, m) in enumerate(SPANS):
                                ins = dve.tensor_tensor(dst[:, b, a:a + m], ps[:, 2 * (i % 2) + s, 0:m], rstd[:, a:a + m], ALU.mult)
                                did(ins, f"{'zu'[i % 2]}{s}_{n}")
                            dve.sem_inc(out_done, 1)
                            if i != 7:
                                lo_of(i + 2)
                            if i % 2:
                                dve.wait_ge(A.sem, at(c, A, f"sig{n}"))
                                did(dve.tensor_tensor(z[:, b, :], z[:, b, :], sg[:, b, :], ALU.mult), f"zs{n}")
                                did(dve.tensor_tensor(up[:, b, :], z[:, b, :], up[:, b, :], ALU.mult), f"hd{n}")
                                dve.wait_ge(A.sem, at(c, A, f"hh{n}"))
                                did(dve.tensor_tensor(hl[:, n, :], up[:, b, :], hh[:, n, :].bitcast(f32), ALU.subtract), f"hl{n}")
                            if i == 7:
                                lo_of(9)
                        for q in range(4):
                            for m_ in range(4):
                                if m_ < 3:
                                    dve.wait_ge(down_done, c * 12 + (3 * q + m_ + 1))
                                else:
                                    dve.wait_ge(pe_done, c * 12 + (FF0 + 8 + q + 3))
                                for s, (a, m) in enumerate(SPANS):
                                    xi = x[:, 4 * q + m_, a:a + m]
                                    ins = dve.tensor_tensor(xi, ps[:, 2 * (m_ % 2) + s, 0:m], xi, ALU.add)
                                ins.then_inc(out_done, 1)
                            lo_of(10 + q)
                    turns_of(dve, body)

                @block.tensor
                def _(pe):
                    def product(k, kcol, u, wslot, th, tl, first, last):
                        for wt, t in ((whi, th), (whi, tl), (wlo, th)):
                            for s, (a, m) in enumerate(SPANS):
                                mm = pe.matmul(ps[:, 2 * u + s, 0:m], wt[:, wslot, kcol:kcol + 128], t[:, k, a:a + m],
                                               start=(first and wt is whi and t is th), stop=(last and wt is wlo))
                        return mm

                    def body(c, first, last):
                        for i in range(8):
                            pe.wait_ge(wlo_done, c * 12 + (FF0 + i + 1))
                            pe.wait_ge(out_done, c * 24 + (j0 + i + 1))
                            for k in range(KT):
                                if first and i == 0:
                                    pe.wait_ge(lo_done, k + 1)
                                mm = product(k, k * 128, i % 2, i % 2, ah, al, k == 0, k == KT - 1)
                            mm.then_inc(pe_done, 1)
                            if first and i == 0:
                                for k in range(KT):
                                    pe.wait_ge(sq_done, k + 1)
                                    for s, (a, m) in enumerate(SPANS):
                                        mm = pe.matmul(ps[:, 4 + s, 0:m], C("ones"), sq[:, k % 2, a:a + m], start=(k == 0), stop=(k == KT - 1))
                                    mm.then_inc(ssq_done, 1)
                        for q in range(4):
                            pe.wait_ge(wlo_done, c * 12 + (FF0 + 8 + q + 1))
                            for m_ in range(4):
                                pe.wait_ge(out_done, c * 24 + (j0 + 8 + 4 * q + m_ + 1))
                                for k in range(4):
                                    if q == 0 and m_ == 0:
                                        pe.wait_ge(W.sem, at(c, W, f"hl{k}"))
                                    mm = product(k, (m_ * 4 + k) * 128, m_ % 2, q % 2, hh, hl, k == 0, k == 3)
                                mm.then_inc(down_done if m_ < 3 else pe_done, 1)
                    turns_of(pe, body)

        with ExitStack() as st:
            sq = sb(st, "sq_g", [128, 2, TOK])
            rstd = sb(st, "rstd_g", [128, TOK])
            fin = sem("fin_act")
            fin_pe, fin_dve, fin_out = sem("fin_pe"), sem("fin_dve"), sem("fin_out")
            with nc.Block() as block:
                @block.scalar
                def _(act):
                    for k in range(KT):
                        if k >= 2:
                            act.wait_ge(fin_pe, k - 1)
                        act.activation(sq[:, k % 2, :], x[:, k, :], ACT.Square).then_inc(fin, 1)
                    act.wait_ge(fin_dve, 2)
                    act.activation(rstd[:, :], rstd[:, :], ACT.Sqrt).then_inc(fin, 1)

                @block.tensor
                def _(pe):
                    for k in range(KT):
                        pe.wait_ge(fin, k + 1)
                        for s, (a, m) in enumerate(SPANS):
                            mm = pe.matmul(ps[:, 4 + s, 0:m], C("ones"), sq[:, k % 2, a:a + m], start=(k == 0), stop=(k == KT - 1))
                        mm.then_inc(fin_pe, 1)

                @block.vector
                def _(dve):
                    dve.wait_ge(fin_pe, KT)
                    for s, (a, m) in enumerate(SPANS):
                        dve.tensor_scalar(rstd[:, a:a + m], ps[:, 4 + s, 0:m], 1.0 / D, 1e-6, ALU.mult, ALU.add).then_inc(fin_dve, 1)
                    dve.wait_ge(fin, KT + 1)
                    dve.reciprocal(rstd[:, :], rstd[:, :]).then_inc(fin_dve, 1)
                    dve.wait_ge(fin_dve, 3)
                    for k in range(KT):
                        dve.scalar_tensor_tensor(x[:, k, :], x[:, k, :], V("g_final", k), rstd[:, :], ALU.mult, ALU.mult).then_inc(fin_dve, 1)

                @block.sync
                def _(sp):
                    for k in range(KT):
                        sp.wait_ge(fin_dve, 4 + k)
                        sp.dma_start(yo[k, :, :], x[:, k, :]).then_inc(fin_out, 16)
                    sp.wait_ge(fin_out, 16 * KT)




def blocks16(wt):
    n = wt.shape[1]
    return wt.reshape(KT, 128, n // 128, 128).transpose(2, 1, 0, 3).reshape(n // 128, 128, BLK)


def prepare(i):
    a = {k: np.asarray(v) for k, v in i.items()}
    w_in = a["w_in"][0]
    cv = a["w_cv"][0].reshape(4, 4, 128, 4, 512).transpose(3, 0, 2, 1, 4).reshape(16, 128, BLK)
    gate, up = blocks16(a["w_gate"][0]), blocks16(a["w_up"][0])
    down = a["w_down"][0].reshape(FFC, 4, 128, 4, 4, 128).transpose(0, 3, 2, 4, 1, 5).reshape(FFC, 4, 128, BLK)
    gu = np.stack([gate, up], 1).reshape(FFC, 8, 128, BLK)
    w = np.concatenate([blocks16(w_in[:, RW_PROJ:]), blocks16(w_in[:, :RW_PROJ]), blocks16(a["w_ck"][0]), cv,
                        blocks16(a["w_o"][0]), blocks16(a["w_cq"][0]), blocks16(a["w_co"][0]),
                        np.concatenate([gu, down], 1).reshape(12 * FFC, 128, BLK)])

    def feat(v):
        return np.asarray(v).reshape(-1, 128).T
    vec = np.concatenate([feat(a["norm_mix_g"][0]), feat(a["norm_mem_g"][0]), feat(a["norm_cross_g"][0]),
                          feat(a["norm_ffn_g"][0]), feat(a["final_norm_g"]), feat(a["tok_shift_mu"][0]),
                          feat(a["rwkv_w0"][0]), feat(a["rwkv_a0"][0]), feat(a["rwkv_k_k"][0]), feat(a["rwkv_k_a"][0]),
                          feat(a["rwkv_r_k"][0]), feat(a["rwkv_lnx_g"][0]), feat(a["rwkv_lnx_b"][0]),
                          feat(a["diff_subln_g"][0]),
                          np.concatenate([a["diff_lq1"][0], a["diff_lq2"][0]])[:, None],
                          np.concatenate([a["diff_lk1"][0], a["diff_lk2"][0]])[:, None],
                          a["state_shift"][0].reshape(NS, PROJ_T, 128).transpose(2, 1, 0).reshape(128, PROJ_T * NS)], 1)
    x = np.concatenate([a["x_prompt"][0], a["x_sample"][:, 0]])
    npool = a["cache_k"].shape[1]
    return {
        "w": w, "vec": vec, "con": shape_constants(),
        "xt": x.T.reshape(KT, 128, TOK),
        "memt": a["mem_prompt"][0].T.reshape(KT, 128, MEM),
        "kc": a["cache_k"][0].transpose(0, 3, 2, 1),
        "vc": a["cache_v"][0],
        "mkc": a["cache_mem_k"][0].reshape(NS, MEM, 16, 128).transpose(0, 3, 2, 1),
        "mvc": a["cache_mem_v"][0].reshape(NS, 2, 128, D).transpose(0, 2, 1, 3),
        "s0": a["state_wkv"][0].reshape(NS, RT, 2, 64, 64).transpose(2, 1, 0, 3, 4).reshape(128, 64, 64),
        "pages": a["page_table"].reshape(1, -1),
        "w2a2": np.concatenate([a["rwkv_w2"][0], a["rwkv_a2"][0]]),
        "g2": a["rwkv_g2"][0],
    }


OUTS = {"qkv": (24, 128, TOK), "yo": (KT, 128, TOK), "wkv_p": (128, RT, 64), "wkv_s": (128, 64, 64),
        "shift": (128, PROJ_T, 1 + NS), "mk_o": (KT, 128, MEM), "mv_o": (2, 128, D)}


def build(nc, shapes, upto=99):
    args = {n: nc.dram_tensor(n, s, i32 if n == "pages" else f32, kind="ExternalInput").ap() for n, s in shapes.items()}
    args |= {n: nc.dram_tensor(n, s, f32, kind="ExternalOutput").ap() for n, s in OUTS.items()}
    args["ymix"] = nc.dram_tensor("ymix", (KT, 128, TOK), f32, kind="ExternalOutput" if upto < 99 else "Internal").ap()
    for n, s in {"srow": (NS, 2 * DA_HEADS, PAST), "orow": (NS, DA_HEADS * (RW + 128)), "xsrow": (NS, XH, MEM),
                 "xorow": (NS, XH * (D + XD))}.items():
        args[n] = nc.dram_tensor(n, s, f32, kind="Internal").ap()
    decoder_kernel(nc, **args, upto=upto)


def kernel(**inputs):
    import concourse.bacc as bacc
    from concourse.bass_utils import run_bass_kernel_spmd
    arrays = {n: np.ascontiguousarray(v) for n, v in prepare(inputs).items()}
    nc = bacc.Bacc("TRN2", target_bir_lowering=False, num_devices=1)
    build(nc, {n: v.shape for n, v in arrays.items()})
    r = run_bass_kernel_spmd(nc, [arrays], core_ids=[0]).results[0]
    r = {n: np.asarray(r[n]) for n in OUTS}
    y = r["yo"].reshape(D, TOK).T
    k = r["qkv"][8:16].reshape(RW, TOK).T
    v = r["qkv"][16:24].reshape(RW, TOK).T
    sh = r["shift"].transpose(2, 1, 0).reshape(1 + NS, RW_PROJ)
    wp = r["wkv_p"].reshape(2, 64, RT, 64).transpose(2, 0, 3, 1).reshape(1, 1, 2 * RT, 64, 64)
    ws = r["wkv_s"].reshape(2, RT, NS, 64, 64).transpose(2, 1, 0, 3, 4).reshape(1, NS, 2 * RT, 64, 64)
    c = np.ascontiguousarray
    return (c(y[None, :SEQ]), c(y[SEQ:, None]), c(k[:SEQ].reshape(1, 1, SEQ, 8, 128)), c(v[:SEQ].reshape(1, 1, SEQ, 8, 128)),
            c(k[SEQ:].reshape(1, NS, 1, 8, 128)), c(v[SEQ:].reshape(1, NS, 1, 8, 128)), c(wp), c(ws),
            c(sh[None, :1]), c(sh[None, 1:]),
            c(r["mk_o"].reshape(D, MEM).T.reshape(1, 1, MEM, XH, XD)), c(r["mv_o"].reshape(1, 1, MEM, XH, XD)))
```

```python
import math
from contextlib import ExitStack

import numpy as np
import concourse.bass as bass
from concourse import mybir

D = 2048
SEQ = 512
NS = 8
TOK = SEQ + NS
HALF = TOK // 2
PAST, PAGE = 2048, 128
PAGES = PAST // PAGE
RW = D // 2
RW_PROJ = 3 * RW + 256
DA_HEADS = 8
MEM = 256
XH, XD = 4, 512
D_FF = ((8 * D + 767) // 768) * 256
KT = D // 128
RT = RW // 128
PROJ_T = RW_PROJ // 128
CH = 64
NCH = SEQ // CH
FFC = D_FF // 512
LAM_INIT = 0.8 - 0.6 * math.exp(-0.3 * 0)
DECAY = math.exp(-0.5)
BLK = 2048

QKV0 = 0
RWK0 = QKV0 + 24
CK0 = RWK0 + PROJ_T
CV0 = CK0 + KT
WO0 = CV0 + KT
CQ0 = WO0 + KT
CO0 = CQ0 + KT
FF0 = CO0 + KT
NBLK = FF0 + 12 * FFC

_cols = [("g_mix", KT), ("g_mem", KT), ("g_cross", KT), ("g_ffn", KT), ("g_final", KT), ("mu", PROJ_T),
         ("w0", RT), ("a0", RT), ("k_k", RT), ("k_a", RT), ("r_k", RT), ("lnx_g", RT), ("lnx_b", RT),
         ("subln", 1), ("lam_q", 1), ("lam_k", 1), ("shift", PROJ_T * NS)]
VEC = {}
_at = 0
for _n, _w in _cols:
    VEC[_n] = _at
    _at += _w
NVEC = _at
_cols = [("ident", 128), ("ones", 128), ("pair", 128), ("halves", 256), ("causal", 128), ("gram", 128),
         ("diag", CH), ("diag_t", CH), ("off_t", CH), ("start", TOK), ("two", 2), ("map0", 64), ("map1", 64)]
CON = {}
_at = 0
for _n, _w in _cols:
    CON[_n] = (_at, _at + _w)
    _at += _w
NCON = _at

f32 = mybir.dt.float32
f32r = mybir.dt.float32r
i32 = mybir.dt.int32
ALU = mybir.AluOpType
ACT = mybir.ActivationFunctionType
AX = mybir.AxisListType
SPANS = [(0, HALF), (HALF, HALF)]


def shape_constants():
    c = np.zeros((128, NCON), np.float32)

    def put(name, a):
        c[:, CON[name][0]:CON[name][1]] = a
    p = np.arange(128)[:, None]
    q = np.arange(128)[None, :]
    put("ident", p == q)
    put("ones", 1.0)
    put("pair", p // 64 == q // 64)
    put("halves", np.concatenate([np.broadcast_to(p < 64, (128, 128)), np.broadcast_to(p >= 64, (128, 128))], 1))
    put("causal", np.where(q <= p, 0.0, -1e30))
    s, t = p % 64, q % 64
    put("gram", np.where(q < 64, s < t, s <= t))
    s, t = p % 64, np.arange(64)[None, :]
    put("diag", (s < t) & (s // 8 == t // 8))
    put("diag_t", (t < s) & (s // 8 == t // 8))
    put("off_t", (t < s) & (s // 8 != t // 8))
    put("start", (np.arange(TOK) % CH != 0) & (np.arange(TOK) < SEQ))
    row, col = np.arange(128)[:, None], np.arange(64)[None, :]
    put("map0", row == 2 * col)
    put("map1", row == 2 * col + 1)
    put("two", np.concatenate([p < 64, p >= 64], 1))
    return c


class Steps:

    def __init__(self, sem, names):
        self.sem, self.names = sem, list(names)
        assert len(set(self.names)) == len(self.names)

    def at(self, name, turn=0):
        return turn * len(self.names) + self.names.index(name) + 1


def decoder_kernel(nc, w, vec, con, xt, memt, kc, vc, mkc, mvc, s0, pages, w2a2, g2,
                   qkv, yo, wkv_p, wkv_s, shift, mk_o, mv_o, ymix,
                   srow, orow, xsrow, xorow):
    stack = ExitStack()
    nsem = [0]

    def sem(name):
        nsem[0] += 1
        return stack.enter_context(nc.semaphore(name))

    def sb(st, name, shape, dt=f32):
        return st.enter_context(nc.sbuf_tensor(name, shape, dt))

    with stack:
        vt = sb(stack, "vt", [128, NVEC])
        cn = sb(stack, "cn", [128, NCON])
        lam = sb(stack, "lam", [128, 4])
        raw = sb(stack, "raw", [128, 2, BLK])
        ps = stack.enter_context(nc.psum_tensor("ps", [128, 8, 512], f32))
        bank = [ps[:, i, :] for i in range(8)]

        def C(name):
            return cn[:, CON[name][0]:CON[name][1]]

        def V(name, k=0):
            return vt[:, VEC[name] + k:VEC[name] + k + 1]

        const_in = sem("const_in")
        raw_in = [sem("raw_in0"), sem("raw_in1")]
        whi_done = sem("whi_done")
        wlo_done = sem("wlo_done")
        pe_done = sem("pe_done")
        out_done = sem("out_done")

        with nc.Block() as block:
            @block.sync
            def _(sp):
                sp.dma_start(vt[:, :], vec).then_inc(const_in, 16)
                sp.dma_start(cn[:, :], con).then_inc(const_in, 16)
                sp.dma_start(raw[:, 0, :], w[0, :, :]).then_inc(raw_in[0], 16)
                sp.wait_ge(const_in, 32)

            @block.tensor
            def _(pe):
                pe.sem_inc(pe_done, 2)

            @block.vector
            def _(dve):
                dve.sem_inc(out_done, 2)

        def load_block(sp, g, u, ahead=2):
            sp.wait_ge(wlo_done, g + 1)
            src = w[g + ahead, :, :] if isinstance(g, int) else w[bass.ds(g + ahead, 1), :, :].rearrange("o p n -> p (o n)")
            sp.dma_start(raw[:, u, :], src).then_inc(raw_in[u], 16)

        def weight_hi(act, whi, g, u, turn):
            act.wait_ge(raw_in[u], turn * 16 + 16)
            act.wait_ge(pe_done, g + 1)
            act.activation(whi[:, u, :], raw[:, u, :], ACT.Copy).then_inc(whi_done, 1)

        def weight_lo(dve, whi, wlo, g, u):
            dve.wait_ge(whi_done, g + 1)
            dve.tensor_tensor(wlo[:, u, :], raw[:, u, :], whi[:, u, :].bitcast(f32),
                              ALU.subtract).then_inc(wlo_done, 1)

        def inverse_root(act, t, done, before):
            act.activation(t, t, ACT.Ln).then_inc(done, 1)
            act.wait_ge(done, before + 1)
            act.activation(t, t, ACT.Exp, scale=-0.5).then_inc(done, 1)

        jobs = [0]

        def project(name, g0, n, ah, al, whi, wlo, spans, evac, src=None, gain=None, stat=None, extra=None, src_in=None):
            j0 = jobs[0]
            jobs[0] += n
            assert g0 % 2 == 0 and n % 2 == 0 and j0 % 2 == 0
            h0 = g0 // 2
            T = spans[-1][0] + spans[-1][1]
            hi_done, lo_done, sq_done, ssq_done, ms_done, rms_done = (
                [sem(f"{name}_{x}") for x in ("hi", "lo", "sq", "ssq", "ms", "rms")] if src is not None else [None] * 6)
            scale = (lambda k: V(gain, k)) if gain else (lambda k: 1.0)

            def block_product(pe, g, j, u, first=False):
                pe.wait_ge(wlo_done, g + 1)
                pe.wait_ge(out_done, j + 1)
                for k in range(KT):
                    if first:
                        pe.wait_ge(lo_done, k + 1)
                    ks = slice(k * 128, k * 128 + 128)
                    for wt, at in ((whi, ah), (whi, al), (wlo, ah)):
                        for i, (a, m) in enumerate(spans):
                            mm = pe.matmul(bank[2 * u + i][:, 0:m], wt[:, u, ks], at[:, k, a:a + m],
                                           start=(k == 0 and wt is whi and at is ah),
                                           stop=(k == KT - 1 and wt is wlo))
                mm.then_inc(pe_done, 1)

            with nc.Block() as block:
                @block.sync
                def _(sp):
                    if g0 + n == NBLK:
                        with sp.Fori(0, n // 2 - 1) as t:
                            for u in range(2):
                                load_block(sp, t * 2 + (g0 + u), u)
                    else:
                        with sp.Fori(0, n // 2) as t:
                            for u in range(2):
                                load_block(sp, t * 2 + (g0 + u), u)

                @block.scalar
                def _(act):
                    for u in range(2):
                        weight_hi(act, whi, g0 + u, u, h0)
                        if u == 0 and src is not None:
                            for k in range(KT):
                                if src_in and k % 4 == 0:
                                    act.wait_ge(src_in[k // 4], 16)
                                act.activation(ah[:, k, :], src[:, k, :], ACT.Copy, scale=scale(k)).then_inc(hi_done, 1)
                    if stat:
                        rstd, sq = stat
                        for k in range(KT):
                            if k >= 2:
                                act.wait_ge(ssq_done, k - 1)
                            act.activation(sq[:, k % 2, 0:T], src[:, k, :], ACT.Square).then_inc(sq_done, 1)
                        act.wait_ge(ms_done, len(spans))
                        inverse_root(act, rstd[:, 0:T], rms_done, 0)
                    with act.Fori(1, n // 2) as t:
                        for u in range(2):
                            weight_hi(act, whi, t * 2 + (g0 + u), u, t + h0)

                @block.vector
                def _(dve):
                    for u in range(2):
                        weight_lo(dve, whi, wlo, g0 + u, u)
                        if u == 0 and src is not None:
                            for k in range(KT):
                                dve.wait_ge(hi_done, k + 1)
                                dve.scalar_tensor_tensor(al[:, k, :], src[:, k, :], scale(k), ah[:, k, :].bitcast(f32),
                                                         ALU.mult, ALU.subtract).then_inc(lo_done, 1)
                    if stat:
                        rstd, sq = stat
                        dve.wait_ge(ssq_done, KT)
                        for i, (a, m) in enumerate(spans):
                            dve.tensor_scalar(rstd[:, a:a + m], bank[4 + i][:, 0:m], 1.0 / D, 1e-6,
                                              ALU.mult, ALU.add).then_inc(ms_done, 1)
                        dve.wait_ge(rms_done, 2)
                    with dve.Fori(0, n // 2 - 1) as t:
                        for u in range(2):
                            dve.wait_ge(pe_done, t * 2 + (g0 + u + 3))
                            evac(dve, t * 2 + u, u, t)
                            weight_lo(dve, whi, wlo, t * 2 + (g0 + u + 2), u)
                    for u in range(2):
                        dve.wait_ge(pe_done, g0 + n + u + 1)
                        evac(dve, n - 2 + u, u, n // 2 - 1)

                @block.tensor
                def _(pe):
                    for u in range(2):
                        block_product(pe, g0 + u, j0 + u, u, first=(u == 0 and src is not None))
                        if u == 0 and stat:
                            for k in range(KT):
                                pe.wait_ge(sq_done, k + 1)
                                for i, (a, m) in enumerate(spans):
                                    mm = pe.matmul(bank[4 + i][:, 0:m], C("ones"), stat[1][:, k % 2, a:a + m],
                                                   start=(k == 0), stop=(k == KT - 1))
                                mm.then_inc(ssq_done, 1)
                    with pe.Fori(1, n // 2) as t:
                        for u in range(2):
                            block_product(pe, t * 2 + (g0 + u), t * 2 + (j0 + u), u)

                if extra:
                    extra(block)

        def tile_of(t, i):
            if isinstance(i, int):
                return t[:, i, :]
            return t[:, bass.ds(i, 1), :].rearrange("p o n -> p (o n)")

        def dram_tile(t, i):
            if isinstance(i, int):
                return t[i, :, :]
            return t[bass.ds(i, 1), :, :].rearrange("o p n -> p (o n)")

        with ExitStack() as mixing:
            rkv = sb(mixing, "rkv", [128, PROJ_T, TOK])
            with ExitStack() as st:
                ah = sb(st, "h_hi", [128, KT, TOK], f32r)
                al = sb(st, "h_lo", [128, KT, TOK], f32r)
                rstd = sb(st, "rstd_mix", [128, TOK])
                with ExitStack() as s2:
                    whi = sb(s2, "whi_a", [128, 2, BLK], f32r)
                    wlo = sb(s2, "wlo_a", [128, 2, BLK], f32r)
                    sq = sb(s2, "sq_a", [128, 2, TOK])
                    ev = sb(s2, "ev_a", [128, 2, TOK])
                    ev_out = sem("ev_out")
                    ev_free = sem("ev_free")
                    x_in = [sem(f"x_in{i}") for i in range(4)]
                    x = rkv[:, 0:KT, :]

                    with nc.Block() as block:
                        @block.sync
                        def _(sp):
                            for k in range(0, KT, 4):
                                sp.dma_start(x[:, k:k + 4, :], xt[k:k + 4, :, :].rearrange("k p n -> p k n")).then_inc(x_in[k // 4], 16)
                            sp.dma_start(raw[:, 1, :], w[1, :, :]).then_inc(raw_in[1], 16)

                        @block.gpsimd
                        def _(pool):
                            pool.sem_inc(ev_free, 2)

                    def evac_qkv(dve, i, u, t):
                        dve.wait_ge(ev_free, i + 1)
                        for s, (a, m) in enumerate(SPANS):
                            ins = dve.tensor_tensor(ev[:, u, a:a + m], bank[2 * u + s][:, 0:m], rstd[:, a:a + m], ALU.mult)
                        ins.then_inc(out_done, 1)

                    def store_qkv(block):
                        @block.gpsimd
                        def _(pool):
                            with pool.Fori(0, 12) as t:
                                for u in range(2):
                                    pool.wait_ge(out_done, t * 2 + (u + 3))
                                    pool.dma_start(dram_tile(qkv, t * 2 + u), ev[:, u, :]).then_inc(ev_out, 16)
                                    pool.wait_ge(ev_out, t * 32 + 16 * (u + 1))
                                    pool.sem_inc(ev_free, 1)

                    project("qkv", QKV0, 24, ah, al, whi, wlo, SPANS, evac_qkv, x, "g_mix", (rstd, sq), store_qkv, x_in)

                    p = sb(s2, "p_row", [128, 1 + TOK])
                    dif = sb(s2, "p_dif", [128, TOK])
                    last = sb(s2, "p_last", [128, PROJ_T, 1 + NS])
                    sh = Steps(sem("shift_steps"), ["p0", "p1", "dif", "dif_s", "last", "ps"])
                    sh_out = sem("sh_out")

                    with nc.Block() as block:
                        @block.vector
                        def _(dve):
                            dve.memset(p[:, 0:1], 0.0).then_inc(sh_out, 1)
                            dve.wait_ge(sh_out, 1)

                    def evac_shift(dve, i, u, t):
                        for s, (a, m) in enumerate(SPANS):
                            dve.tensor_tensor(p[:, 1 + a:1 + a + m], bank[2 * u + s][:, 0:m], rstd[:, a:a + m],
                                              ALU.mult).then_inc(sh.sem, 1)
                        dve.wait_ge(sh.sem, i * 6 + 2)
                        dve.tensor_tensor(dif[:, 0:SEQ], p[:, 0:SEQ], p[:, 1:1 + SEQ], ALU.subtract).then_inc(sh.sem, 1)
                        prev = vt[:, bass.ds(VEC["shift"] + i * NS, NS)]
                        dve.tensor_tensor(dif[:, SEQ:TOK], prev, p[:, 1 + SEQ:1 + TOK], ALU.subtract).then_inc(sh.sem, 1)
                        dve.tensor_copy(tile_of(last, i), p[:, SEQ:1 + TOK]).then_inc(sh.sem, 1)
                        dve.wait_ge(sh.sem, i * 6 + 4)
                        dve.scalar_tensor_tensor(tile_of(rkv, i), dif[:, :], vt[:, bass.ds(VEC["mu"] + i, 1)], p[:, 1:1 + TOK],
                                                 ALU.mult, ALU.add).then_inc(sh.sem, 1)
                        dve.wait_ge(sh.sem, i * 6 + 6)
                        dve.sem_inc(out_done, 1)

                    project("rwkv", RWK0, PROJ_T, ah, al, whi, wlo, SPANS, evac_shift)

                    with nc.Block() as block:
                        @block.sync
                        def _(sp):
                            sp.dma_start(shift, last[:, :, :]).then_inc(sh_out, 16)
                            sp.wait_ge(sh_out, 17)


            attn = ExitStack()
            yd = sb(attn, "yd", [128, DA_HEADS, TOK])
            ready = Steps(sem("lam_steps"), ["prod", "rhs", "sum", "exp", "lam", "neg", "g"])
            lam_e = lam[:, 0:2]
            neg_lam = lam[:, 2:3]
            sub_g = lam[:, 3:4]
            samples = ExitStack()
            HC = 2 * DA_HEADS
            SLOTS, SPLITS = 4, 4
            tab = sb(samples, "page_ids", [1, NS * PAGES], i32)
            qs = sb(samples, "qkv_s", [128, 24, NS])
            qbd = sb(samples, "q_blocks", [128, NS, DA_HEADS, 2])
            qz = sb(samples, "q_columns", [128, NS, DA_HEADS * HC])
            ring = sb(samples, "page_ring", [128, SLOTS, RW])
            split = sb(samples, "page_split", [128, SPLITS, 2, RW], f32r)
            cur = sb(samples, "page_standing", [128, 2, 256], f32r)
            rows = sb(samples, "rows_out", [128, 2, PAST])
            prod = sb(samples, "qk_new", [128, NS, DA_HEADS, 2])
            col = sb(samples, "softmax_cols", [128, 8])
            snew, m1, nm, part, enew, inv = [col[:, i:i + 1] for i in range(6)]
            comb = sb(samples, "combine", [128, 64])
            comb_n = sb(samples, "combine_new", [128, 64])
            ov = sb(samples, "new_v", [128, NS, DA_HEADS])
            samp_in = sem("samp_in")
            q_ready = sem("q_blocks_ready")
            cur_in = sem("page_standing_in")
            page_in = [sem(f"page_in{i}") for i in range(SLOTS)]
            page_hi = sem("page_hi")
            page_lo = sem("page_lo")
            page_used = sem("page_used")
            cur_hi = sem("page_standing_hi")
            half_out = sem("half_out")
            group_out = sem("group_out")
            sums_out = sem("sums_out")
            row_out = sem("row_out")
            row_free = sem("row_free")

            with nc.Block() as block:
                @block.sync
                def _(sp):
                    sp.dma_start(tab[:, :], pages).then_inc(samp_in, 16)
                    sp.dma_start(qs[:, :, :], qkv[:, :, SEQ:TOK].rearrange("k p n -> p k n")).then_inc(samp_in, 16)
                    sp.wait_ge(samp_in, 32)

                @block.tensor
                def _(pe):
                    pe.sem_inc(page_used, SPLITS)

                @block.gpsimd
                def _(pool):
                    pool.sem_inc(row_free, 2)

                @block.vector
                def _(dve):
                    dve.sem_inc(sums_out, 2)
                    dve.sem_inc(group_out, 1)
                    dve.sem_inc(page_lo, SLOTS)
                    dve.memset(qz[:, :, :], 0.0).then_inc(q_ready, 1)
                    dve.memset(qbd[:, :, :, :], 0.0).then_inc(q_ready, 1)
                    dve.wait_ge(samp_in, 32)
                    dve.wait_ge(q_ready, 2)
                    for c in range(2):
                        half = slice(64 * c, 64 * c + 64)
                        q = qs[half, 0:8, :].rearrange("p h b -> p b h")
                        dve.tensor_copy(qbd[half, :, :, c], q).then_inc(q_ready, 1)
                        dve.tensor_copy(qz[half, :, c::HC + 2], q).then_inc(q_ready, 1)
                    dve.wait_ge(q_ready, 6)
                    k = qs[:, 8:16, :].rearrange("p h b -> p b h").unsqueeze(3).to_broadcast([128, NS, DA_HEADS, 2])
                    dve.tensor_tensor(prod[:, :, :, :], qbd[:, :, :, :], k, ALU.mult).then_inc(q_ready, 1)

            def load_pages(sp, cache, t, bb, g0, places, landed):
                slots = len(places)
                for pg in range(PAGES):
                    n = t * 32 + (bb * PAGES + pg)
                    sp.wait_ge(page_lo, n + (g0 + 1 + SLOTS - slots))
                    page = sp.value_load(tab[0:1, bass.ds(n, 1)], min_val=0, max_val=cache.shape[0] - 1)
                    src = cache[bass.ds(page, 1), :, :, :].rearrange("o p a b -> p (o a b)")
                    sp.dma_start(places[pg % slots], src).then_inc(landed[pg % slots], 16)

            k_places = [ring[:, i, :] for i in range(SLOTS)]

            def operands_of(queries):
                return lambda b, bb: (cur[:, bb, :].rearrange("p (g s n) -> p g s n", g=DA_HEADS, s=2),
                                      queries[:, bass.ds(b, 1), :].rearrange("p o (g n) -> p (o g) n", g=DA_HEADS))
            k_operands = operands_of(qz)

            def k_parts(bb, i):
                return (ps[0:2 * HC, 5:7, :].rearrange("p a (b s n) -> p a b s n", b=2, s=2),
                        rows[0:2 * HC, bb, 512 * i:512 * i + 512].rearrange("p (a b n) -> p a b n", a=2, b=2))

            with ExitStack() as st:
                tmp = sb(st, "lam_tmp", [128, 4])
                qh = sb(st, "qkv_head", [128, 2, 3, TOK])
                vtok = sb(st, "v_tok", [128, 2, 4, 128])
                ex = sb(st, "exps", [128, 2, 2, SEQ])
                wt_ = sb(st, "weights", [128, 2, SEQ])
                wT = sb(st, "weights_T", [128, 2, 4, 128])
                mx = sb(st, "row_max", [128, 2, 2])
                nmx = sb(st, "neg_max", [128, 2, 2])
                rs = sb(st, "row_sum", [128, 2, 2])
                ri = sb(st, "row_inv", [128, 2, 2])
                heads_in = [sem("head_in0"), sem("head_in1")]
                act_start = sem("turn_start")
                head_ok = sem("head_ok")
                by_head = qkv.rearrange("(c h) p n -> h p c n", c=3)

                def head_rows(h):
                    return by_head[bass.ds(h, 1), :, :, :].rearrange("o p c n -> p (o c) n")
                turns = [(hh, i) for hh in range(2) for i in range(4)]
                P = Steps(sem("att_pe"), [x for hh in range(2) for x in
                                          [f"vt{hh}", f"s{hh}0"] + [y for i in range(4) for y in
                                           ([f"s{hh}{i + 1}"] if i < 3 else []) + [f"t{hh}{i}", f"o{hh}{i}"]]])
                A = Steps(sem("att_act"), [x for hh in range(2) for x in [f"vt{hh}"] + [y for i in range(4) for y in
                                           (f"e{hh}{i}0", f"e{hh}{i}1", f"t{hh}{i}")] + [f"o{hh}"]])
                V_ = Steps(sem("att_dve"), [f"{y}{hh}{i}" for hh, i in turns for y in
                                            ("mask", "max", "neg", "inv", "invl", "w0_", "w1_")])
                with nc.Block() as block:
                    @block.vector
                    def _(dve):
                        dve.tensor_tensor(tmp[:, 0:1], V("lam_q"), V("lam_k"), ALU.mult).then_inc(ready.sem, 1)
                        dve.wait_ge(ready.sem, ready.at("prod"))
                        dve.tensor_scalar(tmp[:, 1:3], C("two"), tmp[:, 0:1], None, ALU.mult).then_inc(ready.sem, 1)
                        dve.wait_ge(ready.sem, ready.at("exp"))
                        dve.scalar_tensor_tensor(tmp[:, 3:4], lam_e[:, 0:1], LAM_INIT, lam_e[:, 1:2], ALU.add,
                                                 ALU.subtract).then_inc(ready.sem, 1)
                        dve.wait_ge(ready.sem, ready.at("lam"))
                        dve.tensor_scalar(neg_lam, tmp[:, 3:4], -1.0, None, ALU.mult).then_inc(ready.sem, 1)
                        dve.tensor_scalar(sub_g, V("subln"), 1.0 - LAM_INIT, None, ALU.mult).then_inc(ready.sem, 1)
                        dve.wait_ge(ready.sem, ready.at("g"))

                    @block.tensor
                    def _(pe):
                        pe.wait_ge(ready.sem, ready.at("rhs"))
                        pe.matmul(ps[:, 7, 0:2], C("ones"), tmp[:, 1:3], start=True, stop=True).then_inc(ready.sem, 1)

                    @block.scalar
                    def _(act):
                        act.wait_ge(ready.sem, ready.at("sum"))
                        act.activation(lam_e, ps[:, 7, 0:2], ACT.Exp).then_inc(ready.sem, 1)

                    @block.sync
                    def _(sp):
                        for u in range(2):
                            sp.dma_start(qh[:, u, :, :], head_rows(u)).then_inc(heads_in[u], 16)

                with nc.Block() as block:
                    @block.sync
                    def _(sp):
                        with sp.Fori(0, 3) as t:
                            for u in range(2):
                                load_pages(sp, kc, t, u, 0, k_places, page_in)
                                sp.wait_ge(P.sem, t * len(P.names) + P.at(f"s{u}3"))
                                sp.dma_start(qh[:, u, :, :], head_rows(t * 2 + (2 + u))).then_inc(heads_in[u], 16)
                        for u in range(2):
                            load_pages(sp, kc, 3, u, 0, k_places, page_in)

                    @block.gpsimd
                    def _(pool):
                        with pool.Fori(0, 4) as t:
                            for hh in range(2):
                                pool.wait_ge(sums_out, t * 2 + (hh + 3))
                                for s_ in range(2):
                                    pool.dma_start(srow[s_, bass.ds(t * 2 + hh, 1), :, :].rearrange("o r n -> (o r) n"),
                                                   rows[HC * s_:HC * s_ + HC, hh, :]).then_inc(row_out, 16)
                                pool.wait_ge(row_out, t * 64 + 32 * (hh + 1))
                                pool.sem_inc(row_free, 1)

                    @block.tensor
                    def _(pe):
                        def at(t, steps, name):
                            return t * len(steps.names) + steps.at(name)

                        def scores(t, hh, i):
                            n = turns.index((hh, i))
                            if n >= 2:
                                pe.wait_ge(A.sem, at(t, A, "e%d%d1" % turns[n - 2]))
                            else:
                                pe.wait_ge(act_start, t + 1)
                            for c in range(2):
                                q = qh[64 * c:64 * c + 64, hh, 0, i * 128:i * 128 + 128]
                                k = qh[64 * c:64 * c + 64, hh, 1, 0:(i + 1) * 128]
                                mm = pe.matmul(ps[:, 2 * (i % 2) + c, 0:(i + 1) * 128], q, k, start=True, stop=True)
                            mm.then_inc(P.sem, 1)

                        def two_pages(t, hh, i, pair):
                            for k in range(2):
                                pg = 4 * i + 2 * pair + k
                                pe.wait_ge(page_lo, t * 32 + (hh * PAGES + pg + SLOTS + 1))
                                for h in range(DA_HEADS):
                                    mm = pe.matmul(ps[0:2 * HC, 5 + pair, k * 256:k * 256 + 256], cur[:, hh, h * 32:h * 32 + 32],
                                                   split[:, pg % SPLITS, :, h * 128:h * 128 + 128], start=(h == 0), stop=(h == DA_HEADS - 1))
                                mm.then_inc(page_used, 1)

                        with pe.Fori(0, 4) as t:
                            for hh in range(2):
                                pe.wait_ge(heads_in[hh], t * 16 + 16)
                                pe.wait_ge(head_ok, t * 2 + hh + 1)
                                for i in range(4):
                                    mm = pe.transpose(ps[:, 7, i * 128:i * 128 + 128], qh[:, hh, 2, i * 128:i * 128 + 128], C("ident"))
                                mm.then_inc(P.sem, 1)
                                scores(t, hh, 0)
                                for i in range(4):
                                    if i < 3:
                                        scores(t, hh, i + 1)
                                    if i == 0:
                                        pe.wait_ge(cur_in, t * 2 + (hh + 1))
                                    pe.wait_ge(group_out, t * 8 + (hh * 4 + i + 1))
                                    two_pages(t, hh, i, 0)
                                    pe.wait_ge(V_.sem, at(t, V_, f"w1_{hh}{i}"))
                                    if (hh, i) != (0, 0):
                                        pe.wait_ge(A.sem, at(t, A, "t%d%d" % turns[turns.index((hh, i)) - 1]))
                                    for s in range(i + 1):
                                        mm = pe.transpose(ps[:, 4, s * 128:s * 128 + 128], wt_[:, i % 2, s * 128:s * 128 + 128], C("ident"))
                                    mm.then_inc(P.sem, 1)
                                    two_pages(t, hh, i, 1)
                                    pe.wait_ge(A.sem, at(t, A, f"t{hh}{i}"))
                                    if i == 0 and hh == 1:
                                        pe.wait_ge(A.sem, at(t, A, "o0"))
                                    for s in range(i + 1):
                                        mm = pe.matmul(ps[:, 7, i * 128:i * 128 + 128], vtok[:, hh, s, :], wT[:, i % 2, s, :],
                                                       start=(s == 0), stop=(s == i))
                                    mm.then_inc(P.sem, 1)

                    @block.scalar
                    def _(act):
                        def at(t, steps, name):
                            return t * len(steps.names) + steps.at(name)
                        def page_his(t, hh, i, pair):
                            for k in range(2):
                                pg = 4 * i + 2 * pair + k
                                act.wait_ge(page_in[pg % SLOTS], t * (512 // SLOTS) + 16 * ((hh * PAGES + pg) // SLOTS + 1))
                                act.wait_ge(page_used, t * 32 + (hh * PAGES + pg + 1))
                                act.activation(split[:, pg % SPLITS, 0, :], ring[:, pg % SLOTS, :], ACT.Copy).then_inc(page_hi, 1)

                        def half_of(t, hh, i, before):
                            parts, to = k_parts(hh, i)
                            if i == 0:
                                act.wait_ge(row_free, t * 2 + (hh + 1))
                            act.wait_ge(page_used, t * 32 + (SPLITS + 4 * before))
                            act.activation(to, parts[:, :, :, 0, :], ACT.Copy).then_inc(half_out, 1)

                        def body(t, first):
                            act.sem_inc(act_start, 1)
                            act.sem_inc(head_ok, 1)
                            for hh, i in turns:
                                u = turns.index((hh, i))
                                if i == 0:
                                    act.wait_ge(P.sem, at(t, P, f"vt{hh}"))
                                    act.activation(vtok[:, hh, :, :], ps[:, 7, :], ACT.Copy).then_inc(A.sem, 1)
                                    dst, src = k_operands(t * 2 + hh, hh)
                                    act.wait_ge(sums_out, t * 2 + (hh + 1))
                                    act.activation(dst[:, :, 0, :], src, ACT.Copy).then_inc(cur_hi, 1)
                                page_his(t, hh, i, 0)
                                if u or not first:
                                    half_of(t, *turns[u - 1], u)
                                n = (i + 1) * 128
                                act.wait_ge(V_.sem, at(t, V_, f"neg{hh}{i}"))
                                for c in range(2):
                                    act.activation(ex[:, i % 2, c, 0:n], ps[:, 2 * (i % 2) + c, 0:n], ACT.Exp,
                                                   bias=nmx[:, i % 2, c:c + 1], scale=0.125,
                                                   accum_out=rs[:, i % 2, c:c + 1]).then_inc(A.sem, 1)
                                page_his(t, hh, i, 1)
                                act.wait_ge(P.sem, at(t, P, f"t{hh}{i}"))
                                act.activation(wT[:, i % 2, 0:i + 1, :], ps[:, 4, 0:n], ACT.Copy).then_inc(A.sem, 1)
                                if i == 3:
                                    act.wait_ge(P.sem, at(t, P, f"o{hh}3"))
                                    to = yd[:, t * 2 + hh, 0:SEQ] if first else \
                                        yd[:, bass.ds(t * 2 + hh, 1), 0:SEQ].rearrange("p o n -> p (o n)")
                                    act.activation(to, ps[:, 7, :], ACT.Copy).then_inc(A.sem, 1)
                                    act.wait_ge(A.sem, at(t, A, f"o{hh}"))
                                    if hh == 0:
                                        act.sem_inc(head_ok, 1)
                        body(0, True)
                        with act.Fori(1, 4) as t:
                            body(t, False)
                        half_of(3, 1, 3, 8)

                    @block.vector
                    def _(dve):
                        def at(t, steps, name):
                            return t * len(steps.names) + steps.at(name)
                        def page_los(t, hh, i, pair):
                            for k in range(2):
                                pg = 4 * i + 2 * pair + k
                                dve.wait_ge(page_hi, t * 32 + (hh * PAGES + pg + 1))
                                dve.tensor_tensor(split[:, pg % SPLITS, 1, :], ring[:, pg % SLOTS, :],
                                                  split[:, pg % SPLITS, 0, :].bitcast(f32), ALU.subtract).then_inc(page_lo, 1)

                        def add_of(t, hh, i, before):
                            parts, to = k_parts(hh, i)
                            dve.wait_ge(half_out, t * 8 + before)
                            dve.tensor_tensor(to, to, parts[:, :, :, 1, :], ALU.add).then_inc(group_out, 1)
                            if i == 3:
                                dve.wait_ge(group_out, t * 8 + (before + 1))
                                dve.sem_inc(sums_out, 1)

                        def body(t, first):
                            for hh, i in turns:
                                n, b = (i + 1) * 128, i % 2
                                dve.wait_ge(P.sem, at(t, P, f"s{hh}{i}"))
                                diag = ps[:, 2 * b:2 * b + 2, i * 128:n]
                                mask = C("causal").unsqueeze(1).to_broadcast([128, 2, 128])
                                dve.tensor_tensor(diag, diag, mask, ALU.add).then_inc(V_.sem, 1)
                                dve.wait_ge(V_.sem, at(t, V_, f"mask{hh}{i}"))
                                dve.reduce_max(mx[:, b, :], ps[:, 2 * b:2 * b + 2, 0:n], AX.X).then_inc(V_.sem, 1)
                                dve.wait_ge(V_.sem, at(t, V_, f"max{hh}{i}"))
                                dve.tensor_scalar(nmx[:, b, :], mx[:, b, :], -0.125, None, ALU.mult).then_inc(V_.sem, 1)
                                if i == 0:
                                    dst, src = k_operands(t * 2 + hh, hh)
                                    dve.wait_ge(cur_hi, t * 2 + (hh + 1))
                                    dve.tensor_tensor(dst[:, :, 1, :], src, dst[:, :, 0, :].bitcast(f32), ALU.subtract).then_inc(cur_in, 1)
                                page_los(t, hh, i, 0)
                                if turns.index((hh, i)) or not first:
                                    add_of(t, *turns[turns.index((hh, i)) - 1], turns.index((hh, i)))
                                dve.wait_ge(A.sem, at(t, A, f"e{hh}{i}1"))
                                dve.reciprocal(ri[:, b, :], rs[:, b, :]).then_inc(V_.sem, 1)
                                dve.wait_ge(V_.sem, at(t, V_, f"inv{hh}{i}"))
                                dve.tensor_tensor(ri[:, b, 1:2], ri[:, b, 1:2], neg_lam, ALU.mult).then_inc(V_.sem, 1)
                                turn = turns.index((hh, i))
                                if turn >= 2:
                                    dve.wait_ge(P.sem, at(t, P, "t%d%d" % turns[turn - 2]))
                                dve.tensor_scalar(wt_[:, b, 0:n], ex[:, b, 0, 0:n], ri[:, b, 0:1], None, ALU.mult).then_inc(V_.sem, 1)
                                dve.wait_ge(V_.sem, at(t, V_, f"w0_{hh}{i}"))
                                dve.scalar_tensor_tensor(wt_[:, b, 0:n], ex[:, b, 1, 0:n], ri[:, b, 1:2], wt_[:, b, 0:n],
                                                         ALU.mult, ALU.add).then_inc(V_.sem, 1)
                                page_los(t, hh, i, 1)
                        body(0, True)
                        with dve.Fori(1, 4) as t:
                            body(t, False)
                        add_of(3, 1, 3, 8)

            with ExitStack() as st:
                sc = sb(st, "scores_s", [128, PAST])
                ws = sb(st, "w_pages", [128, PAGES, NS * DA_HEADS])
                oT = sb(st, "out_rows", [64, 2, 128])
                more = sb(st, "page_ring_more", [128, SLOTS, RW])
                v_places = k_places + [more[:, i, :] for i in range(SLOTS)]
                v_in = [sem(f"value_page_in{i}") for i in range(2 * SLOTS)]

                def pass_block(cache, g0, operands, product, collect, stores):
                    first = g0 // PAGES
                    with nc.Block() as block:
                        @block.sync
                        def _(sp):
                            with sp.Fori(0, NS // 2) as t:
                                for bb in range(2):
                                    load_pages(sp, cache, t, bb, g0, v_places, v_in)

                        @block.scalar
                        def _(act):
                            with act.Fori(0, NS // 2) as t:
                                for bb in range(2):
                                    dst, src = operands(t * 2 + bb, bb)
                                    act.wait_ge(sums_out, t * 2 + (bb + 1 + first))
                                    act.activation(dst[:, :, 0, :], src, ACT.Copy).then_inc(cur_hi, 1)
                                    for pg in range(PAGES):
                                        n = t * 32 + (g0 + bb * PAGES + pg)
                                        act.wait_ge(v_in[pg % 8], t * 64 + 16 * ((bb * PAGES + pg) // 8 + 1))
                                        act.wait_ge(page_used, n + 1)
                                        act.activation(split[:, pg % SPLITS, 0, :], v_places[pg % 8], ACT.Copy).then_inc(page_hi, 1)

                        @block.vector
                        def _(dve):
                            with dve.Fori(0, NS // 2) as t:
                                for bb in range(2):
                                    dst, src = operands(t * 2 + bb, bb)
                                    dve.wait_ge(cur_hi, t * 2 + (bb + 1 + first))
                                    dve.tensor_tensor(dst[:, :, 1, :], src, dst[:, :, 0, :].bitcast(f32), ALU.subtract).then_inc(cur_in, 1)
                                    dve.wait_ge(row_free, t * 2 + (bb + 1 + first))
                                    for pg in range(PAGES):
                                        n = t * 32 + (g0 + bb * PAGES + pg)
                                        dve.wait_ge(page_hi, n + 1)
                                        dve.tensor_tensor(split[:, pg % SPLITS, 1, :], v_places[pg % 8],
                                                          split[:, pg % SPLITS, 0, :].bitcast(f32), ALU.subtract).then_inc(page_lo, 1)
                                        collect(dve, t, bb, pg)
                                    dve.wait_ge(page_used, t * 32 + (SPLITS + g0 + (bb + 1) * PAGES))
                                    collect(dve, t, bb, PAGES)
                                    dve.sem_inc(sums_out, 1)

                        @block.tensor
                        def _(pe):
                            with pe.Fori(0, NS // 2) as t:
                                for bb in range(2):
                                    pe.wait_ge(cur_in, t * 2 + (bb + 1 + first))
                                    pe.wait_ge(sums_out, t * 2 + (bb + 1 + first))
                                    for pg in range(PAGES):
                                        pe.wait_ge(page_lo, t * 32 + (g0 + bb * PAGES + pg + SLOTS + 1))
                                        product(pe, t, bb, pg).then_inc(page_used, 1)

                        @block.gpsimd
                        def _(pool):
                            with pool.Fori(0, NS // 2) as t:
                                for bb in range(2):
                                    pool.wait_ge(sums_out, t * 2 + (bb + 3 + first))
                                    for to, source in stores(t * 2 + bb, bb):
                                        pool.dma_start(to, source).then_inc(row_out, 16)
                                    pool.wait_ge(row_out, t * 64 + 32 * (bb + 1 + first))
                                    pool.sem_inc(row_free, 1)

                S = Steps(sem("soft_steps"), ["snew_mm", "snew", "sum", "m1", "m", "nm", "exp", "enew", "tot", "inv", "cmb0", "cmb", "cmb_n",
                                              "wn_mm", "ws_mm0", "ws_mm1", "ws0", "ws1", "ov"])
                with nc.Block() as block:
                    @block.sync
                    def _(sp):
                        for s_, to in enumerate((sc[:, :], rows[:, 0, :])):
                            sp.dma_start(to, srow[s_, :, :, :].rearrange("b r n -> (b r) n")).then_inc(samp_in, 16)

                    @block.tensor
                    def _(pe):
                        pe.matmul(ps[:, 4, 0:1], prod[:, :, :, :].rearrange("p a b c -> p (a b c)"), C("ones")[:, 0:1],
                                  start=True, stop=True).then_inc(S.sem, 1)
                        pe.wait_ge(S.sem, S.at("cmb_n"))
                        pe.matmul(ps[:, 4, 64:128], C("ones"), comb_n[:, :], start=True, stop=True).then_inc(S.sem, 1)
                        for half in range(2):
                            for g in range(8):
                                pg = half * 8 + g
                                mm = pe.matmul(ps[:, half, g * 64:g * 64 + 64], sc[:, pg * PAGE:pg * PAGE + PAGE], comb[:, :],
                                               start=True, stop=True)
                            mm.then_inc(S.sem, 1)

                    @block.scalar
                    def _(act):
                        act.wait_ge(S.sem, S.at("nm"))
                        act.activation(sc[:, :], sc[:, :], ACT.Exp, bias=nm, scale=0.125, accum_out=part).then_inc(S.sem, 1)
                        act.wait_ge(S.sem, S.at("exp"))
                        act.activation(enew, snew, ACT.Exp, bias=nm, scale=0.125).then_inc(S.sem, 1)

                    @block.vector
                    def _(dve):
                        def did(ins, name):
                            ins.then_inc(S.sem, 1)
                            dve.wait_ge(S.sem, S.at(name))
                        dve.wait_ge(S.sem, S.at("snew_mm"))
                        did(dve.tensor_copy(snew, ps[:, 4, 0:1]), "snew")
                        dve.wait_ge(samp_in, 64)
                        did(dve.tensor_tensor(sc[:, :], sc[:, :], rows[:, 0, :], ALU.add), "sum")
                        did(dve.reduce_max(m1, sc[:, :], AX.X), "m1")
                        did(dve.tensor_tensor(m1, m1, snew, ALU.max), "m")
                        did(dve.tensor_scalar(nm, m1, -0.125, None, ALU.mult), "nm")
                        dve.wait_ge(S.sem, S.at("enew"))
                        did(dve.tensor_tensor(part, part, enew, ALU.add), "tot")
                        did(dve.reciprocal(inv, part), "inv")
                        did(dve.scalar_tensor_tensor(comb[:, :], C("map1"), neg_lam, C("map0"), ALU.mult, ALU.add), "cmb0")
                        did(dve.tensor_scalar(comb[:, :], comb[:, :], inv, None, ALU.mult), "cmb")
                        did(dve.tensor_scalar(comb_n[:, :], comb[:, :], enew, None, ALU.mult), "cmb_n")
                        dve.wait_ge(S.sem, S.at("ws_mm1"))
                        for half in range(2):
                            did(dve.tensor_copy(ws[:, 8 * half:8 * half + 8, :].rearrange("p a b -> p (a b)"), ps[:, half, :]), f"ws{half}")
                        did(dve.tensor_tensor(ov[:, :, :], qs[:, 16:24, :].rearrange("p h b -> p b h"),
                                              ps[:, 4, 64:128].rearrange("p (b h) -> p b h", h=DA_HEADS), ALU.mult), "ov")

                def v_operands(b, bb):
                    return (cur[:, bb, :].rearrange("p (g s n) -> p g s n", g=PAGES, s=2), ws[:, :, bass.ds(b * DA_HEADS, DA_HEADS)])

                def v_product(pe, t, bb, pg):
                    for part in range(2):
                        for n in range(2):
                            mm = pe.matmul(ps[0:2 * DA_HEADS, 2 * bb + n, :], cur[:, bb, pg * 16:pg * 16 + 16],
                                           split[:, pg % SPLITS, part, n * 512:n * 512 + 512],
                                           start=(pg == 0 and part == 0), stop=(pg == PAGES - 1 and part == 1))
                    return mm

                def v_collect(dve, t, bb, pg):
                    if pg == PAGES:
                        dve.tensor_copy(rows[0:16, bb, 0:RW], ps[0:16, 2 * bb:2 * bb + 2, :].rearrange("p a b -> p (a b)")).then_inc(group_out, 1)
                        dve.wait_ge(group_out, t * 2 + (1 + 4 * NS + bb + 1))

                pass_block(vc, 128, v_operands, v_product, v_collect,
                           lambda b, bb: [(orow[s_, bass.ds(b, 1), 0:DA_HEADS * RW].rearrange("o (h n) -> (o h) n", n=RW),
                                           rows[DA_HEADS * s_:DA_HEADS * s_ + DA_HEADS, bb, 0:RW]) for s_ in range(2)])
                own = [orow[s_, :, :].rearrange("b (h m) -> (b h) m", m=RW + 128)[:, 0:128] for s_ in range(2)]
                with nc.Block() as block:
                    @block.sync
                    def _(sp):
                        for s_ in range(2):
                            sp.dma_start(oT[:, s_, :], own[s_]).then_inc(samp_in, 16)

                    @block.tensor
                    def _(pe):
                        pe.wait_ge(samp_in, 96)
                        for s_ in range(2):
                            mm = pe.matmul(ps[:, 4, 0:64], oT[:, s_, :], C("ident")[0:64, 0:64], start=(s_ == 0), stop=(s_ == 1))
                        mm.then_inc(q_ready, 1)

                    @block.vector
                    def _(dve):
                        dve.wait_ge(q_ready, 8)
                        dve.tensor_tensor(yd[:, :, SEQ:TOK].rearrange("p h b -> p b h"),
                                          ps[:, 4, 0:64].rearrange("p (b h) -> p b h", h=DA_HEADS), ov[:, :, :], ALU.add).then_inc(q_ready, 1)

            with ExitStack() as st:
                sq = sb(st, "yd_sq", [128, 2, TOK])
                rn = sb(st, "yd_rms", [128, DA_HEADS, TOK])
                y_out = sem("y_out")
                H = range(DA_HEADS)
                NQ = Steps(sem("subln_act"), [f"{x}{h}" for x in ("sq", "ln", "rt") for h in H])
                NP = Steps(sem("subln_pe"), [f"mm{h}" for h in H])
                NV = Steps(sem("subln_dve"), [f"{x}{h}" for h in H for x in ("ms0_", "ms1_")] + [f"y{h}" for h in H])
                with nc.Block() as block:
                    @block.scalar
                    def _(act):
                        for h in H:
                            if h >= 2:
                                act.wait_ge(NP.sem, NP.at(f"mm{h - 2}"))
                            act.activation(sq[:, h % 2, :], yd[:, h, :], ACT.Square).then_inc(NQ.sem, 1)
                        for h in H:
                            act.wait_ge(NV.sem, NV.at(f"ms1_{h}"))
                            act.activation(rn[:, h, :], rn[:, h, :], ACT.Ln).then_inc(NQ.sem, 1)
                        for h in H:
                            act.wait_ge(NQ.sem, NQ.at(f"ln{h}"))
                            act.activation(rn[:, h, :], rn[:, h, :], ACT.Exp, scale=-0.5).then_inc(NQ.sem, 1)

                    @block.tensor
                    def _(pe):
                        for h in H:
                            pe.wait_ge(NQ.sem, NQ.at(f"sq{h}"))
                            if h >= 4:
                                pe.wait_ge(NV.sem, NV.at(f"ms1_{h - 4}"))
                            for i, (a, m) in enumerate(SPANS):
                                mm = pe.matmul(ps[:, 2 * (h % 4) + i, 0:m], C("ones"), sq[:, h % 2, a:a + m], start=True, stop=True)
                            mm.then_inc(NP.sem, 1)

                    @block.vector
                    def _(dve):
                        for h in H:
                            dve.wait_ge(NP.sem, NP.at(f"mm{h}"))
                            for i, (a, m) in enumerate(SPANS):
                                dve.tensor_scalar(rn[:, h, a:a + m], ps[:, 2 * (h % 4) + i, 0:m], 1.0 / 128, 1e-6,
                                                  ALU.mult, ALU.add).then_inc(NV.sem, 1)
                        for h in H:
                            dve.wait_ge(NQ.sem, NQ.at(f"rt{h}"))
                            dve.scalar_tensor_tensor(yd[:, h, :], yd[:, h, :], sub_g, rn[:, h, :], ALU.mult, ALU.mult).then_inc(NV.sem, 1)

                    @block.sync
                    def _(sp):
                        for h in H:
                            sp.wait_ge(NV.sem, NV.at(f"y{h}"))
                            sp.dma_start(ymix[8 + h, :, :], yd[:, h, :]).then_inc(y_out, 16)
                        sp.wait_ge(y_out, 128)
            samples.close()
            attn.close()

            tile_r, tile_k, tile_v = rkv[:, 0:RT, :], rkv[:, RT:2 * RT, :], rkv[:, 2 * RT:3 * RT, :]
            au = sb(mixing, "iclr", [128, RT, TOK])
            kk = sb(mixing, "kk", [128, RT, TOK])
            cum = sb(mixing, "cum", [128, RT, TOK])
            g2s = sb(mixing, "g2s", [128, RW])
            flat = lambda a: a.rearrange("p a b -> p (a b)")
            lora_in = sem("lora_in")
            with ExitStack() as st:
                wa = sb(st, "w2a2s", [128, RW])
                sq = sb(st, "kk_sq", [128, 2, TOK])
                nr = sb(st, "kk_norm", [128, RT, TOK])
                tk = sb(st, "k_gain", [128, TOK])
                J = range(RT)
                A = Steps(sem("prep_act"), ["tanh"] + [f"sq{j}" for j in J] + [f"ln{j}" for j in J] + [f"rt{j}" for j in J] + ["sig"]
                          + [f"{x}{j}" for j in J for x in ("w0_", "w1_", "a0_", "a1_")])
                P = Steps(sem("prep_pe"), [f"n{j}" for j in J] + [f"{x}{j}" for j in J for x in ("w", "a")])
                W = Steps(sem("prep_dve"), [f"kk{j}" for j in J] + [f"{x}{j}" for j in J for x in ("m0_", "m1_")]
                          + [f"{x}{j}" for j in J for x in ("t", "kn", "cum", "kmod", "b")])
                with nc.Block() as block:
                    @block.sync
                    def _(sp):
                        sp.dma_start(wa[:, :], w2a2).then_inc(lora_in, 16)
                        sp.dma_start(g2s[:, :], g2).then_inc(lora_in, 16)

                    @block.scalar
                    def _(act):
                        act.activation(rkv[0:64, 24, :], rkv[0:64, 24, :], ACT.Tanh).then_inc(A.sem, 1)
                        for j in J:
                            act.wait_ge(W.sem, W.at(f"kk{j}"))
                            if j >= 2:
                                act.wait_ge(P.sem, P.at(f"n{j - 2}"))
                            act.activation(sq[:, j % 2, :], kk[:, j, :], ACT.Square).then_inc(A.sem, 1)
                        for j in J:
                            act.wait_ge(W.sem, W.at(f"m1_{j}"))
                            act.activation(nr[:, j, :], nr[:, j, :], ACT.Ln).then_inc(A.sem, 1)
                        for j in J:
                            act.wait_ge(A.sem, A.at(f"ln{j}"))
                            act.activation(nr[:, j, :], nr[:, j, :], ACT.Exp, scale=-0.5).then_inc(A.sem, 1)
                        act.activation(rkv[:, 25, :], rkv[:, 25, :], ACT.Sigmoid).then_inc(A.sem, 1)
                        for j in J:
                            for x, (out, bias) in enumerate(((cum, "w0"), (au, "a0"))):
                                act.wait_ge(P.sem, P.at("wa"[x] + str(j)))
                                for i, (a, m) in enumerate(SPANS):
                                    act.activation(out[:, j, a:a + m], ps[:, 4 * (j % 2) + 2 * x + i, 0:m], ACT.Sigmoid,
                                                   bias=V(bias, j)).then_inc(A.sem, 1)

                    @block.tensor
                    def _(pe):
                        for j in J:
                            pe.wait_ge(A.sem, A.at(f"sq{j}"))
                            if j >= 2:
                                pe.wait_ge(W.sem, W.at(f"m1_{j - 2}"))
                            for i, (a, m) in enumerate(SPANS):
                                mm = pe.matmul(ps[:, 4 + 2 * (j % 2) + i, 0:m], C("pair"), sq[:, j % 2, a:a + m], start=True, stop=True)
                            mm.then_inc(P.sem, 1)
                        pe.wait_ge(lora_in, 32)
                        for j in J:
                            if j == 1:
                                pe.wait_ge(W.sem, W.at(f"m1_{RT - 1}"))
                            for x in range(2):
                                if j >= 2:
                                    pe.wait_ge(A.sem, A.at("wa"[x] + f"1_{j - 2}"))
                                half = slice(64 * x, 64 * x + 64)
                                for i, (a, m) in enumerate(SPANS):
                                    mm = pe.matmul(ps[:, 4 * (j % 2) + 2 * x + i, 0:m], wa[half, j * 128:j * 128 + 128],
                                                   rkv[half, 24, a:a + m], start=True, stop=True)
                                mm.then_inc(P.sem, 1)

                    @block.vector
                    def _(dve):
                        def need(name):
                            dve.wait_ge(W.sem, W.at(name))
                        for j in J:
                            dve.tensor_scalar(kk[:, j, :], tile_k[:, j, :], V("k_k", j), None, ALU.mult).then_inc(W.sem, 1)
                        for j in J:
                            dve.wait_ge(P.sem, P.at(f"n{j}"))
                            for i, (a, m) in enumerate(SPANS):
                                dve.tensor_scalar(nr[:, j, a:a + m], ps[:, 4 + 2 * (j % 2) + i, 0:m], 1e-24, None,
                                                  ALU.max).then_inc(W.sem, 1)
                        for j in J:
                            dve.wait_ge(A.sem, A.at(f"a1_{j}"))
                            if j:
                                need(f"kmod{j - 1}")
                            dve.tensor_scalar(tk[:, :], au[:, j, :], -1.0, V("k_a", j), ALU.add, ALU.mult).then_inc(W.sem, 1)
                            need(f"kk{j}")
                            dve.tensor_tensor(kk[:, j, :], kk[:, j, :], nr[:, j, :], ALU.mult).then_inc(W.sem, 1)
                            dve.tensor_tensor_scan(cum[:, j, :], C("start"), cum[:, j, :], 0.0, ALU.mult, ALU.add).then_inc(W.sem, 1)
                            need(f"t{j}")
                            dve.scalar_tensor_tensor(tile_k[:, j, :], tk[:, :], 1.0, tile_k[:, j, :], ALU.add, ALU.mult).then_inc(W.sem, 1)
                            need(f"kn{j}")
                            dve.tensor_tensor(au[:, j, :], kk[:, j, :], au[:, j, :], ALU.mult).then_inc(W.sem, 1)

            with ExitStack() as st:
                sv = sb(st, "step_in", [128, 6, 2, 64])
                tv = sb(st, "step_vecs", [128, 6, 64])
                state = sb(st, "step_state", [128, 64, 64])
                prod = sb(st, "step_prod", [128, 64, 64])
                dec = sb(st, "step_decay", [128, RT, NS])
                sa = sb(st, "step_sa", [128, 64])
                yb = sb(st, "step_y", [128, 64])
                yd2 = sb(st, "step_y2", [128, 128])
                state_in, state_out = sem("state_in"), sem("state_out")
                S = Steps(sem("step"), ["dec"] + [f"v{i}" for i in range(6)] + ["T", "ta", "tb", "Sa", "sa", "Sw", "sab", "S1",
                                        "vk", "S2", "Sr", "y", "y0", "ya", "yb", "yT", "t2", "t2r", "oa", "ob"])
                with nc.Block() as block:
                    @block.sync
                    def _(sp):
                        sp.dma_start(state[:, :, :], s0).then_inc(state_in, 16)
                        sp.wait_ge(S.sem, S.at("S2"))
                        sp.dma_start(wkv_s, state[:, :, :]).then_inc(state_out, 16)
                        sp.wait_ge(state_out, 16)

                    @block.scalar
                    def _(act):
                        act.activation(dec[:, :, :], cum[:, :, SEQ:TOK], ACT.Exp, scale=-DECAY).then_inc(S.sem, 1)

                    @block.tensor
                    def _(pe):
                        pe.wait_ge(S.sem, S.at("v5"))
                        for i in range(6):
                            mm = pe.transpose(ps[:, i // 4, i % 4 * 128:i % 4 * 128 + 128], sv[:, i, :, :].rearrange("p a b -> p (a b)"),
                                              C("ident"))
                        mm.then_inc(S.sem, 1)
                        pe.wait_ge(S.sem, S.at("yb"))
                        pe.transpose(ps[:, 2, 0:128], yd2[:, :], C("ident")).then_inc(S.sem, 1)

                    @block.vector
                    def _(dve):
                        def did(ins, name):
                            ins.then_inc(S.sem, 1)
                            dve.wait_ge(S.sem, S.at(name))
                        dve.wait_ge(S.sem, S.at("dec"))
                        rows = [kk[:, :, SEQ:TOK], dec[:, :, :], au[:, :, SEQ:TOK], tile_k[:, :, SEQ:TOK], tile_v[:, :, SEQ:TOK],
                                tile_r[:, :, SEQ:TOK]]
                        for i, v in enumerate(rows):
                            did(dve.tensor_copy(sv[:, i, :, :].rearrange("p t (a b) -> p t a b", a=RT),
                                                v.unsqueeze(1).to_broadcast([128, 2, RT, NS])), f"v{i}")
                        dve.wait_ge(S.sem, S.at("T"))
                        both = ps[:, 0:2, :].rearrange("p a (b c) -> p (a b) c", b=4)
                        did(dve.tensor_copy(tv[0:64, :, :], both[0:64, 0:6, 0:64]), "ta")
                        did(dve.tensor_copy(tv[64:128, :, :], both[64:128, 0:6, 64:128]), "tb")
                        cols = lambda i: tv[:, i, :].unsqueeze(1).to_broadcast([128, 64, 64])
                        rows_ = lambda a: a.unsqueeze(2).to_broadcast([128, 64, 64])
                        st_, pr = state[:, :, :], prod[:, :, :]
                        dve.wait_ge(state_in, 16)
                        did(dve.tensor_tensor(pr, st_, cols(0), ALU.mult), "Sa")
                        did(dve.reduce_sum(sa[:, :], pr, AX.X), "sa")
                        did(dve.tensor_tensor(st_, st_, cols(1), ALU.mult), "Sw")
                        did(dve.tensor_tensor(pr, rows_(sa[:, :]), cols(2), ALU.mult), "sab")
                        did(dve.tensor_tensor(st_, st_, pr, ALU.subtract), "S1")
                        did(dve.tensor_tensor(pr, rows_(tv[:, 4, :]), cols(3), ALU.mult), "vk")
                        did(dve.tensor_tensor(st_, st_, pr, ALU.add), "S2")
                        did(dve.tensor_tensor(pr, st_, cols(5), ALU.mult), "Sr")
                        did(dve.reduce_sum(yb[:, :], pr, AX.X), "y")
                        did(dve.memset(yd2[:, :], 0.0), "y0")
                        did(dve.tensor_copy(yd2[0:64, 0:64], yb[0:64, :]), "ya")
                        did(dve.tensor_copy(yd2[64:128, 64:128], yb[64:128, :]), "yb")
                        dve.wait_ge(S.sem, S.at("yT"))
                        last_r, last_a = tile_r[:, :, SEQ:TOK], au[:, :, SEQ:TOK]
                        rk = vt[:, VEC["r_k"]:VEC["r_k"] + RT].unsqueeze(2).to_broadcast([128, RT, NS])
                        did(dve.tensor_tensor(last_a, last_r, tile_k[:, :, SEQ:TOK], ALU.mult), "t2")
                        did(dve.tensor_tensor(last_a, last_a, rk, ALU.mult), "t2r")
                        for x, name in ((0, "oa"), (64, "ob")):
                            did(dve.tensor_copy(last_r[x:x + 64], ps[x:x + 64, 2, x:x + 64].rearrange("p (a b) -> p a b", a=RT)), name)

            with ExitStack() as st:
                e65 = sb(st, "decay", [128, RT, CH + 1])
                ei = sb(st, "decay_inv", [128, RT, CH])
                stg = sb(st, "chunk", [128, RT, 4, CH])
                vst = sb(st, "chunk_v", [128, RT, 2, CH])
                qa = sb(st, "rhs_left", [128, 2, RT, CH])
                gr = sb(st, "out_right", [128, 2, RT, CH])
                sl = sb(st, "inverse", [128, 2, 6, 4 * 128])
                xs = sb(st, "solve", [128, RT, 128])
                svb = sb(st, "state_v", [128, 2, RT, CH])
                zb = sb(st, "sa_v", [128, 2, RT, CH])
                sbd = sb(st, "state_diag", [128, RT, 128])
                rh = sb(st, "rhs", [128, RT, CH])
                bk = sb(st, "bk_tok", [128, RT, 128])
                rc = sb(st, "chunk_r", [128, RT, CH])
                wl = sb(st, "chunk_decay", [128, RT, 1])
                turn_ok = sem("turn_ok")
                zeroed = sem("zeroed")
                pool_woke = sem("pool_woke")
                A0 = Steps(sem("stage_act"), ["E", "Ei", "qa_a", "qa_b"])
                W0 = Steps(sem("stage_dve"), ["at", "rt", "u2a", "u3a", "u2b", "u3b"])
                P0 = Steps(sem("gram_pe"), ["mg0", "mg1"])
                W1 = Steps(sem("mask_dve"), [f"{x}0" for x in ("dA", "dB", "tA", "tB", "oA", "oB", "x1", "kA", "kB", "gA", "gB")]
                           + [f"{x}1" for x in ("dA", "dB", "tA", "tB", "oA", "oB", "x1", "gA", "gB", "kA", "kB")])
                A = Steps(sem("rw_act"), ["wl", "D2t0", "bk", "D2t1", "D4t0", "D4t1", "v1", "v2", "v3", "v4"]
                          + [f"{x}{q}" for x in ("Nt", "XDt", "N2t", "N4t", "X") for q in range(2)] + ["rhs", "za", "y", "sd_a", "sd_b"])
                P = Steps(sem("rw_pe"), ["D20", "D2t0", "bk", "D21", "D2t1", "D4t0", "DX0", "D4t1", "DX1", "v"]
                          + [f"{x}{q}" for xs_ in (("DXX",), ("N", "Nt"), ("XDt",), ("N2", "N2t"), ("N4t", "NY"), ("NYY",), ("X",))
                             for q in range(2) for x in xs_] + ["rhs", "sa", "y", "s"])
                W = Steps(sem("rw_dve"), [f"{x}{q}" for xs_ in (("D2",), ("X2",), ("XD",), ("N", "Y1"), ("N2",), ("Y2",), ("Y3",))
                                          for q in range(2) for x in xs_] + ["zb", "sA", "sB", "swA", "swB"])
                G = Steps(sem("rw_pool"), ["vst", "rc", "t2", "t2r"])

                def at(c, steps, name):
                    return c * len(steps.names) + steps.at(name)

                def chunk(t, c):
                    return t[:, :, bass.ds(c * CH, CH)]

                def blocks(t):
                    return t.rearrange("p (a b) -> p a b", a=4)

                def turns_of(eng, body):
                    with eng.Fori(0, NCH - 1) as c:
                        body(c, False)
                    body(NCH - 1, True)

                AA, BB = slice(0, 64), slice(64, 128)
                with nc.Block() as block:
                    @block.vector
                    def _(dve):
                        dve.memset(sl[:, :, :, :], 0.0).then_inc(zeroed, 1)
                        dve.memset(svb[:, :, :, :], 0.0).then_inc(zeroed, 1)
                        dve.memset(sbd[:, :, :], 0.0).then_inc(zeroed, 1)
                        dve.memset(e65[:, :, 0:1], 1.0).then_inc(zeroed, 1)
                        dve.sem_inc(turn_ok, 1)

                with nc.Block() as block:
                    @block.gpsimd
                    def _(pool):
                        pool.wait_ge(W0.sem, W0.at("u3b"))
                        with pool.Fori(0, NCH) as c:
                            pool.wait_ge(turn_ok, c + 1)
                            pool.tensor_copy(vst[:, :, :, :], chunk(tile_v, c).unsqueeze(2).to_broadcast([128, RT, 2, CH])).then_inc(G.sem, 1)
                            pool.tensor_copy(rc[:, :, :], stg[:, :, 1, :]).then_inc(G.sem, 1)
                            pool.tensor_tensor(chunk(au, c), chunk(tile_r, c), chunk(tile_k, c), ALU.mult).then_inc(G.sem, 1)
                            pool.wait_ge(G.sem, at(c, G, "t2"))
                            pool.sem_inc(pool_woke, 1)
                            rk = vt[:, VEC["r_k"]:VEC["r_k"] + RT].unsqueeze(2).to_broadcast([128, RT, CH])
                            pool.tensor_tensor(chunk(au, c), chunk(au, c), rk, ALU.mult).then_inc(G.sem, 1)

                    @block.scalar
                    def _(act):
                        def decays(n):
                            act.activation(e65[:, :, 1:CH + 1], chunk(cum, n), ACT.Exp, scale=-DECAY).then_inc(A0.sem, 1)
                            act.activation(ei[:, :, :], chunk(cum, n), ACT.Exp, scale=DECAY).then_inc(A0.sem, 1)

                        def left_a(n):
                            act.wait_ge(W0.sem, at(n, W0, "at"))
                            act.activation(qa[AA, 0, :, :], stg[AA, :, 0, :], ACT.Copy).then_inc(A0.sem, 1)
                            act.activation(qa[BB, 1, :, :], stg[BB, :, 0, :], ACT.Copy).then_inc(A0.sem, 1)

                        def body(c, last):
                            def leave(dst, src, name):
                                act.wait_ge(P.sem, at(c, P, name))
                                act.activation(dst, src, ACT.Copy).then_inc(A.sem, 1)

                            def chain(name, slot, b, q):
                                leave(sl[:, q, slot, :], ps[:, 4 * q + b, :], f"{name}{q}")
                            act.activation(wl[:, :, :], e65[:, :, CH:CH + 1], ACT.Copy).then_inc(A.sem, 1)
                            chain("D2t", 5, 1, 0)
                            leave(bk[:, :, :], ps[:, 2:4, :], "bk")
                            chain("D2t", 5, 1, 1)
                            for q in range(2):
                                chain("D4t", 0, 0, q)
                            if not last:
                                act.wait_ge(A.sem, at(c, A, "wl"))
                                decays(c + 1)
                            vv = ps[:, 6:8, :].rearrange("p a (b c) -> p (a b) c", b=4)
                            act.wait_ge(P.sem, at(c, P, "v"))
                            for t in (svb, zb):
                                act.activation(t[BB, 0, :, :], vv[BB, :, 0:64], ACT.Copy).then_inc(A.sem, 1)
                                act.activation(t[AA, 1, :, :], vv[AA, :, 64:128], ACT.Copy).then_inc(A.sem, 1)
                            for name, slot, b in (("Nt", 1, 1), ("XDt", 4, 0), ("N2t", 3, 0), ("N4t", 0, 0)):
                                for q in range(2):
                                    chain(name, slot, b, q)
                            for q in range(2):
                                leave(xs[:, 4 * q:4 * q + 4, :], ps[:, 4 * q + 1, :], f"X{q}")
                            leave(rh[:, :, :], ps[:, 6, :], "rhs")
                            if not last:
                                left_a(c + 1)
                            act.wait_ge(P.sem, at(c, P, "sa"))
                            act.activation(zb[AA, 0, :, :], ps[AA, 7, :], ACT.Copy).then_inc(A.sem, 1)
                            act.wait_ge(G.sem, at(c, G, "t2r"))
                            act.wait_ge(P.sem, at(c, P, "y"))
                            act.activation(chunk(tile_r, c), ps[:, 4, :].rearrange("p (a b) -> p a b", a=RT), ACT.Copy).then_inc(A.sem, 1)
                            act.wait_ge(W.sem, at(c, W, "swB"))
                            act.activation(sbd[AA, :, 0:64], svb[AA, 0, :, :], ACT.Copy).then_inc(A.sem, 1)
                            act.activation(sbd[BB, :, 64:128], svb[BB, 1, :, :], ACT.Copy).then_inc(A.sem, 1)
                        decays(0)
                        left_a(0)
                        turns_of(act, body)

                    @block.vector
                    def _(dve):
                        def mask(name, rows, n):
                            return C(name)[rows, 0:n].unsqueeze(1).to_broadcast([64, 4, n])

                        def did(c, steps, ins, name):
                            ins.then_inc(steps.sem, 1)
                            dve.wait_ge(steps.sem, at(c, steps, name))

                        def stage(n, name):
                            rows = AA if name[-1] == "a" else BB
                            u = (au, tile_k) if name[-1] == "a" else (tile_k, au)
                            if name == "at":
                                dve.wait_ge(A0.sem, at(n, A0, "E"))
                                ins = dve.scalar_tensor_tensor(stg[:, :, 0, :], chunk(kk, n), -1.0, e65[:, :, 0:CH], ALU.mult, ALU.mult)
                            elif name == "rt":
                                ins = dve.tensor_tensor(stg[:, :, 1, :], chunk(tile_r, n), e65[:, :, 1:CH + 1], ALU.mult)
                            else:
                                if name == "u2a":
                                    dve.wait_ge(A0.sem, at(n, A0, "Ei"))
                                slot = int(name[1])
                                ins = dve.tensor_tensor(stg[rows, :, slot, :], chunk(u[slot - 2], n)[rows], ei[rows, :, :], ALU.mult)
                            did(n, W0, ins, name)

                        def powers(n, q, which):
                            slot, m, name = {"d": (0, 0, "diag"), "t": (1, 1, "diag_t"), "o": (2, 1, "off_t")}[which]
                            for rows, y, off in ((AA, "A", 0), (BB, "B", 64)):
                                src = ps[rows, 4 * q + (off > 0), :].rearrange("p (a m b) -> p a m b", a=4, m=2)[:, :, m, :]
                                did(n, W1, dve.tensor_tensor(blocks(sl[rows, q, slot, :])[:, :, off:off + 64], src,
                                                             mask(name, rows, 64), ALU.mult), f"{which}{y}{q}")

                        def plus_one(n, q):
                            did(n, W1, dve.tensor_tensor(blocks(sl[:, q, 3, :]), blocks(sl[:, q, 0, :]),
                                                         C("ident").unsqueeze(1).to_broadcast([128, 4, 128]), ALU.add), f"x1{q}")

                        def rights(n, q):
                            for y, b in (("A", 2), ("B", 3)):
                                did(n, W1, dve.tensor_tensor(gr[:, b - 2, 4 * q:4 * q + 4, :], blocks(ps[:, 4 * q + b, :])[:, :, 64:128],
                                                             C("gram")[:, 64:128].unsqueeze(1).to_broadcast([128, 4, 64]), ALU.mult), f"g{y}{q}")

                        def lefts(n, q):
                            for y, b, rows in (("A", 2, BB), ("B", 3, AA)):
                                did(n, W1, dve.tensor_tensor(qa[rows, b - 2, 4 * q:4 * q + 4, :], blocks(ps[rows, 4 * q + b, :])[:, :, 0:64],
                                                             mask("gram", rows, 64), ALU.mult), f"k{y}{q}")

                        def body(c, last):
                            def did_(ins, name):
                                did(c, W, ins, name)

                            def both(name, need, fn):
                                for q in range(2):
                                    dve.wait_ge(P.sem, at(c, P, f"{need}{q}"))
                                    did_(fn(q), f"{name}{q}")
                            out = lambda q, b: ps[:, 4 * q + b, :]

                            def next_stage(name):
                                if not last:
                                    stage(c + 1, name)
                            dve.wait_ge(P0.sem, at(c, P0, "mg1"))
                            for x in "dto":
                                powers(c, 1, x)
                            plus_one(c, 1)
                            dve.wait_ge(P.sem, at(c, P, "D20"))
                            did_(dve.tensor_copy(sl[:, 0, 4, :], out(0, 0)), "D20")
                            rights(c, 1)
                            lefts(c, 1)
                            dve.wait_ge(P.sem, at(c, P, "D21"))
                            did_(dve.tensor_copy(sl[:, 1, 4, :], out(1, 0)), "D21")
                            both("X2", "DX", lambda q: dve.tensor_tensor(sl[:, q, 3, :], out(q, 1), sl[:, q, 3, :], ALU.add))
                            dve.wait_ge(G.sem, at(c, G, "rc"))
                            next_stage("at")
                            both("XD", "DXX", lambda q: dve.tensor_tensor(sl[:, q, 3, :], out(q, 0), sl[:, q, 3, :], ALU.add))
                            next_stage("rt")
                            for q in range(2):
                                dve.wait_ge(P.sem, at(c, P, f"N{q}"))
                                did_(dve.tensor_copy(sl[:, q, 0, :], out(q, 0)), f"N{q}")
                                did_(dve.tensor_tensor(blocks(sl[:, q, 5, :]), blocks(sl[:, q, 0, :]),
                                                       C("ident").unsqueeze(1).to_broadcast([128, 4, 128]), ALU.add), f"Y1{q}")
                            next_stage("u2a")
                            both("N2", "N2", lambda q: dve.tensor_copy(sl[:, q, 2, :], out(q, 1)))
                            next_stage("u3a")
                            both("Y2", "NY", lambda q: dve.tensor_tensor(sl[:, q, 5, :], out(q, 1), sl[:, q, 5, :], ALU.add))
                            next_stage("u2b")
                            both("Y3", "NYY", lambda q: dve.tensor_tensor(sl[:, q, 5, :], out(q, 0), sl[:, q, 5, :], ALU.add))
                            next_stage("u3b")
                            if not last:
                                dve.wait_ge(P0.sem, at(c + 1, P0, "mg0"))
                                for x in "dt":
                                    powers(c + 1, 0, x)
                            dve.wait_ge(P.sem, at(c, P, "sa"))
                            did_(dve.tensor_copy(zb[BB, 1, :, :], ps[BB, 7, :]), "zb")
                            if not last:
                                powers(c + 1, 0, "o")
                                plus_one(c + 1, 0)
                                lefts(c + 1, 0)
                                dve.wait_ge(P.sem, at(c, P, "y"))
                                rights(c + 1, 0)
                            dve.wait_ge(P.sem, at(c, P, "s"))
                            halves = ((AA, 0, "A"), (BB, 1, "B"))
                            for rows, x, y in halves:
                                did_(dve.tensor_tensor(svb[rows, x, :, :], ps[rows, 5, :].rearrange("p (a b) -> p a b", a=RT),
                                                       svb[rows, x, :, :], ALU.add), f"s{y}")
                            for rows, x, y in halves:
                                did_(dve.tensor_tensor(svb[rows, x, :, :], svb[rows, x, :, :],
                                                       wl[rows, :, :].to_broadcast([64, RT, CH]), ALU.mult), f"sw{y}")
                            dve.wait_ge(A.sem, at(c, A, "sd_b"))
                            dve.sem_inc(turn_ok, 1)

                        for name in W0.names:
                            stage(0, name)
                        dve.wait_ge(P0.sem, P0.at("mg0"))
                        for x in "dto":
                            powers(0, 0, x)
                        plus_one(0, 0)
                        lefts(0, 0)
                        rights(0, 0)
                        turns_of(dve, body)

                    @block.tensor
                    def _(pe):
                        def grams(q):
                            for n in range(4):
                                j = 4 * q + n
                                for rows, b in ((AA, 2), (BB, 3)):
                                    pe.matmul(ps[:, 4 * q + b, n * 128:n * 128 + 128], stg[rows, j, 2:4, :], stg[rows, j, 0:2, :],
                                              start=True, stop=True)
                                for rows, unit, b in ((AA, 2, 0), (BB, 3, 1)):
                                    pe.matmul(ps[rows, 4 * q + b, n * 128:n * 128 + 64], stg[rows, j, unit, :], stg[rows, j, 0, :],
                                              start=True, stop=True)
                                    mm = pe.matmul(ps[rows, 4 * q + b, n * 128 + 64:n * 128 + 128], stg[rows, j, 0, :],
                                                   stg[rows, j, unit, :], start=True, stop=True)
                            mm.then_inc(P0.sem, 1)

                        def four(q, b, left, right):
                            for n in range(4):
                                ns = slice(n * 128, n * 128 + 128)
                                mm = pe.matmul(ps[:, 4 * q + b, ns], sl[:, q, left, ns], sl[:, q, right, ns], start=True, stop=True)
                            mm.then_inc(P.sem, 1)

                        def heads(b, left, right):
                            for j in range(RT):
                                for rows, x in ((AA, 0), (BB, 1)):
                                    mm = pe.matmul(ps[rows, b, j * 64:j * 64 + 64], left(x, j), right(x, j), start=True, stop=True)
                            mm.then_inc(P.sem, 1)

                        def body(c, last):
                            pe.wait_ge(W1.sem, at(c, W1, "x10"))
                            four(0, 0, 1, 0)
                            four(0, 1, 0, 1)
                            pe.wait_ge(W1.sem, at(c, W1, "gB0"))
                            for j in range(RT):
                                mm = pe.transpose(ps[:, 2 + j // 4, j % 4 * 128:j % 4 * 128 + 128], stg[:, j, 2:4, :], C("ident"))
                            mm.then_inc(P.sem, 1)
                            pe.wait_ge(W1.sem, at(c, W1, "x11"))
                            four(1, 0, 1, 0)
                            four(1, 1, 0, 1)
                            for q in range(2):
                                pe.wait_ge(W.sem, at(c, W, f"D2{q}"))
                                pe.wait_ge(A.sem, at(c, A, f"D2t{q}"))
                                four(q, 0, 4, 5)
                                four(q, 1, 5, 3)
                            pe.wait_ge(W1.sem, at(c, W1, "kB1"))
                            pe.wait_ge(G.sem, at(c, G, "vst"))
                            for j in range(RT):
                                mm = pe.transpose(ps[:, 6 + j // 4, j % 4 * 128:j % 4 * 128 + 128], vst[:, j, :, :], C("ident"))
                            mm.then_inc(P.sem, 1)
                            for q in range(2):
                                pe.wait_ge(A.sem, at(c, A, f"D4t{q}"))
                                pe.wait_ge(W.sem, at(c, W, f"X2{q}"))
                                four(q, 0, 0, 3)
                            for q in range(2):
                                pe.wait_ge(W.sem, at(c, W, f"XD{q}"))
                                four(q, 0, 2, 3)
                                four(q, 1, 3, 2)
                            for q in range(2):
                                pe.wait_ge(W.sem, at(c, W, f"N{q}"))
                                for n in range(4):
                                    ns = slice(n * 128, n * 128 + 128)
                                    mm = pe.transpose(ps[:, 4 * q, ns], sl[:, q, 3, ns], C("ident"))
                                mm.then_inc(P.sem, 1)
                            for q in range(2):
                                pe.wait_ge(A.sem, at(c, A, f"Nt{q}"))
                                four(q, 1, 1, 0)
                                pe.wait_ge(A.sem, at(c, A, f"XDt{q}"))
                                four(q, 0, 0, 1)
                            for q in range(2):
                                pe.wait_ge(W.sem, at(c, W, f"N2{q}"))
                                pe.wait_ge(A.sem, at(c, A, f"N2t{q}"))
                                four(q, 0, 2, 3)
                                four(q, 1, 3, 5)
                            for q in range(2):
                                pe.wait_ge(A.sem, at(c, A, f"N4t{q}"))
                                pe.wait_ge(W.sem, at(c, W, f"Y2{q}"))
                                four(q, 0, 0, 5)
                            for q in range(2):
                                pe.wait_ge(W.sem, at(c, W, f"Y3{q}"))
                                four(q, 1, 4, 5)
                            pe.wait_ge(A0.sem, at(c, A0, "qa_b"))
                            pe.wait_ge(A.sem, at(c, A, "v4"))
                            pe.wait_ge(turn_ok, c + 1)
                            heads(6, lambda x, j: qa[:, x, j, :], lambda x, j: svb[:, x, j, :])
                            if not last:
                                pe.wait_ge(A.sem, at(c, A, "X0"))
                                pe.wait_ge(W0.sem, at(c + 1, W0, "u3b"))
                                grams(0)
                            pe.wait_ge(A.sem, at(c, A, "rhs"))
                            for j in range(RT):
                                mm = pe.matmul(ps[:, 7, j * 64:j * 64 + 64], xs[:, j, :], rh[:, j, :], start=True, stop=True)
                            mm.then_inc(P.sem, 1)
                            pe.wait_ge(A.sem, at(c, A, "za"))
                            pe.wait_ge(W.sem, at(c, W, "zb"))
                            for j in range(RT):
                                js = slice(j * 64, j * 64 + 64)
                                pe.matmul(ps[:, 4, js], sbd[:, j, :], rc[:, j, :], start=True, stop=False, skip_group_check=True)
                                for rows, x in ((AA, 0), (BB, 1)):
                                    mm = pe.matmul(ps[rows, 4, js], zb[:, x, j, :], gr[:, x, j, :], start=False, stop=True,
                                                   skip_group_check=True)
                            mm.then_inc(P.sem, 1)
                            heads(5, lambda x, j: bk[:, j, 64 * x:64 * x + 64], lambda x, j: zb[:, x, j, :])
                            if not last:
                                pe.wait_ge(A.sem, at(c, A, "y"))
                                pe.wait_ge(W.sem, at(c, W, "sB"))
                                grams(1)
                        pe.wait_ge(W0.sem, W0.at("u3b"))
                        for q in range(2):
                            grams(q)
                        turns_of(pe, body)

                wkv_out = sem("wkv_out")
                with nc.Block() as block:
                    @block.sync
                    def _(sp):
                        for rows, x in ((AA, 0), (BB, 1)):
                            sp.dma_start(wkv_p[rows], svb[rows, x, :, :]).then_inc(wkv_out, 16)
                        sp.wait_ge(wkv_out, 32)

            with ExitStack() as st:
                sq = sb(st, "y_sq", [128, 2, TOK])
                rn = sb(st, "y_rms", [128, RT, TOK])
                bv = sb(st, "bonus", [128, RT, TOK])
                J = range(RT)
                J = range(RT)
                P = Steps(sem("gn_pe"), [f"{x}{j - d}" for j in range(RT + 1) for x, d in (("mean", 0), ("var", 1)) if 0 <= j - d < RT]
                          + [f"{x}{j}" for x in ("bon", "gate") for j in J])
                A = Steps(sem("gn_act"), [f"{x}{j}" for x in ("sq", "ln", "rt") for j in J])
                W = Steps(sem("gn_dve"), [f"{x}{j - d}" for j in range(RT + 1) for xs_, d in ((("c0_", "c1_"), 0), (("m0_", "m1_"), 1))
                                          for x in xs_ if 0 <= j - d < RT] + [f"{x}{j}" for j in J for x in ("bv0_", "bv1_")]
                          + [f"{x}{j}" for j in J for x in ("n", "add", "o0_", "o1_")])
                y_out = sem("yr_out")
                with nc.Block() as block:
                    @block.tensor
                    def _(pe):
                        def summed(j, part, left, right):
                            for i, (a, m) in enumerate(SPANS):
                                mm = pe.matmul(ps[:, 4 * (j % 2) + 2 * part + i, 0:m], left, right[:, a:a + m], start=True, stop=True)
                            mm.then_inc(P.sem, 1)
                        for j in range(RT + 1):
                            if j < RT:
                                if j >= 2:
                                    pe.wait_ge(W.sem, W.at(f"c1_{j - 2}"))
                                summed(j, 0, C("pair"), tile_r[:, j, :])
                            if j:
                                pe.wait_ge(A.sem, A.at(f"sq{j - 1}"))
                                if j >= 3:
                                    pe.wait_ge(W.sem, W.at(f"m1_{j - 3}"))
                                summed(j - 1, 1, C("pair"), sq[:, (j - 1) % 2, :])
                        for j in J:
                            pe.wait_ge(W.sem, W.at(f"bv1_{j - 2}") if j >= 2 else W.at(f"c1_{RT - 1}"))
                            summed(j, 0, C("pair"), au[:, j, :])
                        for j in J:
                            pe.wait_ge(W.sem, W.at(f"o1_{j - 2}") if j >= 2 else W.at(f"m1_{RT - 1}"))
                            summed(j, 1, g2s[:, j * 128:(j + 1) * 128], rkv[:, 25, :])

                    @block.scalar
                    def _(act):
                        for j in J:
                            act.wait_ge(W.sem, W.at(f"c1_{j}"))
                            if j >= 2:
                                act.wait_ge(P.sem, P.at(f"var{j - 2}"))
                            act.activation(sq[:, j % 2, :], tile_r[:, j, :], ACT.Square).then_inc(A.sem, 1)
                        for j in J:
                            act.wait_ge(W.sem, W.at(f"m1_{j}"))
                            act.activation(rn[:, j, :], rn[:, j, :], ACT.Ln).then_inc(A.sem, 1)
                        for j in J:
                            act.wait_ge(A.sem, A.at(f"ln{j}"))
                            act.activation(rn[:, j, :], rn[:, j, :], ACT.Exp, scale=-0.5).then_inc(A.sem, 1)

                    @block.vector
                    def _(dve):
                        def did(ins, name):
                            ins.then_inc(W.sem, 1)
                            dve.wait_ge(W.sem, W.at(name))
                        for j in range(RT + 1):
                            if j < RT:
                                dve.wait_ge(P.sem, P.at(f"mean{j}"))
                                for i, (a, m) in enumerate(SPANS):
                                    dve.scalar_tensor_tensor(tile_r[:, j, a:a + m], ps[:, 4 * (j % 2) + i, 0:m], -1.0 / 64,
                                                             tile_r[:, j, a:a + m], ALU.mult, ALU.add).then_inc(W.sem, 1)
                            if j:
                                dve.wait_ge(P.sem, P.at(f"var{j - 1}"))
                                for i, (a, m) in enumerate(SPANS):
                                    dve.tensor_scalar(rn[:, j - 1, a:a + m], ps[:, 4 * ((j - 1) % 2) + 2 + i, 0:m], 1.0 / 64, 64e-5,
                                                      ALU.mult, ALU.add).then_inc(W.sem, 1)
                        for j in J:
                            dve.wait_ge(P.sem, P.at(f"bon{j}"))
                            for i, (a, m) in enumerate(SPANS):
                                dve.tensor_tensor(bv[:, j, a:a + m], ps[:, 4 * (j % 2) + i, 0:m], tile_v[:, j, a:a + m], ALU.mult).then_inc(W.sem, 1)
                        for j in J:
                            dve.wait_ge(A.sem, A.at(f"rt{j}"))
                            did(dve.scalar_tensor_tensor(tile_r[:, j, :], tile_r[:, j, :], V("lnx_g", j), rn[:, j, :], ALU.mult, ALU.mult), f"n{j}")
                            did(dve.scalar_tensor_tensor(tile_r[:, j, :], tile_r[:, j, :], V("lnx_b", j), bv[:, j, :], ALU.add, ALU.add), f"add{j}")
                            dve.wait_ge(P.sem, P.at(f"gate{j}"))
                            for i, (a, m) in enumerate(SPANS):
                                dve.tensor_tensor(tile_r[:, j, a:a + m], ps[:, 4 * (j % 2) + 2 + i, 0:m], tile_r[:, j, a:a + m],
                                                  ALU.mult).then_inc(W.sem, 1)

                    @block.sync
                    def _(sp):
                        for j in range(RT):
                            sp.wait_ge(W.sem, W.at(f"o1_{j}"))
                            sp.dma_start(ymix[j, :, :], tile_r[:, j, :]).then_inc(y_out, 16)
                        sp.wait_ge(y_out, 16 * RT)

        x = sb(stack, "x", [128, KT, TOK])
        mixed = ExitStack()
        y = sb(mixed, "y_mix", [128, KT, TOK])
        y_in = sem("y_in")
        with ExitStack() as st:
            mkb = sb(st, "mk", [128, KT, MEM])
            mvb = sb(st, "mv", [128, 2, D])
            memx = mvb[:, :, :].rearrange("p a (b c) -> p (a b) c", c=MEM)
            mh = sb(st, "mem_hi", [128, KT, MEM], f32r)
            ml = sb(st, "mem_lo", [128, KT, MEM], f32r)
            whi = sb(st, "whi_b", [128, 2, BLK], f32r)
            wlo = sb(st, "wlo_b", [128, 2, BLK], f32r)
            rstd = sb(st, "rstd_mem", [128, MEM])
            sq = sb(st, "sq_b", [128, 2, MEM])
            rcol = sb(st, "rstd_col", [128, 2])
            mem_in, mem_out, mv_out, col_done = sem("mem_in"), sem("mem_out"), sem("mv_out"), sem("col_done")
            with nc.Block() as block:
                @block.sync
                def _(sp):
                    sp.dma_start(memx, memt.rearrange("k p n -> p k n")).then_inc(mem_in, 16)
                    sp.wait_ge(mem_in, 16)

            def evac_ck(dve, i, u, t):
                dve.tensor_tensor(tile_of(mkb, i), ps[:, 2 * u, 0:MEM], rstd[:, :], ALU.mult).then_inc(out_done, 1)

            project("ck", CK0, KT, mh, ml, whi, wlo, [(0, MEM)], evac_ck, memx, "g_mem", (rstd, sq))

            j0 = jobs[0]
            jobs[0] += 4
            with nc.Block() as block:
                @block.sync
                def _(sp):
                    sp.dma_start(mk_o.rearrange("k p n -> p k n"), mkb[:, :, :]).then_inc(mem_out, 16)
                    with sp.Fori(0, 8) as t:
                        for u in range(2):
                            load_block(sp, t * 2 + (CV0 + u), u)

                @block.scalar
                def _(act):
                    act.wait_ge(col_done, 1)
                    act.activation(rcol[:, :], ps[:, 6, 0:2], ACT.Copy).then_inc(col_done, 1)
                    with act.Fori(0, 8) as t:
                        for u in range(2):
                            weight_hi(act, whi, t * 2 + (CV0 + u), u, t + CV0 // 2)

                @block.vector
                def _(dve):
                    dve.wait_ge(col_done, 2)
                    with dve.Fori(0, 2) as t:
                        for n in range(2):
                            for k in range(4):
                                weight_lo(dve, whi, wlo, t * 8 + (CV0 + 4 * n + k), k % 2)
                            dve.wait_ge(pe_done, t * 8 + (CV0 + 4 * n + 3 + 3))
                            for m in range(2):
                                ins = dve.tensor_scalar(mvb[:, m, bass.ds((t * 2 + n) * 512, 512)], ps[:, 2 * n + m, :],
                                                        rcol[:, m:m + 1], None, ALU.mult)
                            ins.then_inc(out_done, 1)

                @block.gpsimd
                def _(pool):
                    for i in range(8):
                        k = i % 4 * 4
                        pool.wait_ge(wlo_done, CV0 + 1 + i)
                        to, source = ((y, ymix), (x, xt))[i // 4]
                        pool.dma_start(to[:, k:k + 4, :], source[k:k + 4, :, :].rearrange("k p n -> p k n")).then_inc(y_in, 16)
                    for g in range(4):
                        pool.wait_ge(out_done, j0 + g + 3)
                        gs = slice(512 * g, 512 * g + 512)
                        pool.dma_start(mv_o.rearrange("m p n -> p m n")[:, :, gs], mvb[:, :, gs]).then_inc(mv_out, 16)

                @block.tensor
                def _(pe):
                    for m in range(2):
                        mm = pe.matmul(ps[:, 6, m:m + 1], rstd[0:1, m * 128:m * 128 + 128], C("ones")[0:1, 0:1], start=True, stop=True)
                    mm.then_inc(col_done, 1)
                    with pe.Fori(0, 2) as t:
                        for n in range(2):
                            pe.wait_ge(out_done, t * 2 + (j0 + n + 1))
                            for k4 in range(4):
                                pe.wait_ge(wlo_done, t * 8 + (CV0 + 4 * n + k4 + 1))
                                for k in range(4):
                                    for at, wt in ((mh, whi), (mh, wlo), (ml, whi)):
                                        for m in range(2):
                                            mm = pe.matmul(ps[:, 2 * n + m, :], at[:, 4 * k4 + k, m * 128:m * 128 + 128],
                                                           wt[:, k4 % 2, k * 512:k * 512 + 512],
                                                           start=(k4 == 0 and k == 0 and at is mh and wt is whi),
                                                           stop=(k4 == 3 and k == 3 and at is ml))
                                mm.then_inc(pe_done, 1)

            with nc.Block() as block:
                @block.sync
                def _(sp):
                    sp.wait_ge(mem_out, 16)
                    sp.wait_ge(mv_out, 64)

        def add_to_x(dve, i, u, t):
            for s, (a, m) in enumerate(SPANS):
                if isinstance(i, int):
                    xi = x[:, i, a:a + m]
                else:
                    xi = x[:, bass.ds(i, 1), a:a + m].rearrange("p o n -> p (o n)")
                ins = dve.tensor_tensor(xi, ps[:, 2 * u + s, 0:m], xi, ALU.add)
            ins.then_inc(out_done, 1)

        late = ExitStack()
        with ExitStack() as st:
            ah = sb(st, "y_hi", [128, KT, TOK], f32r)
            al = sb(st, "y_lo", [128, KT, TOK], f32r)
            whi = sb(st, "whi_c", [128, 2, BLK], f32r)
            wlo = sb(st, "wlo_c", [128, 2, BLK], f32r)
            with nc.Block() as block:
                @block.sync
                def _(sp):
                    sp.wait_ge(y_in, 128)
            project("wo", WO0, KT, ah, al, whi, wlo, SPANS, add_to_x, y)
        mixed.close()

        qc = sb(late, "qc", [128, KT, TOK])
        with ExitStack() as st:
            ah = sb(st, "hx_hi", [128, KT, TOK], f32r)
            al = sb(st, "hx_lo", [128, KT, TOK], f32r)
            whi = sb(st, "whi_d", [128, 2, BLK], f32r)
            wlo = sb(st, "wlo_d", [128, 2, BLK], f32r)
            rstd = sb(st, "rstd_x", [128, TOK])
            sq = sb(st, "sq_d", [128, 2, TOK])

            def evac_q(dve, i, u, t):
                for s, (a, m) in enumerate(SPANS):
                    qi = qc[:, i, a:a + m] if isinstance(i, int) else qc[:, bass.ds(i, 1), a:a + m].rearrange("p o n -> p (o n)")
                    ins = dve.tensor_tensor(qi, ps[:, 2 * u + s, 0:m], rstd[:, a:a + m], ALU.mult)
                ins.then_inc(out_done, 1)
            project("cq", CQ0, KT, ah, al, whi, wlo, SPANS, evac_q, x, "g_cross", (rstd, sq))

        XS = XD ** -0.5
        with ExitStack() as st:
            mkb = sb(st, "mk2", [128, KT, MEM])
            mvb = sb(st, "mv2", [128, 2, D])
            ex = sb(st, "x_exp", [128, 2, MEM])
            xT = sb(st, "x_exp_T", [128, 2, 2, SEQ])
            mxs = sb(st, "x_max", [128, 2])
            nmx = sb(st, "x_neg", [128, 2])
            rs = sb(st, "x_sum", [128, 2])
            ri = sb(st, "x_inv", [128, 2])
            units = [(h, i) for h in range(XH) for i in range(4)]
            mkv_in = sem("mkv_in")
            P = Steps(sem("xp_pe"), ["s00"] + [y for n, (h, i) in enumerate(units) for y in
                      ([f"s{units[n + 1][0]}{units[n + 1][1]}"] if n < 15 else []) + [f"t{h}{i}"]
                      + ([f"o{h}{e}" for e in range(4)] if i == 3 else [])])
            A = Steps(sem("xp_act"), [y for h, i in units for y in [f"e{h}{i}", f"t{h}{i}"] + ([f"o{h}{e}" for e in range(4)] if i == 3 else [])])
            W = Steps(sem("xp_dve"), [f"{y}{h}{i}" for h, i in units for y in ("max", "neg", "inv", "w")])
            with nc.Block() as block:
                @block.sync
                def _(sp):
                    sp.dma_start(mkb[:, :, :], mk_o.rearrange("k p n -> p k n")).then_inc(mkv_in, 16)
                    sp.dma_start(mvb[:, :, :], mv_o.rearrange("m p n -> p m n")).then_inc(mkv_in, 16)

                @block.tensor
                def _(pe):
                    def scores(n):
                        h, i = units[n]
                        if n >= 2:
                            pe.wait_ge(A.sem, A.at("e%d%d" % units[n - 2]))
                        for e in range(4):
                            mm = pe.matmul(ps[:, n % 2, 0:MEM], qc[:, 4 * h + e, i * 128:i * 128 + 128], mkb[:, 4 * h + e, :],
                                           start=(e == 0), stop=(e == 3))
                        mm.then_inc(P.sem, 1)
                    pe.wait_ge(mkv_in, 32)
                    scores(0)
                    for n, (h, i) in enumerate(units):
                        if n < 15:
                            scores(n + 1)
                        pe.wait_ge(W.sem, W.at(f"w{h}{i}"))
                        if n >= 2:
                            pe.wait_ge(A.sem, A.at("t%d%d" % units[n - 2]))
                        for m in range(2):
                            mm = pe.transpose(ps[:, 2 + n % 2, m * 128:m * 128 + 128], ex[:, n % 2, m * 128:m * 128 + 128], C("ident"))
                        mm.then_inc(P.sem, 1)
                        if i == 3:
                            pe.wait_ge(A.sem, A.at(f"t{h}3"))
                            for e in range(4):
                                if h:
                                    pe.wait_ge(A.sem, A.at(f"o{h - 1}{e}"))
                                for m in range(2):
                                    mm = pe.matmul(ps[:, 4 + e, :], mvb[:, m, (4 * h + e) * 128:(4 * h + e) * 128 + 128],
                                                   xT[:, h % 2, m, :], start=(m == 0), stop=(m == 1))
                                mm.then_inc(P.sem, 1)

                @block.scalar
                def _(act):
                    for n, (h, i) in enumerate(units):
                        act.wait_ge(W.sem, W.at(f"neg{h}{i}"))
                        act.activation(ex[:, n % 2, :], ps[:, n % 2, 0:MEM], ACT.Exp, bias=nmx[:, n % 2:n % 2 + 1], scale=XS,
                                       accum_out=rs[:, n % 2:n % 2 + 1]).then_inc(A.sem, 1)
                        act.wait_ge(P.sem, P.at(f"t{h}{i}"))
                        act.activation(xT[:, h % 2, :, i * 128:i * 128 + 128], ps[:, 2 + n % 2, 0:256].rearrange("p (a b) -> p a b", a=2),
                                       ACT.Copy).then_inc(A.sem, 1)
                        if i == 3:
                            for e in range(4):
                                act.wait_ge(P.sem, P.at(f"o{h}{e}"))
                                act.activation(qc[:, 4 * h + e, 0:SEQ], ps[:, 4 + e, :], ACT.Copy).then_inc(A.sem, 1)

                @block.vector
                def _(dve):
                    def did(ins, name):
                        ins.then_inc(W.sem, 1)
                        dve.wait_ge(W.sem, W.at(name))
                    for n, (h, i) in enumerate(units):
                        b = slice(n % 2, n % 2 + 1)
                        dve.wait_ge(P.sem, P.at(f"s{h}{i}"))
                        did(dve.reduce_max(mxs[:, b], ps[:, n % 2, 0:MEM], AX.X), f"max{h}{i}")
                        if n >= 2:
                            dve.wait_ge(P.sem, P.at("t%d%d" % units[n - 2]))
                        did(dve.tensor_scalar(nmx[:, b], mxs[:, b], -XS, None, ALU.mult), f"neg{h}{i}")
                        dve.wait_ge(A.sem, A.at(f"e{h}{i}"))
                        did(dve.reciprocal(ri[:, b], rs[:, b]), f"inv{h}{i}")
                        did(dve.tensor_scalar(ex[:, n % 2, :], ex[:, n % 2, :], ri[:, b], None, ALU.mult), f"w{h}{i}")

        with ExitStack() as st:
            ring = sb(st, "mem_ring", [128, 2, KT * MEM])
            qz = sb(st, "x_q_columns", [128, NS, KT * XH])
            cur = sb(st, "x_standing", [128, 2, KT * XH])
            rows = sb(st, "x_rows_out", [XH, 2, D])
            sc = sb(st, "x_scores", [NS * XH, MEM])
            col = sb(st, "x_softmax_cols", [NS * XH, 4])
            m1, nm, part, inv = [col[:, i:i + 1] for i in range(4)]
            scale_ = sb(st, "x_scale", [NS * XH, NS * XH])
            ws = sb(st, "x_weights", [128, 2, NS * XH])
            oT = sb(st, "x_out_rows", [NS * XH, XD])
            mem_c_in = [sem("mem_c_in0"), sem("mem_c_in1")]
            mem_c_used = sem("mem_c_used")
            cols_out = sem("cols_out")
            cur_in = sem("x_standing_in")
            row_out = sem("x_row_out")
            row_free = sem("x_row_free")
            q_ready = sem("x_q_ready")
            rows_in = sem("x_rows_in")
            with nc.Block() as block:
                @block.tensor
                def _(pe):
                    pe.sem_inc(mem_c_used, 2)

                @block.gpsimd
                def _(pool):
                    pool.sem_inc(row_free, 2)

                @block.vector
                def _(dve):
                    dve.sem_inc(cols_out, 2)
                    dve.memset(qz[:, :, :], 0.0).then_inc(q_ready, 1)
                    dve.wait_ge(q_ready, 1)
                    for h in range(XH):
                        at = 4 * h * XH + h
                        dve.tensor_copy(qz[:, :, at:at + 3 * XH + 1:XH],
                                        qc[:, 4 * h:4 * h + 4, SEQ:TOK].rearrange("p e b -> p b e")).then_inc(q_ready, 1)

            def memory_pass(cache, b0, operands, product, summed, store_to, store_from):
                with nc.Block() as block:
                    @block.sync
                    def _(sp):
                        with sp.Fori(0, NS // 2) as t:
                            for u in range(2):
                                sp.wait_ge(mem_c_used, t * 2 + (b0 + u + 1))
                                sp.dma_start(ring[:, u, :], cache[bass.ds(t * 2 + u, 1), :, :, :].rearrange("o p a b -> p (o a b)"))\
                                  .then_inc(mem_c_in[u], 16)

                    @block.tensor
                    def _(pe):
                        with pe.Fori(0, NS // 2) as t:
                            for u in range(2):
                                pe.wait_ge(cols_out, t * 2 + (b0 + u + 1))
                                pe.wait_ge(cur_in, t * 2 + (b0 + u + 1))
                                pe.wait_ge(mem_c_in[u], t * 16 + (b0 * 8 + 16))
                                product(pe, u).then_inc(mem_c_used, 1)

                    @block.scalar
                    def _(act):
                        with act.Fori(0, NS // 2) as t:
                            for u in range(2):
                                act.wait_ge(mem_c_used, t * 2 + (b0 + u + 1))
                                dst, src = operands(t * 2 + u, u)
                                act.activation(dst, src, ACT.Copy).then_inc(cur_in, 1)

                    @block.vector
                    def _(dve):
                        with dve.Fori(0, NS // 2) as t:
                            for u in range(2):
                                dve.wait_ge(mem_c_used, t * 2 + (b0 + u + 3))
                                dve.wait_ge(row_free, t * 2 + (b0 + u + 1))
                                dve.tensor_copy(store_from(u), summed(u)).then_inc(cols_out, 1)

                    @block.gpsimd
                    def _(pool):
                        with pool.Fori(0, NS // 2) as t:
                            for u in range(2):
                                pool.wait_ge(cols_out, t * 2 + (b0 + u + 3))
                                pool.dma_start(store_to(t * 2 + u), store_from(u)).then_inc(row_out, 16)
                                pool.wait_ge(row_out, t * 32 + 16 * (b0 + u + 1))
                                pool.sem_inc(row_free, 1)

            def score_operands(b, u):
                return cur[:, u, :], qz[:, bass.ds(b, 1), :].rearrange("p o n -> p (o n)")

            def score_product(pe, u):
                for k in range(KT):
                    mm = pe.matmul(ps[0:XH, 4 * u, 0:MEM], cur[:, u, k * XH:k * XH + XH], ring[:, u, k * MEM:(k + 1) * MEM],
                                   start=(k == 0), stop=(k == KT - 1))
                return mm

            memory_pass(mkc, 0, score_operands, score_product, lambda u: ps[0:XH, 4 * u, 0:MEM],
                        lambda b: xsrow[bass.ds(b, 1), :, :].rearrange("o r n -> (o r) n"), lambda u: rows[:, u, 0:MEM])
            S = Steps(sem("xs_soft"), ["m1", "nm", "exp", "inv", "scale", "mm", "ws"])
            with nc.Block() as block:
                @block.sync
                def _(sp):
                    sp.dma_start(sc[:, :], xsrow.rearrange("b r n -> (b r) n")).then_inc(rows_in, 16)

                @block.tensor
                def _(pe):
                    pe.wait_ge(S.sem, S.at("scale"))
                    for m in range(2):
                        mm = pe.matmul(ps[:, 4, m * 32:m * 32 + 32], sc[:, m * 128:m * 128 + 128], scale_[:, :], start=True, stop=True)
                    mm.then_inc(S.sem, 1)

                @block.scalar
                def _(act):
                    act.wait_ge(S.sem, S.at("nm"))
                    act.activation(sc[:, :], sc[:, :], ACT.Exp, bias=nm, scale=XS, accum_out=part).then_inc(S.sem, 1)

                @block.vector
                def _(dve):
                    def did(ins, name):
                        ins.then_inc(S.sem, 1)
                        dve.wait_ge(S.sem, S.at(name))
                    dve.wait_ge(rows_in, 16)
                    did(dve.reduce_max(m1, sc[:, :], AX.X), "m1")
                    did(dve.tensor_scalar(nm, m1, -XS, None, ALU.mult), "nm")
                    dve.wait_ge(S.sem, S.at("exp"))
                    did(dve.reciprocal(inv, part), "inv")
                    did(dve.tensor_scalar(scale_[:, :], C("ident")[0:32, 0:32], inv, None, ALU.mult), "scale")
                    dve.wait_ge(S.sem, S.at("mm"))
                    did(dve.tensor_copy(ws[:, :, :].rearrange("p a b -> p (a b)"), ps[:, 4, 0:64]), "ws")

            def value_operands(b, u):
                return (cur[:, u, 0:2 * XH].rearrange("p (a b) -> p a b", a=2), ws[:, :, bass.ds(b * XH, XH)])

            def value_product(pe, u):
                for m in range(2):
                    for n in range(4):
                        mm = pe.matmul(ps[0:XH, 4 * u + n, :], cur[:, u, m * XH:m * XH + XH],
                                       ring[:, u, m * D + n * 512:m * D + n * 512 + 512], start=(m == 0), stop=(m == 1))
                return mm

            memory_pass(mvc, NS, value_operands, value_product,
                        lambda u: ps[0:XH, 4 * u:4 * u + 4, :].rearrange("p a b -> p (a b)"),
                        lambda b: xorow[bass.ds(b, 1), 0:XH * D].rearrange("o (h n) -> (o h) n", n=D), lambda u: rows[:, u, :])
            own = xorow.rearrange("b (h m) -> (b h) m", m=D + XD)[:, 0:XD]
            with nc.Block() as block:
                @block.sync
                def _(sp):
                    sp.dma_start(oT[:, :], own).then_inc(rows_in, 16)

                @block.tensor
                def _(pe):
                    pe.wait_ge(rows_in, 32)
                    for e in range(4):
                        mm = pe.transpose(ps[:, 4, e * 32:e * 32 + 32], oT[:, e * 128:e * 128 + 128], C("ident")[0:32, 0:32])
                    mm.then_inc(q_ready, 1)

                @block.vector
                def _(dve):
                    dve.wait_ge(q_ready, XH + 2)
                    for e in range(4):
                        dve.tensor_copy(qc[:, e::4, SEQ:TOK].rearrange("p h b -> p b h"),
                                        ps[:, 4, e * 32:e * 32 + 32].rearrange("p (b h) -> p b h", h=XH)).then_inc(q_ready, 1)

        with ExitStack() as st:
            ah = sb(st, "o_hi", [128, KT, TOK], f32r)
            al = sb(st, "o_lo", [128, KT, TOK], f32r)
            whi = sb(st, "whi_e", [128, 2, BLK], f32r)
            wlo = sb(st, "wlo_e", [128, 2, BLK], f32r)
            project("co", CO0, KT, ah, al, whi, wlo, SPANS, add_to_x, qc)
        late.close()

        with ExitStack() as st:
            ah = sb(st, "hf_hi", [128, KT, TOK], f32r)
            al = sb(st, "hf_lo", [128, KT, TOK], f32r)
            whi = sb(st, "whi_f", [128, 2, BLK], f32r)
            wlo = sb(st, "wlo_f", [128, 2, BLK], f32r)
            hh = sb(st, "hid_hi", [128, 4, TOK], f32r)
            hl = sb(st, "hid_lo", [128, 4, TOK], f32r)
            z = sb(st, "gate", [128, 2, TOK])
            sg = sb(st, "sigm", [128, 2, TOK])
            up = sb(st, "up", [128, 2, TOK])
            rstd = sb(st, "rstd_f", [128, TOK])
            sq = sb(st, "sq_f", [128, 2, TOK])
            j0 = jobs[0]
            assert j0 % 2 == 0 and FF0 % 2 == 0
            A = Steps(sem("ff_act"), [f"{y}{n}" for n in range(4) for y in ("sig", "hh")])
            W = Steps(sem("ff_dve"), [f"{y}{n}" for n in range(4) for y in ("z0_", "z1_", "u0_", "u1_", "zs", "hd", "hl")])
            down_done = sem("down_done")
            hi_done, lo_done, sq_done, ssq_done, ms_done, rms_done = [
                sem(f"ff_{y}") for y in ("hi", "lo", "sq", "ssq", "ms", "rms")]

            def at(c, steps, name):
                return c * len(steps.names) + steps.at(name)

            def turns_of(eng, body):
                body(0, True, False)
                with eng.Fori(1, FFC - 1) as c:
                    body(c, False, False)
                body(FFC - 1, False, True)

            with nc.Block() as block:
                @block.sync
                def _(sp):
                    with sp.Fori(0, 6 * FFC - 1) as t:
                        for u in range(2):
                            load_block(sp, t * 2 + (FF0 + u), u)

                @block.scalar
                def _(act):
                    def hi_of(c, i):
                        weight_hi(act, whi, c * 12 + (FF0 + i), i % 2, c * 6 + (FF0 // 2 + i // 2))

                    def body(c, first, last):
                        if first:
                            hi_of(0, 0)
                            for k in range(KT):
                                act.activation(ah[:, k, :], x[:, k, :], ACT.Copy, scale=V("g_ffn", k)).then_inc(hi_done, 1)
                            hi_of(0, 1)
                            for k in range(KT):
                                if k >= 2:
                                    act.wait_ge(ssq_done, k - 1)
                                act.activation(sq[:, k % 2, :], x[:, k, :], ACT.Square).then_inc(sq_done, 1)
                            act.wait_ge(ms_done, 2)
                            inverse_root(act, rstd[:, :], rms_done, 0)
                        for i in range(12):
                            if not (last and i >= 10) and i != 7:
                                hi_of(c, i + 2)
                            if i < 8 and i % 2 == 0:
                                n = i // 2
                                act.wait_ge(W.sem, at(c, W, f"z1_{n}"))
                                act.activation(sg[:, n % 2, :], z[:, n % 2, :], ACT.Sigmoid).then_inc(A.sem, 1)
                            elif i < 8:
                                n = i // 2
                                act.wait_ge(W.sem, at(c, W, f"hd{n}"))
                                act.activation(hh[:, n, :], up[:, n % 2, :], ACT.Copy).then_inc(A.sem, 1)
                            if i == 7:
                                hi_of(c, 9)
                    turns_of(act, body)

                @block.vector
                def _(dve):
                    def body(c, first, last):
                        def did(ins, name):
                            ins.then_inc(W.sem, 1)
                            dve.wait_ge(W.sem, at(c, W, name))

                        def lo_of(i):
                            if not (last and i >= 12):
                                weight_lo(dve, whi, wlo, c * 12 + (FF0 + i), i % 2)
                        if first:
                            lo_of(0)
                            for k in range(KT):
                                dve.wait_ge(hi_done, k + 1)
                                dve.scalar_tensor_tensor(al[:, k, :], x[:, k, :], V("g_ffn", k), ah[:, k, :].bitcast(f32),
                                                         ALU.mult, ALU.subtract).then_inc(lo_done, 1)
                            lo_of(1)
                            dve.wait_ge(ssq_done, KT)
                            for i, (a, m) in enumerate(SPANS):
                                dve.tensor_scalar(rstd[:, a:a + m], ps[:, 4 + i, 0:m], 1.0 / D, 1e-6, ALU.mult, ALU.add).then_inc(ms_done, 1)
                            dve.wait_ge(rms_done, 2)
                        for i in range(8):
                            n, b = i // 2, (i // 2) % 2
                            dve.wait_ge(pe_done, c * 12 + (FF0 + i + 3))
                            dst = (z, up)[i % 2]
                            for s, (a, m) in enumerate(SPANS):
                                ins = dve.tensor_tensor(dst[:, b, a:a + m], ps[:, 2 * (i % 2) + s, 0:m], rstd[:, a:a + m], ALU.mult)
                                did(ins, f"{'zu'[i % 2]}{s}_{n}")
                            dve.sem_inc(out_done, 1)
                            if i != 7:
                                lo_of(i + 2)
                            if i % 2:
                                dve.wait_ge(A.sem, at(c, A, f"sig{n}"))
                                did(dve.tensor_tensor(z[:, b, :], z[:, b, :], sg[:, b, :], ALU.mult), f"zs{n}")
                                did(dve.tensor_tensor(up[:, b, :], z[:, b, :], up[:, b, :], ALU.mult), f"hd{n}")
                                dve.wait_ge(A.sem, at(c, A, f"hh{n}"))
                                did(dve.tensor_tensor(hl[:, n, :], up[:, b, :], hh[:, n, :].bitcast(f32), ALU.subtract), f"hl{n}")
                            if i == 7:
                                lo_of(9)
                        for q in range(4):
                            for m_ in range(4):
                                if m_ < 3:
                                    dve.wait_ge(down_done, c * 12 + (3 * q + m_ + 1))
                                else:
                                    dve.wait_ge(pe_done, c * 12 + (FF0 + 8 + q + 3))
                                for s, (a, m) in enumerate(SPANS):
                                    xi = x[:, 4 * q + m_, a:a + m]
                                    ins = dve.tensor_tensor(xi, ps[:, 2 * m_ + s, 0:m], xi, ALU.add)
                                ins.then_inc(out_done, 1)
                            lo_of(10 + q)
                    turns_of(dve, body)

                @block.tensor
                def _(pe):
                    def product(k, kcol, u, wslot, th, tl, first, last):
                        for wt, t in ((whi, th), (whi, tl), (wlo, th)):
                            for s, (a, m) in enumerate(SPANS):
                                mm = pe.matmul(ps[:, 2 * u + s, 0:m], wt[:, wslot, kcol:kcol + 128], t[:, k, a:a + m],
                                               start=(first and wt is whi and t is th), stop=(last and wt is wlo))
                        return mm

                    def body(c, first, last):
                        for i in range(8):
                            pe.wait_ge(wlo_done, c * 12 + (FF0 + i + 1))
                            pe.wait_ge(out_done, c * 24 + (j0 + i + 1))
                            for k in range(KT):
                                if first and i == 0:
                                    pe.wait_ge(lo_done, k + 1)
                                mm = product(k, k * 128, i % 2, i % 2, ah, al, k == 0, k == KT - 1)
                            mm.then_inc(pe_done, 1)
                            if first and i == 0:
                                for k in range(KT):
                                    pe.wait_ge(sq_done, k + 1)
                                    for s, (a, m) in enumerate(SPANS):
                                        mm = pe.matmul(ps[:, 4 + s, 0:m], C("ones"), sq[:, k % 2, a:a + m], start=(k == 0), stop=(k == KT - 1))
                                    mm.then_inc(ssq_done, 1)
                        for q in range(4):
                            pe.wait_ge(wlo_done, c * 12 + (FF0 + 8 + q + 1))
                            def down(m_, k):
                                if k == 0:
                                    ago = 2 if q == 0 and m_ < 2 else 4
                                    pe.wait_ge(out_done, c * 24 + (j0 + 8 + 4 * q + m_ + 3 - ago))
                                if q == 0 and m_ == 0:
                                    pe.wait_ge(W.sem, at(c, W, f"hl{k}"))
                                return product(k, (m_ * 4 + k) * 128, m_, q % 2, hh, hl, k == 0, k == 3)
                            head = [(0, 0), (0, 1), (0, 2), (1, 0), (1, 1), (1, 2), (0, 3), (1, 3)] if q == 0 else \
                                [(m_, k) for m_ in range(2) for k in range(4)]
                            for m_, k in head + [(m_, k) for m_ in (2, 3) for k in range(4)]:
                                mm = down(m_, k)
                                if k == 3:
                                    mm.then_inc(down_done if m_ < 3 else pe_done, 1)
                    turns_of(pe, body)

        with ExitStack() as st:
            sq = sb(st, "sq_g", [128, 2, TOK])
            rstd = sb(st, "rstd_g", [128, TOK])
            fin = sem("fin_act")
            fin_pe, fin_dve, fin_out = sem("fin_pe"), sem("fin_dve"), sem("fin_out")
            with nc.Block() as block:
                @block.scalar
                def _(act):
                    for k in range(KT):
                        if k >= 2:
                            act.wait_ge(fin_pe, k - 1)
                        act.activation(sq[:, k % 2, :], x[:, k, :], ACT.Square).then_inc(fin, 1)
                    act.wait_ge(fin_dve, 2)
                    inverse_root(act, rstd[:, :], fin, KT)

                @block.tensor
                def _(pe):
                    for k in range(KT):
                        pe.wait_ge(fin, k + 1)
                        for s, (a, m) in enumerate(SPANS):
                            mm = pe.matmul(ps[:, 4 + s, 0:m], C("ones"), sq[:, k % 2, a:a + m], start=(k == 0), stop=(k == KT - 1))
                        mm.then_inc(fin_pe, 1)

                @block.vector
                def _(dve):
                    dve.wait_ge(fin_pe, KT)
                    for s, (a, m) in enumerate(SPANS):
                        dve.tensor_scalar(rstd[:, a:a + m], ps[:, 4 + s, 0:m], 1.0 / D, 1e-6, ALU.mult, ALU.add).then_inc(fin_dve, 1)
                    dve.wait_ge(fin, KT + 2)
                    for k in range(KT):
                        dve.scalar_tensor_tensor(x[:, k, :], x[:, k, :], V("g_final", k), rstd[:, :], ALU.mult, ALU.mult).then_inc(fin_dve, 1)

                @block.sync
                def _(sp):
                    for k in range(KT):
                        sp.wait_ge(fin_dve, 3 + k)
                        sp.dma_start(yo[k, :, :], x[:, k, :]).then_inc(fin_out, 16)
                    sp.wait_ge(fin_out, 16 * KT)




def blocks16(wt):
    n = wt.shape[1]
    return wt.reshape(KT, 128, n // 128, 128).transpose(2, 1, 0, 3).reshape(n // 128, 128, BLK)


def prepare(i):
    a = {k: np.asarray(v) for k, v in i.items()}
    w_in = a["w_in"][0]
    cv = a["w_cv"][0].reshape(4, 4, 128, 4, 512).transpose(3, 0, 2, 1, 4).reshape(16, 128, BLK)
    gate, up = blocks16(a["w_gate"][0]), blocks16(a["w_up"][0])
    down = a["w_down"][0].reshape(FFC, 4, 128, 4, 4, 128).transpose(0, 3, 2, 4, 1, 5).reshape(FFC, 4, 128, BLK)
    gu = np.stack([gate, up], 1).reshape(FFC, 8, 128, BLK)
    w = np.concatenate([blocks16(w_in[:, RW_PROJ:]), blocks16(w_in[:, :RW_PROJ]), blocks16(a["w_ck"][0]), cv,
                        blocks16(a["w_o"][0]), blocks16(a["w_cq"][0]), blocks16(a["w_co"][0]),
                        np.concatenate([gu, down], 1).reshape(12 * FFC, 128, BLK)])

    def feat(v):
        return np.asarray(v).reshape(-1, 128).T
    vec = np.concatenate([feat(a["norm_mix_g"][0]), feat(a["norm_mem_g"][0]), feat(a["norm_cross_g"][0]),
                          feat(a["norm_ffn_g"][0]), feat(a["final_norm_g"]), feat(a["tok_shift_mu"][0]),
                          feat(a["rwkv_w0"][0]), feat(a["rwkv_a0"][0]), feat(a["rwkv_k_k"][0]), feat(a["rwkv_k_a"][0]),
                          feat(a["rwkv_r_k"][0]), feat(a["rwkv_lnx_g"][0]), feat(a["rwkv_lnx_b"][0]),
                          feat(a["diff_subln_g"][0]),
                          np.concatenate([a["diff_lq1"][0], a["diff_lq2"][0]])[:, None],
                          np.concatenate([a["diff_lk1"][0], a["diff_lk2"][0]])[:, None],
                          a["state_shift"][0].reshape(NS, PROJ_T, 128).transpose(2, 1, 0).reshape(128, PROJ_T * NS)], 1)
    x = np.concatenate([a["x_prompt"][0], a["x_sample"][:, 0]])
    npool = a["cache_k"].shape[1]
    return {
        "w": w, "vec": vec, "con": shape_constants(),
        "xt": x.T.reshape(KT, 128, TOK),
        "memt": a["mem_prompt"][0].T.reshape(KT, 128, MEM),
        "kc": a["cache_k"][0].transpose(0, 3, 2, 1),
        "vc": a["cache_v"][0],
        "mkc": a["cache_mem_k"][0].reshape(NS, MEM, 16, 128).transpose(0, 3, 2, 1),
        "mvc": a["cache_mem_v"][0].reshape(NS, 2, 128, D).transpose(0, 2, 1, 3),
        "s0": a["state_wkv"][0].reshape(NS, RT, 2, 64, 64).transpose(2, 1, 0, 3, 4).reshape(128, 64, 64),
        "pages": a["page_table"].reshape(1, -1),
        "w2a2": np.concatenate([a["rwkv_w2"][0], a["rwkv_a2"][0]]),
        "g2": a["rwkv_g2"][0],
    }


OUTS = {"qkv": (24, 128, TOK), "yo": (KT, 128, TOK), "wkv_p": (128, RT, 64), "wkv_s": (128, 64, 64),
        "shift": (128, PROJ_T, 1 + NS), "mk_o": (KT, 128, MEM), "mv_o": (2, 128, D)}


def build(nc, shapes):
    args = {n: nc.dram_tensor(n, s, i32 if n == "pages" else f32, kind="ExternalInput").ap() for n, s in shapes.items()}
    args |= {n: nc.dram_tensor(n, s, f32, kind="ExternalOutput").ap() for n, s in OUTS.items()}
    args["ymix"] = nc.dram_tensor("ymix", (KT, 128, TOK), f32, kind="Internal").ap()
    for n, s in {"srow": (2, NS, 2 * DA_HEADS, PAST), "orow": (2, NS, DA_HEADS * (RW + 128)), "xsrow": (NS, XH, MEM),
                 "xorow": (NS, XH * (D + XD))}.items():
        args[n] = nc.dram_tensor(n, s, f32, kind="Internal").ap()
    decoder_kernel(nc, **args)


def kernel(**inputs):
    import concourse.bacc as bacc
    from concourse.bass_utils import run_bass_kernel_spmd
    arrays = {n: np.ascontiguousarray(v) for n, v in prepare(inputs).items()}
    nc = bacc.Bacc("TRN2", target_bir_lowering=False, num_devices=1)
    build(nc, {n: v.shape for n, v in arrays.items()})
    r = run_bass_kernel_spmd(nc, [arrays], core_ids=[0]).results[0]
    r = {n: np.asarray(r[n]) for n in OUTS}
    y = r["yo"].reshape(D, TOK).T
    k = r["qkv"][8:16].reshape(RW, TOK).T
    v = r["qkv"][16:24].reshape(RW, TOK).T
    sh = r["shift"].transpose(2, 1, 0).reshape(1 + NS, RW_PROJ)
    wp = r["wkv_p"].reshape(2, 64, RT, 64).transpose(2, 0, 3, 1).reshape(1, 1, 2 * RT, 64, 64)
    ws = r["wkv_s"].reshape(2, RT, NS, 64, 64).transpose(2, 1, 0, 3, 4).reshape(1, NS, 2 * RT, 64, 64)
    c = np.ascontiguousarray
    return (c(y[None, :SEQ]), c(y[SEQ:, None]), c(k[:SEQ].reshape(1, 1, SEQ, 8, 128)), c(v[:SEQ].reshape(1, 1, SEQ, 8, 128)),
            c(k[SEQ:].reshape(1, NS, 1, 8, 128)), c(v[SEQ:].reshape(1, NS, 1, 8, 128)), c(wp), c(ws),
            c(sh[None, :1]), c(sh[None, 1:]),
            c(r["mk_o"].reshape(D, MEM).T.reshape(1, 1, MEM, XH, XD)), c(r["mv_o"].reshape(1, 1, MEM, XH, XD)))
```
